# Optimizing a Trainium2 kernel written in Bass

```python
import math
import jax
import jax.numpy as jnp
from jax import lax
import numpy as np
import jax, jax.numpy as jnp

D_MODEL = 2048
BATCH = 1
SEQ = 256
DEPTH = 1

CTX_LEN = 256
GRID_W = 64
EPS = 1e-6
N_MOD = 6
D_MIX = D_MODEL
HY_W = D_MIX // 2
HY_GROUPS = 8
HY_ORDER = 2
HY_PROJ = (HY_ORDER + 1) * HY_W
HY_CONV = 3
HY_POS_EMB = 33
HY_FILT_H = 64
HY_TARGET = 1e-2
HY_FAST = 0.3
HY_SLOW = 1.5
SSD_W = D_MIX - HY_W
SSD_HEADDIM = 64
SSD_HEADS = SSD_W // SSD_HEADDIM
SSD_GROUPS = 2
SSD_HPG = SSD_HEADS // SSD_GROUPS
SSD_STATE = 128
SSD_CONV = 3
SSD_CHUNK = 128
SSD_XBC = SSD_W + 2 * SSD_GROUPS * SSD_STATE
SSD_DT = 2 * SSD_HEADS
PROJ_W = HY_PROJ + SSD_XBC + SSD_DT + SSD_W
D_FF = 4 * D_MODEL


def rmsnorm(x, w):
    xf = x.astype(jnp.float32)
    y = xf * lax.rsqrt(jnp.mean(xf * xf, axis=-1, keepdims=True) + EPS)
    return (y * w).astype(x.dtype)

def centred_dwconv(u, w, bias, grid):
    b, L, C = u.shape
    if grid is not None:
        u = u.reshape(b, grid[0], grid[1], C)
    K = w.shape[0]
    pad = K // 2
    T = u.shape[-2]
    up = jnp.pad(u, [(0, 0)] * (u.ndim - 2) + [(pad, pad), (0, 0)])
    y = bias + w[0] * up[..., 0:T, :]
    for k in range(1, K):
        y = y + w[k] * up[..., k:k + T, :]
    return y.reshape(b, L, C)

def hyena_kernel_fft(L, fw1, fb1, freq, fw2, fb2, fw3):
    f32 = jnp.float32
    t = jnp.linspace(0.0, 1.0, L, dtype=f32)[:, None]
    bands = (HY_POS_EMB - 1) // 2
    w = 2.0 * math.pi * jnp.arange(L, dtype=f32)[:, None] / L
    f = jnp.linspace(1e-4, bands - 1, bands, dtype=f32)[None, :]
    feats = jnp.concatenate([t, jnp.cos(f * w), -jnp.sin(f * w)], axis=-1)
    hdn = jnp.sin(freq * (feats @ fw1 + fb1))
    hdn = jnp.sin(freq * (hdn @ fw2 + fb2))
    h = (hdn @ fw3).astype(f32).reshape(L, HY_ORDER, 2, HY_W)
    deltas = jnp.linspace(math.log(HY_TARGET) / HY_SLOW, math.log(HY_TARGET) / HY_FAST, HY_W, dtype=f32)
    h = h * jnp.exp(-t[:, :, None, None] * jnp.abs(deltas))
    k = jnp.concatenate([h[:, :, 0], jnp.zeros((1, HY_ORDER, HY_W), f32), h[:0:-1, :, 1]], axis=0)
    k = k / (jnp.sum(jnp.abs(k), axis=0, keepdims=True) + EPS)
    return jnp.fft.rfft(k, axis=0)

def fft_conv(z, kf):
    L = z.shape[1]
    zf = jnp.fft.rfft(z, n=2 * L, axis=1)
    return jnp.fft.irfft(zf * kf[None], n=2 * L, axis=1)[:, :L]

def segsum(a):
    T = a.shape[-1]
    cs = jnp.cumsum(a, axis=-1)
    diff = cs[..., :, None] - cs[..., None, :]
    mask = jnp.tril(jnp.ones((T, T), dtype=bool))
    return jnp.where(mask, diff, -jnp.inf)

def ssd_scan(xdt, da, bm, cm, init, want_y):
    b, l, g, r, p = xdt.shape
    nc = l // SSD_CHUNK
    xdt = xdt.reshape(b, nc, SSD_CHUNK, g, r, p)
    bc = bm.reshape(b, nc, SSD_CHUNK, g, -1)
    a = da.reshape(b, nc, SSD_CHUNK, g, r).transpose(0, 3, 4, 1, 2)
    a_cs = jnp.cumsum(a, axis=-1)
    decay_to_end = jnp.exp(a_cs[..., -1:] - a_cs)
    states = jnp.einsum('bcsgn,bgrcs,bcsgrp->bcgrpn', bc, decay_to_end, xdt)
    chunk_a = jnp.pad(a_cs[..., -1], ((0, 0), (0, 0), (0, 0), (1, 0)))
    states_all = jnp.concatenate([init[:, None], states], axis=1)
    carried = jnp.einsum('bgrzc,bcgrpn->bzgrpn', jnp.exp(segsum(chunk_a)), states_all)
    final = carried[:, -1]
    if not want_y:
        return final
    cc = cm.reshape(b, nc, SSD_CHUNK, g, -1)
    cb = jnp.einsum('bclgn,bcsgn->bgcls', cc, bc)
    y_diag = jnp.einsum('bgcls,bgrcls,bcsgrp->bclgrp', cb, jnp.exp(segsum(a)), xdt)
    y_off = jnp.einsum('bclgn,bcgrpn,bgrcl->bclgrp', cc, carried[:, :-1], jnp.exp(a_cs))
    y = (y_diag + y_off).reshape(b, l, g, r, p)
    return y, final

def ssd_branch(h, init_f, init_b, grid, lp, want_y):
    b, L, _ = h.shape
    f32 = jnp.float32
    w_in = lp['w_in']
    o0 = HY_PROJ
    o1 = o0 + SSD_XBC
    o2 = o1 + SSD_DT
    xbc = jax.nn.silu(centred_dwconv(h @ w_in[:, o0:o1], lp['ssd_conv_w'], lp['ssd_conv_b'], grid)).astype(f32)
    gn = SSD_GROUPS * SSD_STATE
    xs = xbc[..., :SSD_W].reshape(b, L, SSD_GROUPS, SSD_HPG, SSD_HEADDIM)
    bm = xbc[..., SSD_W:SSD_W + gn].reshape(b, L, SSD_GROUPS, SSD_STATE)
    cm = xbc[..., SSD_W + gn:].reshape(b, L, SSD_GROUPS, SSD_STATE)
    dt = jax.nn.softplus((h @ w_in[:, o1:o2]).astype(f32).reshape(b, L, 2, SSD_HEADS) + lp['dt_bias'])
    dt = dt.reshape(b, L, 2, SSD_GROUPS, SSD_HPG)
    a = (-jnp.exp(lp['a_log'].astype(f32))).reshape(2, SSD_GROUPS, SSD_HPG)

    def run(d, init, flip):
        dt_d = dt[:, :, d]
        seqs = (xs * dt_d[..., None], dt_d * a[d], bm, cm)
        if flip:
            seqs = tuple(s[:, ::-1] for s in seqs)
        return ssd_scan(seqs[0], seqs[1], seqs[2], seqs[3], init, want_y)

    if not want_y:
        return run(0, init_f, False), run(1, init_b, True)
    y_f, s_f = run(0, init_f, False)
    y_b, s_b = run(1, init_b, True)
    y = y_f + y_b[:, ::-1] + lp['ssd_d'].reshape(SSD_GROUPS, SSD_HPG)[..., None] * xs
    zg = jax.nn.silu((h @ w_in[:, o2:]).astype(f32))
    y = (y.reshape(b, L, SSD_W) * zg).reshape(b, L, SSD_GROUPS, SSD_W // SSD_GROUPS)
    y = rmsnorm(y, lp['ssd_norm_w'].reshape(SSD_GROUPS, -1)).reshape(b, L, SSD_W)
    return y.astype(h.dtype), s_f, s_b

def token_mixer(h, init_f, init_b, grid, lp):
    b, L, _ = h.shape
    u = centred_dwconv(h @ lp['w_in'][:, :HY_PROJ], lp['hy_conv_w'], lp['hy_conv_b'], grid).astype(jnp.float32)
    v, *gates = jnp.split(u, HY_ORDER + 1, axis=-1)
    kf = hyena_kernel_fft(L, lp['filt_w1'], lp['filt_b1'], lp['filt_freq'], lp['filt_w2'], lp['filt_b2'], lp['filt_w3'])
    z = v
    for o, gate in enumerate(gates):
        z = gate * (fft_conv(z, kf[:, o]) + z * lp['hy_bias'][o])
    y_hy = rmsnorm(z.reshape(b, L, HY_GROUPS, HY_W // HY_GROUPS), lp['hy_norm_w'].reshape(HY_GROUPS, -1))
    y_hy = y_hy.reshape(b, L, HY_W).astype(h.dtype)
    y_ssd, s_f, s_b = ssd_branch(h, init_f, init_b, grid, lp, True)
    out = jnp.concatenate([y_hy, y_ssd], axis=-1) @ lp['w_out']
    return out, s_f, s_b

def sqrelu_mlp(h, w1, w2):
    return jnp.square(jax.nn.relu(h @ w1)) @ w2

def first_inputs(seed: int = 0) -> dict:
    key = jax.random.key(seed)
    ks = jax.random.split(key, 32)

    def nrm(k, shape, scale):
        return scale * jax.random.normal(k, shape, jnp.float32)

    D = D_MODEL
    dt0 = jnp.exp(jax.random.uniform(ks[20], (DEPTH, 2, SSD_HEADS), jnp.float32, math.log(1e-3), math.log(1e-1)))
    return {
        'x': nrm(ks[0], (BATCH, SEQ, D), 1.0),
        'c': nrm(ks[1], (BATCH, D), 1.0),
        'ctx': nrm(ks[2], (BATCH, CTX_LEN, D), 1.0),
        'c_ctx': nrm(ks[3], (D,), 1.0),
        'w_ada': nrm(ks[4], (DEPTH, D, N_MOD * D), 0.5 * D ** -0.5),
        'b_ada': nrm(ks[5], (DEPTH, N_MOD * D), 0.02),
        'norm1_w': 1.0 + nrm(ks[6], (DEPTH, D), 0.05),
        'w_in': nrm(ks[7], (DEPTH, D, PROJ_W), D ** -0.5),
        'hy_conv_w': nrm(ks[8], (DEPTH, HY_CONV, HY_PROJ), HY_CONV ** -0.5),
        'hy_conv_b': nrm(ks[9], (DEPTH, HY_PROJ), 0.02),
        'filt_w1': nrm(ks[10], (DEPTH, HY_POS_EMB, HY_FILT_H), HY_POS_EMB ** -0.5),
        'filt_b1': nrm(ks[11], (DEPTH, HY_FILT_H), 0.1),
        'filt_freq': 1.0 + nrm(ks[12], (DEPTH, HY_FILT_H), 0.1),
        'filt_w2': nrm(ks[13], (DEPTH, HY_FILT_H, HY_FILT_H), HY_FILT_H ** -0.5),
        'filt_b2': nrm(ks[14], (DEPTH, HY_FILT_H), 0.1),
        'filt_w3': nrm(ks[15], (DEPTH, HY_FILT_H, HY_ORDER * 2 * HY_W), HY_FILT_H ** -0.5),
        'hy_bias': nrm(ks[16], (DEPTH, HY_ORDER, HY_W), 0.1),
        'hy_norm_w': 1.0 + nrm(ks[17], (DEPTH, HY_W), 0.05),
        'ssd_conv_w': nrm(ks[18], (DEPTH, SSD_CONV, SSD_XBC), SSD_CONV ** -0.5),
        'ssd_conv_b': nrm(ks[19], (DEPTH, SSD_XBC), 0.02),
        'dt_bias': dt0 + jnp.log(-jnp.expm1(-dt0)),
        'a_log': jnp.log(jax.random.uniform(ks[21], (DEPTH, 2, SSD_HEADS), jnp.float32, 1.0, 16.0)),
        'ssd_d': 1.0 + nrm(ks[22], (DEPTH, SSD_HEADS), 0.05),
        'ssd_norm_w': 1.0 + nrm(ks[23], (DEPTH, SSD_W), 0.05),
        'w_out': nrm(ks[24], (DEPTH, D_MIX, D), D_MIX ** -0.5),
        'norm2_w': 1.0 + nrm(ks[25], (DEPTH, D), 0.05),
        'w_mlp1': nrm(ks[26], (DEPTH, D, D_FF), D ** -0.5),
        'w_mlp2': nrm(ks[27], (DEPTH, D_FF, D), D_FF ** -0.5),
        'final_norm_w': 1.0 + nrm(ks[28], (D,), 0.05),
    }

def first_block(x, c, ctx, c_ctx, w_ada, b_ada, norm1_w, w_in, hy_conv_w, hy_conv_b, filt_w1, filt_b1,
              filt_freq, filt_w2, filt_b2, filt_w3, hy_bias, hy_norm_w, ssd_conv_w, ssd_conv_b, dt_bias,
              a_log, ssd_d, ssd_norm_w, w_out, norm2_w, w_mlp1, w_mlp2, final_norm_w):
    rows = x.shape[1] // GRID_W
    grid = (rows, GRID_W)
    zero_state = jnp.zeros((x.shape[0], SSD_GROUPS, SSD_HPG, SSD_HEADDIM, SSD_STATE), jnp.float32)
    h_ctx = ctx
    for i in range(DEPTH):
        lp = dict(w_in=w_in[i], hy_conv_w=hy_conv_w[i], hy_conv_b=hy_conv_b[i], filt_w1=filt_w1[i],
                  filt_b1=filt_b1[i], filt_freq=filt_freq[i], filt_w2=filt_w2[i], filt_b2=filt_b2[i],
                  filt_w3=filt_w3[i], hy_bias=hy_bias[i], hy_norm_w=hy_norm_w[i], ssd_conv_w=ssd_conv_w[i],
                  ssd_conv_b=ssd_conv_b[i], dt_bias=dt_bias[i], a_log=a_log[i], ssd_d=ssd_d[i],
                  ssd_norm_w=ssd_norm_w[i], w_out=w_out[i])
        mod = (jax.nn.silu(c) @ w_ada[i] + b_ada[i])[:, None, :]
        mod_c = jax.nn.silu(c_ctx) @ w_ada[i] + b_ada[i]
        sh1, sc1, g1, sh2, sc2, g2 = jnp.split(mod, N_MOD, axis=-1)
        csh1, csc1, cg1, csh2, csc2, cg2 = jnp.split(mod_c, N_MOD, axis=-1)
        hc = rmsnorm(h_ctx, norm1_w[i]) * (1.0 + csc1) + csh1
        if i < DEPTH - 1:
            out_c, s_f, s_b = token_mixer(hc, zero_state, zero_state, None, lp)
            h_ctx = h_ctx + cg1 * out_c
            hc2 = rmsnorm(h_ctx, norm2_w[i]) * (1.0 + csc2) + csh2
            h_ctx = h_ctx + cg2 * sqrelu_mlp(hc2, w_mlp1[i], w_mlp2[i])
        else:
            s_f, s_b = ssd_branch(hc, zero_state, zero_state, None, lp, False)
        hl = rmsnorm(x, norm1_w[i]) * (1.0 + sc1) + sh1
        out_l, _, _ = token_mixer(hl, s_f, s_b, grid, lp)
        x = x + g1 * out_l
        hl2 = rmsnorm(x, norm2_w[i]) * (1.0 + sc2) + sh2
        x = x + g2 * sqrelu_mlp(hl2, w_mlp1[i], w_mlp2[i])
    return rmsnorm(x, final_norm_w)


CHUNK = 64
D_MIX_2 = D_MODEL
D_CONV = D_MIX_2 // 2
D_SSM = D_MIX_2 - D_CONV
CONV_WIDTH = 31
SSM_GROUP = 16
SSM_GROUPS = D_SSM // SSM_GROUP
SSM_STATE = 64
N_MEM = 256
MEM_HEADS = 4
MEM_HEAD_DIM = D_MODEL // MEM_HEADS
PEER_HEADS = 8
PEER_KEYS = 128
PEER_EXPERTS = PEER_KEYS * PEER_KEYS
PEER_DKEY = 128
PEER_HALF = PEER_DKEY // 2
PEER_TOPK = 16
PEER_BLOCK = 128


F32 = jnp.float32

def rms_norm(x, g):
    xf = x.astype(F32)
    y = xf * lax.rsqrt(jnp.mean(xf * xf, axis=-1, keepdims=True) + EPS)
    return (y * g.astype(F32)).astype(x.dtype)

def layer_norm(x, g, b):
    xf = x.astype(F32)
    mu = jnp.mean(xf, axis=-1, keepdims=True)
    xc = xf - mu
    y = xc * lax.rsqrt(jnp.mean(xc * xc, axis=-1, keepdims=True) + EPS)
    return (y * g.astype(F32) + b.astype(F32)).astype(x.dtype)

def causal_depthwise_conv(x, w, b):
    k = w.shape[0]
    y = lax.conv_general_dilated(
        x, w[:, None, :].astype(x.dtype), window_strides=(1,), padding=[(k - 1, 0)],
        dimension_numbers=("NWC", "WIO", "NWC"), feature_group_count=x.shape[-1])
    return y + b.astype(x.dtype)

def conformer_conv_group(a, gate, conv_w, conv_b, ln_g, ln_b):
    c = a * jax.nn.sigmoid(gate)
    c = causal_depthwise_conv(c, conv_w, conv_b)
    c = layer_norm(c, ln_g, ln_b)
    return c * jax.nn.sigmoid(c)

def s5_group(u, lam_re, lam_im, log_dt, b_re, b_im, c_re, c_im, d, glu_w):
    bsz, length, _ = u.shape
    uf = u.astype(F32).reshape(bsz, length, SSM_GROUPS, SSM_GROUP)
    lam = lax.complex(lam_re.astype(F32), lam_im.astype(F32))
    dt = jnp.exp(log_dt.astype(F32))[:, None]
    lam_bar = jnp.exp(lam * dt)
    b = lax.complex(b_re.astype(F32), b_im.astype(F32))
    b_bar = ((lam_bar - 1.0) / lam)[..., None] * b
    bu = jnp.einsum("blgh,gph->blgp", uf.astype(jnp.complex64), b_bar)
    a = jnp.broadcast_to(lam_bar, bu.shape)

    def combine(left, right):
        a_l, s_l = left
        a_r, s_r = right
        return a_r * a_l, a_r * s_l + s_r

    _, states = lax.associative_scan(combine, (a, bu), axis=1)
    c = lax.complex(c_re.astype(F32), c_im.astype(F32))
    y = jnp.real(jnp.einsum("blgp,ghp->blgh", states, c))
    y = y + d.astype(F32).reshape(SSM_GROUPS, SSM_GROUP) * uf
    y = y.reshape(bsz, length, D_SSM).astype(u.dtype)
    z = jax.nn.gelu(y)
    return z * jax.nn.sigmoid(z @ glu_w)

def mem_cross_attention(h, mem_n, w_q, w_kv, w_o):
    bsz, length, _ = h.shape
    q = (h @ w_q).reshape(bsz, length, MEM_HEADS, MEM_HEAD_DIM)
    kv = (mem_n @ w_kv).reshape(bsz, mem_n.shape[1], 2, MEM_HEADS, MEM_HEAD_DIM)
    k, v = kv[:, :, 0], kv[:, :, 1]
    s = jnp.einsum("blhd,bmhd->bhlm", q, k).astype(F32) * (1.0 / math.sqrt(MEM_HEAD_DIM))
    p = jax.nn.softmax(s, axis=-1).astype(h.dtype)
    o = jnp.einsum("bhlm,bmhd->blhd", p, v).reshape(bsz, length, D_MODEL)
    return o @ w_o

def peer(h, w_q, sub_keys, u_tab, v_tab):
    bsz, length, dm = h.shape
    q = (h @ w_q).astype(F32).reshape(bsz, length, PEER_HEADS, 2, PEER_HALF)
    s = jnp.einsum("blhsk,hsnk->blhsn", q, sub_keys.astype(F32))
    s1, i1 = lax.top_k(s[..., 0, :], PEER_TOPK)
    s2, i2 = lax.top_k(s[..., 1, :], PEER_TOPK)
    cand_s = (s1[..., :, None] + s2[..., None, :]).reshape(bsz, length, PEER_HEADS, PEER_TOPK * PEER_TOPK)
    cand_i = (i1[..., :, None] * PEER_KEYS + i2[..., None, :]).reshape(bsz, length, PEER_HEADS, PEER_TOPK * PEER_TOPK)
    top_s, pos = lax.top_k(cand_s, PEER_TOPK)
    idx = jnp.take_along_axis(cand_i, pos, axis=-1)
    g = jax.nn.softmax(top_s, axis=-1)
    n_tok = bsz * length
    nb = n_tok // PEER_BLOCK
    xb = h.reshape(nb, PEER_BLOCK, dm)
    ib = idx.reshape(nb, PEER_BLOCK, PEER_HEADS * PEER_TOPK)
    gb = g.astype(h.dtype).reshape(nb, PEER_BLOCK, PEER_HEADS * PEER_TOPK)

    def block(args):
        xt, it, gt = args
        u = jnp.take(u_tab, it, axis=0)
        act = jax.nn.gelu(jnp.einsum("td,tkd->tk", xt, u))
        v = jnp.take(v_tab, it, axis=0)
        return jnp.einsum("tk,tkd->td", gt * act, v)

    out = lax.map(block, (xb, ib, gb))
    return out.reshape(bsz, length, dm)

def second_inputs(seed: int = 0) -> dict:
    key = jax.random.key(seed)
    ks = iter(jax.random.split(key, 40))
    nrm = lambda shape, scale: jax.random.normal(next(ks), shape, F32) * scale
    gain = lambda shape: 1.0 + 0.05 * jax.random.normal(next(ks), shape, F32)
    L = DEPTH
    n_in = 2 * D_CONV + D_SSM
    lam_re = -0.5 + 0.01 * jax.random.normal(next(ks), (L, SSM_GROUPS, SSM_STATE), F32)
    lam_im = (math.pi * jnp.arange(SSM_STATE, dtype=F32))[None, None, :] + 0.01 * jax.random.normal(next(ks), (L, SSM_GROUPS, SSM_STATE), F32)
    log_dt = jax.random.uniform(next(ks), (L, SSM_GROUPS), F32, math.log(1e-3), math.log(1e-1))
    return {
        "x": nrm((BATCH, SEQ, D_MODEL), 1.0),
        "mem": nrm((BATCH, N_MEM, D_MODEL), 1.0),
        "norm_mix_g": gain((L, D_MODEL)),
        "w_in": nrm((L, D_MODEL, n_in), D_MODEL ** -0.5),
        "conv_w": nrm((L, CONV_WIDTH, D_CONV), CONV_WIDTH ** -0.5),
        "conv_b": nrm((L, D_CONV), 0.02),
        "conv_ln_g": gain((L, D_CONV)),
        "conv_ln_b": nrm((L, D_CONV), 0.02),
        "ssm_lam_re": lam_re,
        "ssm_lam_im": lam_im,
        "ssm_log_dt": log_dt,
        "ssm_b_re": nrm((L, SSM_GROUPS, SSM_STATE, SSM_GROUP), (2.0 * SSM_GROUP) ** -0.5),
        "ssm_b_im": nrm((L, SSM_GROUPS, SSM_STATE, SSM_GROUP), (2.0 * SSM_GROUP) ** -0.5),
        "ssm_c_re": nrm((L, SSM_GROUPS, SSM_GROUP, SSM_STATE), (2.0 * SSM_STATE) ** -0.5),
        "ssm_c_im": nrm((L, SSM_GROUPS, SSM_GROUP, SSM_STATE), (2.0 * SSM_STATE) ** -0.5),
        "ssm_d": nrm((L, D_SSM), 1.0),
        "ssm_glu_w": nrm((L, D_SSM, D_SSM), D_SSM ** -0.5),
        "grp_norm_conv_g": gain((L, D_CONV)),
        "grp_norm_ssm_g": gain((L, D_SSM)),
        "w_out": nrm((L, D_MIX_2, D_MODEL), D_MIX_2 ** -0.5),
        "norm_mem_g": gain((L, D_MODEL)),
        "mem_norm_g": gain((L, D_MODEL)),
        "w_q_mem": nrm((L, D_MODEL, D_MODEL), D_MODEL ** -0.5),
        "w_kv_mem": nrm((L, D_MODEL, 2 * D_MODEL), D_MODEL ** -0.5),
        "w_o_mem": nrm((L, D_MODEL, D_MODEL), D_MODEL ** -0.5),
        "norm_ffn_g": gain((L, D_MODEL)),
        "peer_w_q": nrm((L, D_MODEL, PEER_HEADS * PEER_DKEY), D_MODEL ** -0.5),
        "peer_keys": nrm((L, PEER_HEADS, 2, PEER_KEYS, PEER_HALF), PEER_HALF ** -0.5),
        "peer_u": nrm((L, PEER_EXPERTS, D_MODEL), D_MODEL ** -0.5),
        "peer_v": nrm((L, PEER_EXPERTS, D_MODEL), PEER_TOPK ** -0.5),
        "final_norm_g": gain((D_MODEL,)),
    }

def second_block(x, mem, norm_mix_g, w_in, conv_w, conv_b, conv_ln_g, conv_ln_b,
              ssm_lam_re, ssm_lam_im, ssm_log_dt, ssm_b_re, ssm_b_im, ssm_c_re, ssm_c_im,
              ssm_d, ssm_glu_w, grp_norm_conv_g, grp_norm_ssm_g, w_out,
              norm_mem_g, mem_norm_g, w_q_mem, w_kv_mem, w_o_mem,
              norm_ffn_g, peer_w_q, peer_keys, peer_u, peer_v, final_norm_g):
    h = x
    for i in range(DEPTH):
        hn = rms_norm(h, norm_mix_g[i])
        proj = hn @ w_in[i]
        conv_a = proj[..., :D_CONV]
        conv_gate = proj[..., D_CONV:2 * D_CONV]
        ssm_u = proj[..., 2 * D_CONV:]
        yc = conformer_conv_group(conv_a, conv_gate, conv_w[i], conv_b[i], conv_ln_g[i], conv_ln_b[i])
        ys = s5_group(ssm_u, ssm_lam_re[i], ssm_lam_im[i], ssm_log_dt[i], ssm_b_re[i], ssm_b_im[i],
                      ssm_c_re[i], ssm_c_im[i], ssm_d[i], ssm_glu_w[i])
        y = jnp.concatenate([rms_norm(yc, grp_norm_conv_g[i]), rms_norm(ys, grp_norm_ssm_g[i])], axis=-1)
        h = h + y @ w_out[i]
        hn = rms_norm(h, norm_mem_g[i])
        mem_n = rms_norm(mem, mem_norm_g[i])
        h = h + mem_cross_attention(hn, mem_n, w_q_mem[i], w_kv_mem[i], w_o_mem[i])
        hn = rms_norm(h, norm_ffn_g[i])
        h = h + peer(hn, peer_w_q[i], peer_keys[i], peer_u[i], peer_v[i])
    return rms_norm(h, final_norm_g)


def setup_inputs(seed=0):
    out = dict(first_inputs(seed))
    for name, value in second_inputs(seed + 1).items():
        if name != "x":
            out[name + "_2"] = value
    return out


def reference(
    x, c, ctx, c_ctx, w_ada, b_ada, norm1_w, w_in, hy_conv_w, hy_conv_b, filt_w1, filt_b1,
    filt_freq, filt_w2, filt_b2, filt_w3, hy_bias, hy_norm_w, ssd_conv_w, ssd_conv_b, dt_bias,
    a_log, ssd_d, ssd_norm_w, w_out, norm2_w, w_mlp1, w_mlp2, final_norm_w, mem_2, norm_mix_g_2,
    w_in_2, conv_w_2, conv_b_2, conv_ln_g_2, conv_ln_b_2, ssm_lam_re_2, ssm_lam_im_2,
    ssm_log_dt_2, ssm_b_re_2, ssm_b_im_2, ssm_c_re_2, ssm_c_im_2, ssm_d_2, ssm_glu_w_2,
    grp_norm_conv_g_2, grp_norm_ssm_g_2, w_out_2, norm_mem_g_2, mem_norm_g_2, w_q_mem_2,
    w_kv_mem_2, w_o_mem_2, norm_ffn_g_2, peer_w_q_2, peer_keys_2, peer_u_2, peer_v_2,
    final_norm_g_2,
):
    x = first_block(
        x, c, ctx, c_ctx, w_ada, b_ada, norm1_w, w_in, hy_conv_w, hy_conv_b, filt_w1, filt_b1,
        filt_freq, filt_w2, filt_b2, filt_w3, hy_bias, hy_norm_w, ssd_conv_w, ssd_conv_b,
        dt_bias, a_log, ssd_d, ssd_norm_w, w_out, norm2_w, w_mlp1, w_mlp2, final_norm_w,
    )
    return second_block(
        x, mem_2, norm_mix_g_2, w_in_2, conv_w_2, conv_b_2, conv_ln_g_2, conv_ln_b_2,
        ssm_lam_re_2, ssm_lam_im_2, ssm_log_dt_2, ssm_b_re_2, ssm_b_im_2, ssm_c_re_2,
        ssm_c_im_2, ssm_d_2, ssm_glu_w_2, grp_norm_conv_g_2, grp_norm_ssm_g_2, w_out_2,
        norm_mem_g_2, mem_norm_g_2, w_q_mem_2, w_kv_mem_2, w_o_mem_2, norm_ffn_g_2, peer_w_q_2,
        peer_keys_2, peer_u_2, peer_v_2, final_norm_g_2,
    )


_drawn_inputs = setup_inputs


def setup_inputs(seed=0):
    import zlib

    import numpy as np

    out = dict(_drawn_inputs(seed))
    spreads = {}
    factors = {'ctx': 4.897,
     'c_ctx': 5.324,
     'hy_conv_b': 2.906,
     'hy_norm_w': 3.822,
     'ssd_conv_b': 5.938,
     'ssd_d': 5.463,
     'ssd_norm_w': 3.812,
     'conv_ln_b_2': 4.011,
     'ssm_lam_re_2': 64.0,
     'norm_mem_g_2': 8.0,
     'mem_norm_g_2': 6.605,
     'norm_ffn_g_2': 8.0,
     'peer_w_q_2': 3.109,
     'peer_keys_2': 3.09,
     'peer_u_2': 3.458,
     'peer_v_2': 3.113}
    for name, (base, spread) in spreads.items():
        noise = np.random.default_rng([zlib.crc32(name.encode()), seed]).standard_normal(out[name].shape)
        drawn = base * np.exp(spread * noise) if base else spread * noise
        out[name] = jnp.asarray(drawn.astype(out[name].dtype))
    for name, factor in factors.items():
        out[name] = (out[name] * factor).astype(out[name].dtype)
    return out
```

```python
import math
from contextlib import ExitStack

import numpy as np

import concourse.bass as bass
from concourse import mybir

F32 = mybir.dt.float32
U32 = mybir.dt.uint32
ALU = mybir.AluOpType
ACT = mybir.ActivationFunctionType
AX_X = mybir.AxisListType.X

P = 128
T = 256
TT = T // P
D = 2048
KD = D // P
EPS = 1e-6
RING = 4
PIECE = KD * P
BANK = 512

HY = 1024
HT = HY // P
HY_TILES = 3 * HT
XBC_TILES = 12
Z_TILES = 8
GRID = 64
HEADS = 16
HEAD = 64
MLP_TILES = 64
EPS_COL, ZERO_COL, QUARTER_COL = 0, 1, 2

CONV31 = 31
PAIRS = 32
MEM_HEADS = 4
PEER_HEADS = 8
KEYS = 128
TOPK = 16
TWO_PI = 6.283185

PARAM_COLS = dict(
    cond=2 * KD, b_ada=6 * KD, norm1=KD, hy_conv_w=3 * HY_TILES, hy_conv_b=HY_TILES,
    hy_bias=2 * HT, hy_norm=HT, ssd_conv_w=3 * XBC_TILES, ssd_conv_b=XBC_TILES, ssd_d=HT,
    ssd_norm=HT, norm2=KD, final1=KD, norm_mix=KD, conv_b=HT, ln_g=HT, ln_b=HT, grp_conv=HT,
    grp_ssm=HT, norm_mem=KD, mem_norm=KD, norm_ffn=KD, final2=KD, ssm_d=HT, lam_re=PAIRS,
    lam_im=PAIRS, log_dt=PAIRS, dt_bias=2 * HEADS, a_log=2 * HEADS, conv_w=CONV31 * HT,
    filt=4,
)
PARAM_AT, N_PARAM = {}, 0
for _name, _n in PARAM_COLS.items():
    PARAM_AT[_name] = N_PARAM
    N_PARAM += _n

CONST_COLS = dict(ident=P, tri_f=P, tri_b=P, iota=T, group=2)
CONST_AT, N_CONST = {}, 0
for _name, _n in CONST_COLS.items():
    CONST_AT[_name] = N_CONST
    N_CONST += _n


def spread(ap, axis, n):
    v = ap.unsqueeze(axis)
    shape = list(v.shape)
    shape[axis] = n
    return v.broadcast_to(shape)


class Signal:

    def __init__(self, sem):
        self.sem, self.base = sem, 0


class Chain:

    def __init__(self, sem):
        self.sem, self.n, self.per, self.i = sem, 0, 0, None

    def step(self, eng, ins):
        ins.then_inc(self.sem, 1)
        self.n += 1
        eng.wait_ge(self.sem, self.n if self.i is None else self.i * self.per + self.n)

    def loop(self, i, per):
        self.i, self.per, self.start = i, per, self.n

    def end(self, iterations):
        assert self.n - self.start == self.per, (self.n - self.start, self.per)
        self.n += self.per * (iterations - 1)
        self.i = None


class Core:

    def __init__(self, nc, ctx, dram):
        self.nc, self.dram, self.ctx = nc, dram, ctx
        self.sb = lambda name, shape, dt=F32: ctx.enter_context(nc.sbuf_tensor(name, shape, dt))
        self.ring = self.sb("ring", [P, RING, KD, P])
        self.params = self.sb("params", [P, N_PARAM])
        self.consts = self.sb("consts", [P, N_CONST])
        self.ones = self.sb("ones", [P, P])
        self.small = self.sb("small", [P, 4])
        self.mod = self.sb("mod", [P, 6 * KD, 2])
        self.gain = self.sb("gain", [P, 3 * KD])
        self.x = self.sb("x", [P, KD, T])
        self.h = self.sb("h", [P, KD, T])
        self.ps = ctx.enter_context(nc.psum_tensor("ps", [P, 8, BANK], F32))
        self.landed = [self.sem(f"piece_landed{s}") for s in range(RING)]
        self.used = Signal(self.sem("piece_used"))
        self.drained = Signal(self.sem("bank_drained"))
        self.norm_signals = [Signal(self.sem(f"norm_{n}")) for n in ("squared", "summed", "rooted", "scaled")]
        self.hyena_signals = {n: self.sem(f"hyena_{n}") for n in ("turned", "token", "spectrum", "product", "result")}
        self.dve = Chain(self.sem("vector_step"))
        self.act = Chain(self.sem("scalar_step"))
        self.pool = Chain(self.sem("gpsimd_step"))
        self.prm = {n: self.params[:, PARAM_AT[n]:PARAM_AT[n] + c] for n, c in PARAM_COLS.items()}
        self.cst = {n: self.consts[:, CONST_AT[n]:CONST_AT[n] + c] for n, c in CONST_COLS.items()}

    def sem(self, name):
        return self.ctx.enter_context(self.nc.semaphore(name))

    def piece(self, w, n):
        return self.dram[w][n].rearrange("p (k m) -> p k m", k=KD)


def stream(core, sp, w, count, next_w, first=0):
    used = core.used
    rounds = count // RING
    if rounds > 1:
        with sp.Fori(0, rounds - 1) as i:
            for s in range(RING):
                sp.wait_ge(used.sem, i * RING + (used.base + s + 1))
                sp.dma_start(core.ring[:, s], core.piece(w, i * RING + (first + RING + s))).then_inc(core.landed[s], 16)
    for s in range(RING):
        sp.wait_ge(used.sem, used.base + count - RING + s + 1)
        if next_w is not None:
            sp.dma_start(core.ring[:, s], core.piece(next_w[0], next_w[1] + s)).then_inc(core.landed[s], 16)


def piece_landed(core, pe, s, i, at=0):
    pe.wait_ge(core.landed[s], i * 16 + 16 * (core.used.base // RING + at + 1))


def rms_stage(core, name, src, dst, tiles, gain, bias=None):
    nc, ps = core.nc, core.ps
    squared, summed, rooted, scaled = core.norm_signals
    with ExitStack() as own:
        sq = own.enter_context(nc.sbuf_tensor(f"{name}_sq", [P, tiles, T], F32))
        std = own.enter_context(nc.sbuf_tensor(f"{name}_std", [P, T], F32))
        rstd = own.enter_context(nc.sbuf_tensor(f"{name}_rstd", [P, T], F32))
        group = tiles // 4
        with nc.Block() as block:
            @block.scalar
            def _(act):
                for g in range(4):
                    at = slice(g * group, (g + 1) * group)
                    act.activation(sq[:, at, :], src[:, at, :], ACT.Square).then_inc(squared.sem, 1)
                act.wait_ge(summed.sem, summed.base + 1)
                act.activation(std[:], ps[:, 0, 0:T], ACT.Sqrt, bias=core.small[:, EPS_COL:EPS_COL + 1],
                               scale=1.0 / (tiles * P)).then_inc(rooted.sem, 1)
                if bias is not None:
                    for t in range(tiles):
                        act.wait_ge(scaled.sem, scaled.base + t + 1)
                        act.activation(dst[:, t, :], dst[:, t, :], ACT.Identity, bias=bias[:, t:t + 1])

            @block.tensor
            def _(pe):
                for t in range(tiles):
                    if t % group == 0:
                        pe.wait_ge(squared.sem, squared.base + t // group + 1)
                    mm = pe.matmul(ps[:, 0, 0:T], core.ones[:], sq[:, t, :], start=t == 0, stop=t == tiles - 1)
                mm.then_inc(summed.sem, 1)

            @block.vector
            def _(dve):
                dve.wait_ge(rooted.sem, rooted.base + 1)
                core.dve.step(dve, dve.reciprocal(rstd[:], std[:]))
                for t in range(tiles):
                    dve.scalar_tensor_tensor(dst[:, t, :], src[:, t, :], gain[:, t:t + 1], rstd[:],
                                             ALU.mult, ALU.mult).then_inc(scaled.sem, 1)
    for signal, n in ((squared, 4), (summed, 1), (rooted, 1), (scaled, tiles)):
        signal.base += n


def start_stage(core, ctx_tile, const_loads):
    nc, ps, dram = core.nc, core.ps, core.dram
    loaded, made, biased = core.sem("inputs_loaded"), core.sem("constants_made"), core.sem("mod_made")
    tables = core.sem("tables_loaded")
    with nc.sbuf_tensor("silu_c", [P, KD, 2], F32) as silu_c, nc.Block() as block:
        tiles = 6 * KD
        mod_sums = ps[:, 0, 0:2 * tiles].rearrange("p (n c) -> p n c", c=2)

        @block.sync
        def _(sp):
            sp.dma_start(core.params[:], dram["params"]).then_inc(loaded, 16)
            for s in range(RING):
                sp.dma_start(core.ring[:, s], core.piece("w_ada", s)).then_inc(core.landed[s], 16)
            stream(core, sp, "w_ada", tiles, ("w_mix", 0))

        @block.scalar
        def _(act):
            act.dma_start(core.consts[:], dram["consts"]).then_inc(tables, 16)
            act.dma_start(core.x[:], dram["x"]).then_inc(tables, 16)
            act.dma_start(ctx_tile[:], dram["ctx"]).then_inc(tables, 16)
            for tile, name in const_loads:
                act.dma_start(tile, dram[name]).then_inc(tables, 16)
            act.wait_ge(loaded, 16)
            act.activation(silu_c[:], core.prm["cond"].rearrange("p (k c) -> p k c", c=2), ACT.Silu).then_inc(made, 1)
            act.wait_ge(tables, 16 * (3 + len(const_loads)))

        @block.vector
        def _(dve):
            dve.memset(core.ones[:], 1.0)
            for col, value in ((EPS_COL, EPS), (ZERO_COL, 0.0), (QUARTER_COL, 0.25)):
                dve.memset(core.small[:, col:col + 1], value)
            dve.wait_ge(core.used.sem, tiles)
            quarter = tiles // 4
            for q in range(4):
                at = slice(q * quarter, (q + 1) * quarter)
                ins = dve.tensor_tensor(core.mod[:, at, :], mod_sums[:, at, :], spread(core.prm["b_ada"][:, at], 2, 2), ALU.add)
                ins.then_inc(core.drained.sem, 1)
            dve.wait_ge(core.drained.sem, 4)
            for n, (norm, part, who) in enumerate((("norm1", 1, 0), ("norm1", 1, 1), ("norm2", 4, 0))):
                dve.scalar_tensor_tensor(core.gain[:, n * KD:(n + 1) * KD], core.mod[:, part * KD:(part + 1) * KD, who],
                                         1.0, core.prm[norm], ALU.add, ALU.mult)

        @block.tensor
        def _(pe):
            pe.wait_ge(made, 1)
            with pe.Fori(0, tiles // RING) as i:
                for s in range(RING):
                    piece_landed(core, pe, s, i)
                    for k in range(KD):
                        mm = pe.matmul(mod_sums[:, i * RING + s, :], core.ring[:, s, k, :], silu_c[:, k, :],
                                       start=k == 0, stop=k == KD - 1)
                    mm.then_inc(core.used.sem, 1)
    core.used.base += tiles
    core.drained.base += 4


def linear_stage(core, name, w, tiles, next_w, rhs, drain, engine="scalar", helper=None, first=0, kc=1,
                 loads=()):
    nc, ps = core.nc, core.ps
    used, drained = core.used, core.drained
    slots = RING if kc == 1 else 2
    rounds = tiles // slots
    loaded = core.sem(f"{name}_loaded") if loads else None
    with nc.Block() as block:
        @block.sync
        def _(sp):
            for tile, source in loads:
                sp.dma_start(tile, core.dram[source]).then_inc(loaded, 16)
            stream(core, sp, w, tiles * kc, next_w, first)
            if loads:
                sp.wait_ge(loaded, 16 * len(loads))

        @block.tensor
        def _(pe):
            with pe.Fori(0, rounds) as i:
                for s in range(slots):
                    for c in range(kc):
                        at = s * kc + c
                        piece_landed(core, pe, at % RING, i * (slots * kc // RING), at // RING)
                        if c == 0:
                            pe.wait_ge(drained.sem, i * slots + (drained.base + s - (slots - 1)))
                        for j, r in enumerate(rhs):
                            for k in range(KD):
                                mm = pe.matmul(ps[:, s + RING * j, 0:T], core.ring[:, at % RING, k, :],
                                               r[:, c * KD + k, :], start=c + k == 0,
                                               stop=(c, k) == (kc - 1, KD - 1))
                        mm.then_inc(used.sem, 1)

        def draining(eng):
            with eng.Fori(0, rounds) as i:
                for s in range(slots):
                    eng.wait_ge(used.sem, i * (slots * kc) + (used.base + (s + 1) * kc))
                    banks = [ps[:, s + RING * j, 0:T] for j in range(len(rhs))]
                    drain(eng, banks, i * slots + s, i, s).then_inc(drained.sem, 1)

        if engine == "scalar":
            block.scalar(draining)
        else:
            block.vector(draining)
        if helper is not None:
            helper(block)
    used.base += tiles * kc
    drained.base += tiles


def conv3_stage(core, name, w, tiles, next_w, rhs, first, dests, taps, bias, rows):
    centre = core.sem(f"{name}_centred")
    used, ps = core.used, core.ps

    def centres(block):
        @block.scalar
        def _(act):
            with act.Fori(0, tiles // RING) as i:
                for s in range(RING):
                    act.wait_ge(used.sem, i * RING + (base + s + 1))
                    n = i * RING + s
                    for j, dst in enumerate(dests):
                        act.activation(dst[:, n, :], ps[:, s + RING * j, 0:T], ACT.Identity,
                                       bias=bias[:, bass.ds(n, 1)],
                                       scale=taps[:, bass.ds(n + tiles, 1)]).then_inc(centre, 1)

    def drain(dve, banks, n, i, s):
        if s == 0:
            core.dve.loop(i, per)
        for j, (dst, bank) in enumerate(zip(dests, banks)):
            dve.wait_ge(centre, i * (RING * len(rhs)) + (s * len(rhs) + j + 1))
            g = rows[j]
            u = bank.rearrange("p (r t) -> p r t", t=g)
            y = dst[:, n, :].rearrange("p (r t) -> p r t", t=g)
            core.dve.step(dve, dve.scalar_tensor_tensor(
                y[:, :, 1:g], u[:, :, 0:g - 1], taps[:, bass.ds(n, 1)], y[:, :, 1:g], ALU.mult, ALU.add))
            ins = dve.scalar_tensor_tensor(
                y[:, :, 0:g - 1], u[:, :, 1:g], taps[:, bass.ds(n + 2 * tiles, 1)], y[:, :, 0:g - 1],
                ALU.mult, ALU.add)
            if j + 1 < len(dests):
                core.dve.step(dve, ins)
        return ins

    per = (2 * len(rhs) - 1) * RING
    base = used.base
    linear_stage(core, name, w, tiles, next_w, rhs, drain, "vector", centres, first)
    core.dve.end(tiles // RING)


def dt_stage(core, wdt, ctx_tile, ssd):
    nc, ps = core.nc, core.ps
    names = ("sums", "abs", "exp", "grown", "log", "a", "da", "cum", "to_end")
    s = {n: core.sem(f"dt_{n}") for n in names}
    H2 = 2 * HEADS
    with ExitStack() as own:
        sb = lambda name: own.enter_context(nc.sbuf_tensor(f"dt_{name}", [P, 4, H2], F32))
        v, e, u, lnu, zero, den, rest = (sb(n) for n in ("v", "e", "u", "lnu", "zero", "den", "rest"))
        av = sb("av")
        a_row = own.enter_context(nc.sbuf_tensor("a_row", [P, H2], F32))
        with nc.Block() as block:
            @block.tensor
            def _(pe):
                for q in range(4):
                    src = core.h if q < 2 else ctx_tile
                    at = slice((q % 2) * P, (q % 2 + 1) * P)
                    for k in range(KD):
                        mm = pe.matmul(ps[:, 0, q * H2:(q + 1) * H2], src[:, k, at], wdt[:, k, :],
                                       start=k == 0, stop=k == KD - 1)
                mm.then_inc(s["sums"], 1)
                pe.wait_ge(s["da"], 1)
                for q in range(4):
                    for d, tri in enumerate(("tri_f", "tri_b")):
                        at = slice(d * HEADS, (d + 1) * HEADS)
                        pe.matmul(ps[:, 1, q * H2 + d * HEADS:q * H2 + (d + 1) * HEADS], core.cst[tri],
                                  ssd.da[:, q, at], start=True, stop=True)
                mm = pe.matmul(ps[:, 2, 0:4 * H2], core.ones[:], ssd.da[:], start=True, stop=True)
                mm.then_inc(s["cum"], 1)

            @block.scalar
            def _(act):
                act.activation(a_row[:], core.prm["a_log"], ACT.Exp).then_inc(s["a"], 1)
                act.wait_ge(s["abs"], 1)
                act.activation(e[:], av[:], ACT.Exp, scale=-1.0).then_inc(s["exp"], 1)
                act.wait_ge(s["grown"], 1)
                act.activation(lnu[:], u[:], ACT.Ln).then_inc(s["log"], 1)
                act.wait_ge(s["to_end"], 1)
                act.activation(ssd.etot[:], ps[:, 2, 0:4 * H2].rearrange("p (q h) -> p q h", q=4), ACT.Exp)
                act.activation(ssd.to_end[:], ssd.to_end[:], ACT.Exp)

            @block.vector
            def _(dve):
                step = lambda ins: core.dve.step(dve, ins)
                sums = ps[:, 0, 0:4 * H2].rearrange("p (q h) -> p q h", q=4)
                dve.wait_ge(s["sums"], 1)
                step(dve.tensor_tensor(v[:], sums, spread(core.prm["dt_bias"], 1, 4), ALU.add))
                step(dve.tensor_scalar(rest[:], v[:], -1.0, None, ALU.mult))
                dve.tensor_tensor(av[:], v[:], rest[:], ALU.max).then_inc(s["abs"], 1)
                dve.wait_ge(s["exp"], 1)
                dve.tensor_scalar(u[:], e[:], 1.0, None, ALU.add).then_inc(s["grown"], 1)
                dve.wait_ge(s["grown"], 1)
                step(dve.tensor_scalar(den[:], u[:], -1.0, None, ALU.add))
                step(dve.tensor_scalar(zero[:], den[:], 0.0, None, ALU.is_equal))
                step(dve.tensor_tensor(den[:], den[:], zero[:], ALU.add))
                step(dve.reciprocal(den[:], den[:]))
                dve.wait_ge(s["log"], 1)
                step(dve.tensor_tensor(den[:], den[:], lnu[:], ALU.mult))
                step(dve.tensor_tensor(den[:], den[:], zero[:], ALU.add))
                step(dve.tensor_tensor(den[:], den[:], e[:], ALU.mult))
                step(dve.scalar_tensor_tensor(ssd.dt[:], v[:], 0.0, den[:], ALU.max, ALU.add))
                dve.wait_ge(s["a"], 1)
                dve.scalar_tensor_tensor(ssd.da[:], ssd.dt[:], -1.0, spread(a_row[:], 1, 4),
                                         ALU.mult, ALU.mult).then_inc(s["da"], 1)
                dve.wait_ge(s["cum"], 1)
                step(dve.tensor_copy(ssd.cum[:], ps[:, 1, 0:4 * H2].rearrange("p (q h) -> p q h", q=4)))
                dve.tensor_tensor(ssd.to_end[:], ps[:, 2, 0:4 * H2].rearrange("p (q h) -> p q h", q=4),
                                  ssd.cum[:], ALU.subtract).then_inc(s["to_end"], 1)


def sine_steps(core, dve, x, k, bound_done):
    magic = 12582912.0
    c1, c2 = 6.28125, 2 * math.pi - 6.28125
    step = lambda ins: core.dve.step(dve, ins)
    step(dve.tensor_scalar(k, x, 1 / (2 * math.pi), magic, ALU.mult, ALU.add))
    step(dve.tensor_scalar(k, k, -magic, None, ALU.add))
    step(dve.scalar_tensor_tensor(x, k, -c1, x, ALU.mult, ALU.add))
    step(dve.scalar_tensor_tensor(x, k, -c2, x, ALU.mult, ALU.add))
    dve.tensor_scalar(x, x, 3.1415925, -3.1415925, ALU.min, ALU.max).then_inc(bound_done, 1)


COS0, COS1, COS_N, SIN_N, SIN0, SIN1 = range(6)
KA0, KA1, KN0, KN1, KB0, KB1 = range(6)


def filter_stage(core, dft, filters):
    nc, ps, dram = core.nc, core.ps, core.dram
    names = ("in", "fw3", "arg", "bounded", "sine", "taps", "tapped", "abs", "abs_sum", "norm", "even_odd",
             "spectrum", "stored")
    s = {n: core.sem(f"filt_{n}") for n in names}
    h = core.h[:].rearrange("p k t -> p (k t)").rearrange("p (a b c) -> p a b c", a=2, b=2)
    with ExitStack() as own:
        sb = lambda name, shape: own.enter_context(nc.sbuf_tensor(f"filt_{name}", shape, F32))
        fw1, fw2, hdn = sb("w1", [33, 64]), sb("w2", [64, 64]), sb("hdn", [64, T])
        fw3, window = sb("w3", [64, 2, HY]), sb("window", [P, TT, HY])
        tmp, norm = sb("tmp", [P, 4, BANK]), sb("norm", [P, HY])
        x, k, feats = tmp[0:64, 0, 0:T], tmp[0:64, 0, T:2 * T], tmp[0:33, 1, 0:T]
        freq, b1, b2 = (core.prm["filt"][0:64, n:n + 1] for n in range(3))
        with nc.Block() as block:
            @block.sync
            def _(sp):
                sp.dma_start(feats, dram["feats"]).then_inc(s["in"], 16)
                sp.dma_start(fw1[:], dram["filt_w1"]).then_inc(s["in"], 16)
                sp.dma_start(fw2[:], dram["filt_w2"]).then_inc(s["in"], 16)
                sp.dma_start(window[:], dram["window"]).then_inc(s["in"], 16)
                w3 = dram["filt_w3"].rearrange("k (o a c) -> k o a c", o=2, a=2)
                sp.dma_start(fw3[:], w3[:, 0]).then_inc(s["fw3"], 16)
                sp.wait_ge(s["taps"], 1)
                sp.dma_start(fw3[:], w3[:, 1]).then_inc(s["fw3"], 16)

            @block.tensor
            def _(pe):
                pe.wait_ge(s["in"], 64)
                pe.matmul(ps[0:64, 0, 0:T], fw1[:], feats, start=True, stop=True).then_inc(s["arg"], 1)
                pe.wait_ge(s["sine"], 1)
                pe.matmul(ps[0:64, 0, 0:T], fw2[:], hdn[:], start=True, stop=True).then_inc(s["arg"], 1)
                pe.wait_ge(s["sine"], 2)
                for o in range(2):
                    pe.wait_ge(s["fw3"], 16 * (o + 1))
                    if o:
                        pe.wait_ge(s["stored"], 10)
                    for b in range(8):
                        t, a, c = b // 4, b // 2 % 2, b % 2
                        mm = pe.matmul(ps[:, b, :], hdn[:, t * P:(t + 1) * P], fw3[:, a, c * BANK:(c + 1) * BANK],
                                       start=True, stop=True)
                    mm.then_inc(s["taps"], 1)
                    pe.wait_ge(s["tapped"], o + 1)
                    for c in range(2):
                        pe.wait_ge(s["abs"], 2 * o + c + 1)
                        for j in range(4):
                            mm = pe.matmul(ps[:, c, :], core.ones[:], tmp[:, j, :], start=j == 0, stop=j == 3)
                        mm.then_inc(s["abs_sum"], 1)
                    pe.wait_ge(s["even_odd"], o + 1)
                    for n, (mat, side) in enumerate(((COS0, 0), (COS1, 0), (COS_N, 0), (SIN0, 1), (SIN1, 1))):
                        for c in range(2):
                            m = 2 * n + c
                            if m >= 4:
                                pe.wait_ge(s["stored"], 10 * o + m - 3)
                            for t in range(TT):
                                mm = pe.matmul(ps[:, 4 + m % 4, :], dft[:, t, mat, :],
                                               h[:, t, side, c * BANK:(c + 1) * BANK], start=t == 0, stop=t == TT - 1)
                            mm.then_inc(s["spectrum"], 1)

            @block.scalar
            def _(act):
                for n in range(2):
                    act.wait_ge(s["bounded"], n + 1)
                    act.activation(hdn[:], x, ACT.Sin).then_inc(s["sine"], 1)
                for o in range(2):
                    act.wait_ge(s["tapped"], o + 1)
                    for c in range(2):
                        if o or c:
                            act.wait_ge(s["abs_sum"], 2 * o + c)
                        if o and not c:
                            act.wait_ge(s["even_odd"], o)
                        act.activation(tmp[:], h[:, :, :, c * BANK:(c + 1) * BANK].rearrange("p a b c -> p (a b) c"),
                                       ACT.Abs).then_inc(s["abs"], 1)
                    act.wait_ge(s["stored"], 10 * o + 4)
                    act.activation(filters[:, o, KN1, :], filters[:, o, KA1, :], ACT.Copy)

            @block.vector
            def _(dve):
                step = lambda ins: core.dve.step(dve, ins)
                for n, bias in enumerate((b1, b2)):
                    dve.wait_ge(s["arg"], n + 1)
                    if n:
                        dve.wait_ge(s["sine"], n)
                    step(dve.tensor_scalar(x, ps[0:64, 0, 0:T], bias, freq, ALU.add, ALU.mult))
                    sine_steps(core, dve, x, k, s["bounded"])
                for o in range(2):
                    dve.wait_ge(s["taps"], o + 1)
                    if o:
                        dve.wait_ge(s["spectrum"], 10)
                    for b in range(8):
                        t, a, c = b // 4, b // 2 % 2, b % 2
                        at = slice(c * BANK, (c + 1) * BANK)
                        ins = dve.tensor_tensor(h[:, t, a, at], ps[:, b, :], window[:, t, at], ALU.mult)
                    step(ins)
                    dve.memset(h[0:1, 0, 1, :], 0.0).then_inc(s["tapped"], 1)
                    for c in range(2):
                        at = slice(c * BANK, (c + 1) * BANK)
                        dve.wait_ge(s["abs_sum"], 2 * o + c + 1)
                        step(dve.tensor_scalar(norm[:, at], ps[:, c, :], EPS, None, ALU.add))
                        step(dve.reciprocal(norm[:, at], norm[:, at]))
                    sums = tmp[:].rearrange("p j c -> p (j c)").rearrange("p (t c) -> p t c", t=TT)
                    dve.wait_ge(s["tapped"], o + 1)
                    step(dve.tensor_tensor(sums, h[:, :, 0, :], h[:, :, 1, :], ALU.add))
                    step(dve.tensor_tensor(h[:, :, 1, :], h[:, :, 0, :], h[:, :, 1, :], ALU.subtract))
                    dve.tensor_copy(h[:, :, 0, :], sums).then_inc(s["even_odd"], 1)
                    for n, part in enumerate((KA0, KA1, KN0, KB0, KB1)):
                        for c in range(2):
                            m = 2 * n + c
                            at = slice(c * BANK, (c + 1) * BANK)
                            dve.wait_ge(s["spectrum"], 10 * o + m + 1)
                            dve.tensor_tensor(filters[:, o, part, at], ps[:, 4 + m % 4, :], norm[:, at],
                                              ALU.mult).then_inc(s["stored"], 1)


def hyena_stage(core, o, u, dft, inverse, filters):
    nc, ps = core.nc, core.ps
    per = {"turned": 4, "token": 4, "spectrum": 2, "product": 12, "result": 2}
    s = core.hyena_signals
    after = {n: o * c for n, c in per.items()}
    with ExitStack() as own:
        sb = lambda name, shape: own.enter_context(nc.sbuf_tensor(f"hy{o}_{name}", shape, F32))
        z, y = sb("z", [P, TT, HY]), sb("y", [P, 4, BANK])
        t1, t2 = sb("t1", [P, 2, BANK]), sb("t2", [P, 2, BANK])
        with nc.Block() as block:
            @block.tensor
            def _(pe):
                for b in range(4):
                    t, c = b // 2, b % 2
                    for j in range(4):
                        mm = pe.transpose(ps[:, b, j * P:(j + 1) * P], u[:, 4 * c + j, t * P:(t + 1) * P],
                                          core.cst["ident"])
                    mm.then_inc(s["turned"], 1)
                pe.wait_ge(s["token"], after["token"] + 4)
                for c in range(2):
                    if c:
                        pe.wait_ge(s["product"], after["product"] + 6)
                    for b, mat in enumerate((COS0, COS1, SIN_N, SIN1)):
                        for t in range(TT):
                            mm = pe.matmul(ps[:, 4 + b, :], dft[:, t, mat, :], z[:, t, c * BANK:(c + 1) * BANK],
                                           start=t == 0, stop=t == TT - 1)
                    mm.then_inc(s["spectrum"], 1)
                    pe.wait_ge(s["product"], after["product"] + 6 * c + 6)
                    for j in range(4):
                        for f in range(4):
                            mm = pe.matmul(ps[:, 2 * c + j // 2, (j % 2) * T:(j % 2 + 1) * T],
                                           y[:, f, j * P:(j + 1) * P], inverse[:, f, :], start=f == 0, stop=f == 3)
                    mm.then_inc(s["result"], 1)

            @block.scalar
            def _(act):
                for b in range(4):
                    t, c = b // 2, b % 2
                    act.wait_ge(s["turned"], after["turned"] + b + 1)
                    act.activation(z[:, t, c * BANK:(c + 1) * BANK], ps[:, b, :], ACT.Copy).then_inc(s["token"], 1)

            @block.vector
            def _(dve):
                step = lambda ins: core.dve.step(dve, ins)
                za, zb = ps[:, 4:6, :], ps[:, 6:8, :]

                def gate(c):
                    dve.wait_ge(s["result"], after["result"] + c + 1)
                    for j in range(4):
                        n = 4 * c + j
                        bank = ps[:, 2 * c + j // 2, (j % 2) * T:(j % 2 + 1) * T]
                        step(dve.scalar_tensor_tensor(u[:, n, :], u[:, n, :],
                                                      core.prm["hy_bias"][:, o * HT + n:o * HT + n + 1], bank,
                                                      ALU.mult, ALU.add))
                    at = slice(4 * c, 4 * c + 4)
                    gates = slice((o + 1) * HT + 4 * c, (o + 1) * HT + 4 * c + 4)
                    step(dve.tensor_tensor(u[:, at, :], u[:, at, :], u[:, gates, :], ALU.mult))

                for c in range(2):
                    at = slice(c * BANK, (c + 1) * BANK)
                    dve.wait_ge(s["spectrum"], after["spectrum"] + c + 1)
                    if c:
                        dve.wait_ge(s["result"], after["result"] + 1)
                    k = lambda n: filters[:, o, n:n + 2, at]
                    dve.tensor_tensor(t1[:], za, k(KA0), ALU.mult).then_inc(s["product"], 1)
                    dve.tensor_tensor(t2[:], zb, k(KB0), ALU.mult).then_inc(s["product"], 1)
                    dve.wait_ge(s["product"], after["product"] + 6 * c + 2)
                    dve.tensor_tensor(y[:, 0:2, :], t1[:], t2[:], ALU.subtract).then_inc(s["product"], 1)
                    dve.wait_ge(s["product"], after["product"] + 6 * c + 3)
                    dve.tensor_tensor(t1[:], za, k(KB0), ALU.mult).then_inc(s["product"], 1)
                    dve.tensor_tensor(t2[:], zb, k(KN0), ALU.mult).then_inc(s["product"], 1)
                    dve.wait_ge(s["product"], after["product"] + 6 * c + 5)
                    dve.tensor_tensor(y[:, 2:4, :], t1[:], t2[:], ALU.add).then_inc(s["product"], 1)
                gate(0)
                gate(1)


def ssd_state_stage(core, ssd, xbc, xbc_ctx):
    nc, ps = core.nc, core.ps
    F, B = 0, 1
    s = {n: core.sem(f"state_{n}") for n in ("turned", "token", "xdt", "weighted", "sum", "taken")}
    NX = HEADS * HEAD
    jobs = [(2, F), (3, F), (3, B), (2, B), (0, F), (1, B)]
    extra = [(0, B), (1, F)]
    with ExitStack() as own:
        sb = lambda name, shape: own.enter_context(nc.sbuf_tensor(f"st_{name}", shape, F32))
        tok = sb("tok", [P, 4, NX + 2 * P])
        ctx_xdt, xw = sb("ctx_xdt", [P, HEADS, HEAD]), sb("xw", [P, 2, HEADS, HEAD])
        with nc.Block() as block:
            tiles = [(0, 4), (4, 4), (8, 2)]

            @block.tensor
            def _(pe):
                n = 0
                for q in (2, 3, 0, 1):
                    src = xbc if q < 2 else xbc_ctx
                    at = slice((q % 2) * P, (q % 2 + 1) * P)
                    for first, count in tiles:
                        if n >= 4:
                            pe.wait_ge(s["token"], n - 3)
                        for j in range(count):
                            mm = pe.transpose(ps[:, n % 4, j * P:(j + 1) * P], src[:, first + j, at], core.cst["ident"])
                        mm.then_inc(s["turned"], 1)
                        n += 1
                for j, (q, d) in enumerate(jobs):
                    pe.wait_ge(s["weighted"], j + 1)
                    if j >= 2:
                        pe.wait_ge(s["taken"], j - 1)
                    if j == 0:
                        pe.wait_ge(s["token"], 12)
                    for g in range(2):
                        mm = pe.matmul(ps[:, 4 + 2 * (j % 2) + g, :], tok[:, q, NX + g * P:NX + (g + 1) * P],
                                       xw[:, j % 2, 8 * g:8 * g + 8, :].rearrange("p h e -> p (h e)"),
                                       start=True, stop=True)
                    mm.then_inc(s["sum"], 1)

            @block.scalar
            def _(act):
                n = 0
                for q in (2, 3, 0, 1):
                    for first, count in tiles:
                        act.wait_ge(s["turned"], n + 1)
                        act.activation(tok[:, q, first * P:(first + count) * P], ps[:, n % 4, 0:count * P],
                                       ACT.Copy).then_inc(s["token"], 1)
                        n += 1

            @block.vector
            def _(dve):
                step = lambda ins: core.dve.step(dve, ins)
                ready = {2: 3, 3: 6, 0: 9, 1: 12}
                heads = lambda d: slice(d * HEADS, (d + 1) * HEADS)

                def take(j):
                    q, d = jobs[j]
                    dve.wait_ge(s["sum"], j + 1)
                    sums = ps[:, 4 + 2 * (j % 2):6 + 2 * (j % 2), :].rearrange("p g (h e) -> p (g h) e", e=HEAD)
                    etot = lambda q, d: spread(ssd.etot[:, q, heads(d)], 2, HEAD)
                    first = {F: 0, B: 1}[d]
                    dst = ssd.state[:, d, first if q >= 2 else 1 - first]
                    if j in (0, 2):
                        ins = dve.tensor_tensor(dst, sums, etot(5 - q, d), ALU.mult)
                    elif j in (1, 3):
                        ins = dve.tensor_tensor(dst, dst, sums, ALU.add)
                    else:
                        step(dve.tensor_tensor(dst, ssd.state[:, d, first], etot(q, d), ALU.mult))
                        ins = dve.tensor_tensor(dst, dst, sums, ALU.add)
                    ins.then_inc(s["taken"], 1)
                    dve.wait_ge(s["taken"], j + 1)

                for j, (q, d) in enumerate(jobs + extra):
                    dve.wait_ge(s["token"], ready[q])
                    x = tok[:, q, 0:NX].rearrange("p (h e) -> p h e", e=HEAD)
                    xdt = ctx_xdt[:] if q >= 2 else ssd.xdt[:, q, d]
                    step(dve.tensor_tensor(xdt, x, spread(ssd.dt[:, q, heads(d)], 2, HEAD), ALU.mult))
                    if j < len(jobs):
                        if j >= 2:
                            take(j - 2)
                        dve.tensor_tensor(xw[:, j % 2], xdt, spread(ssd.to_end[:, q, heads(d)], 2, HEAD),
                                          ALU.mult).then_inc(s["weighted"], 1)
                        dve.wait_ge(s["weighted"], j + 1)
                take(4)
                take(5)


def ssd_scan_stage(core, ssd, xbc, gate):
    nc, ps = core.nc, core.ps
    s = {n: core.sem(f"scan_{n}") for n in ("cb", "cum", "diff", "grown", "decay", "kernel", "turned_c", "y", "cbm")}
    units = [(c, h4) for c in range(TT) for h4 in range(4)]
    with ExitStack() as own:
        sb = lambda name, shape: own.enter_context(nc.sbuf_tensor(f"scan_{name}", shape, F32))
        cbm = sb("cbm", [P, TT, 2, 2, P])
        grown, decay = sb("grown", [P, 2, 2, 4, P]), sb("decay", [P, 2, 2, 4, P])
        with nc.Block() as block:
            @block.tensor
            def _(pe):
                for c in range(TT):
                    at = slice(c * P, (c + 1) * P)
                    for g in range(2):
                        mm = pe.matmul(ps[:, 2, (2 * c + g) * P:(2 * c + g + 1) * P], xbc[:, 8 + g, at],
                                       xbc[:, 10 + g, at], start=True, stop=True)
                mm.then_inc(s["cb"], 1)

                def sums(u):
                    c, h4 = units[u]
                    if u == 1:
                        pe.wait_ge(s["cbm"], 8)
                    if u >= 2:
                        pe.wait_ge(s["grown"], 2 * u - 2)
                    for d, tri in enumerate(("tri_f", "tri_b")):
                        for h in range(4):
                            hd = d * HEADS + 4 * h4 + h
                            mm = pe.matmul(ps[:, 2 * (u % 2) + d, h * P:(h + 1) * P],
                                           ssd.da[:, c, hd:hd + 1].broadcast_to([P, P]), core.cst[tri],
                                           start=True, stop=True)
                        mm.then_inc(s["cum"], 1)

                sums(0)
                for u, (c, h4) in enumerate(units):
                    if u + 1 < len(units):
                        sums(u + 1)
                    pe.wait_ge(s["kernel"], 2 * u + 2)
                    pe.wait_ge(s["turned_c"], 2 * u + 2)
                    for h in range(4):
                        head = 4 * h4 + h
                        ft, row = head // 2, (head % 2) * HEAD
                        out = ps[row:row + HEAD, 4 + ft // 2, (ft % 2) * T + c * P:(ft % 2) * T + (c + 1) * P]
                        for d in range(2):
                            pe.matmul(out, ssd.xdt[:, c, d, head, :], decay[:, u % 2, d, h, :],
                                      start=d == 0, stop=False)
                            mm = pe.matmul(out, ssd.state[:, d, c, head, :], grown[:, u % 2, d, h, :],
                                           start=False, stop=d == 1)
                    mm.then_inc(s["y"], 1)

            @block.scalar
            def _(act):
                for u in range(len(units)):
                    if u >= 2:
                        act.wait_ge(s["y"], u - 1)
                    for d in range(2):
                        act.wait_ge(s["diff"], 2 * u + d + 1)
                        act.activation(grown[:, u % 2, d].rearrange("p h l -> p (h l)"),
                                       ps[:, 2 * (u % 2) + d, :],
                                       ACT.Exp).then_inc(s["grown"], 1)
                    for d in range(2):
                        act.activation(decay[:, u % 2, d], decay[:, u % 2, d], ACT.Exp).then_inc(s["decay"], 1)

            @block.vector
            def _(dve):
                dve.wait_ge(s["cb"], 1)
                for c in range(TT):
                    for g in range(2):
                        for d, tri in enumerate(("tri_f", "tri_b")):
                            dve.tensor_tensor(cbm[:, c, g, d, :], ps[:, 2, (2 * c + g) * P:(2 * c + g + 1) * P],
                                              core.cst[tri], ALU.mult).then_inc(s["cbm"], 1)
                dve.wait_ge(s["cbm"], 8)

                def diffs(u):
                    c, h4 = units[u]
                    if u >= 2:
                        dve.wait_ge(s["y"], u - 1)
                    for d in range(2):
                        dve.wait_ge(s["cum"], 2 * u + d + 1)
                        for h in range(4):
                            hd = d * HEADS + 4 * h4 + h
                            ins = dve.tensor_scalar(decay[:, u % 2, d, h, :], ps[:, 2 * (u % 2) + d, h * P:(h + 1) * P],
                                                    ssd.cum[:, c, hd:hd + 1], 0.0, ALU.subtract, ALU.min)
                        ins.then_inc(s["diff"], 1)

                diffs(0)
                for u, (c, h4) in enumerate(units):
                    if u + 1 < len(units):
                        diffs(u + 1)
                    g = h4 // 2
                    for d in range(2):
                        slot = grown[:, u % 2, d]
                        dve.wait_ge(s["grown"], 2 * u + d + 1)
                        dve.tensor_tensor(slot, slot, spread(xbc[:, 10 + g, c * P:(c + 1) * P], 1, 4),
                                          ALU.mult).then_inc(s["turned_c"], 1)
                    for d in range(2):
                        slot = decay[:, u % 2, d]
                        dve.wait_ge(s["decay"], 2 * u + d + 1)
                        dve.tensor_tensor(slot, slot, spread(cbm[:, c, g, d, :], 1, 4), ALU.mult).then_inc(s["kernel"], 1)
                dve.wait_ge(s["y"], len(units))
                for ft in range(HT):
                    ins = dve.scalar_tensor_tensor(xbc[:, ft, :], xbc[:, ft, :], core.prm["ssd_d"][:, ft:ft + 1],
                                                   ps[:, 4 + ft // 2, (ft % 2) * T:(ft % 2 + 1) * T],
                                                   ALU.mult, ALU.add)
                core.dve.step(dve, ins)
                dve.tensor_tensor(xbc[:, 0:HT, :], xbc[:, 0:HT, :], gate[:], ALU.mult)


def mixer_norm_stage(core, z, y):
    nc, ps = core.nc, core.ps
    s = {n: core.sem(f"mixnorm_{n}") for n in ("squared", "summed", "rooted")}
    with ExitStack() as own:
        sb = lambda name, shape: own.enter_context(nc.sbuf_tensor(f"mn_{name}", shape, F32))
        sq, std = sb("sq", [P, 2 * HT, T]), sb("std", [P, HT + 2, T])
        with nc.Block() as block:
            @block.scalar
            def _(act):
                act.activation(sq[:, 0:HT, :], z[:, 0:HT, :], ACT.Square).then_inc(s["squared"], 1)
                act.activation(sq[:, HT:, :], y[:, 0:HT, :], ACT.Square).then_inc(s["squared"], 1)
                act.wait_ge(s["summed"], 1)
                eps = core.small[:, EPS_COL:EPS_COL + 1]
                act.activation(std[:, 0:HT, :].rearrange("p (b j) t -> p b (j t)", j=2), ps[:, 0:4, :], ACT.Sqrt,
                               bias=eps, scale=1.0 / P).then_inc(s["rooted"], 1)
                act.wait_ge(s["summed"], 2)
                act.activation(std[:, HT:, :], ps[:, 4:6, 0:T], ACT.Sqrt, bias=eps,
                               scale=2.0 / HY).then_inc(s["rooted"], 1)

            @block.tensor
            def _(pe):
                pe.wait_ge(s["squared"], 1)
                for b in range(4):
                    mm = pe.matmul(ps[:, b, :], core.ones[:], sq[:, 2 * b:2 * b + 2, :].rearrange("p j t -> p (j t)"),
                                   start=True, stop=True)
                mm.then_inc(s["summed"], 1)
                pe.wait_ge(s["squared"], 2)
                for g in range(2):
                    for j in range(4):
                        mm = pe.matmul(ps[:, 4 + g, 0:T], core.ones[:], sq[:, HT + 4 * g + j, :],
                                       start=j == 0, stop=j == 3)
                mm.then_inc(s["summed"], 1)

            @block.vector
            def _(dve):
                for half, (at, src, gain) in enumerate(((slice(0, HT), z, "hy_norm"), (slice(HT, HT + 2), y, "ssd_norm"))):
                    dve.wait_ge(s["rooted"], half + 1)
                    core.dve.step(dve, dve.reciprocal(std[:, at, :], std[:, at, :]))
                    for t in range(HT):
                        r = std[:, t, :] if half == 0 else std[:, HT + t // 4, :]
                        dve.scalar_tensor_tensor(core.h[:, half * HT + t, :], src[:, t, :],
                                                 core.prm[gain][:, t:t + 1], r, ALU.mult, ALU.mult)


def first_block(core):
    nc = core.nc


    class Ssd:
        pass

    with ExitStack() as mixer:
        sb = lambda name, shape: mixer.enter_context(nc.sbuf_tensor(name, shape, F32))
        u, xbc, zg = sb("u", [P, HY_TILES, T]), sb("xbc", [P, XBC_TILES, T]), sb("zg", [P, Z_TILES, T])
        xbc_ctx = sb("xbc_ctx", [P, XBC_TILES, T])
        ssd = Ssd()
        ssd.dt, ssd.da, ssd.cum, ssd.to_end, ssd.etot = (sb(f"ssd_{n}", [P, 4, 2 * HEADS])
                                                         for n in ("dt", "da", "cum", "to_end", "etot"))
        with ExitStack() as projections:
            sb2 = lambda name, shape: projections.enter_context(nc.sbuf_tensor(name, shape, F32))
            ctx_tile, wdt = sb2("context", [P, KD, T]), sb2("wdt", [P, KD, 2 * HEADS])
            start_stage(core, ctx_tile, [(wdt[:], "w_dt")])
            shift = core.mod[:, 0:KD, :]
            rms_stage(core, "norm_x", core.x, core.h, KD, core.gain[:, 0:KD], shift[:, :, 0])
            rms_stage(core, "norm_ctx", ctx_tile, ctx_tile, KD, core.gain[:, KD:2 * KD], shift[:, :, 1])
            conv3_stage(core, "hy_in", "w_mix", HY_TILES, ("w_mix", HY_TILES), [core.h], 0, [u],
                        core.prm["hy_conv_w"], core.prm["hy_conv_b"], [GRID])
            conv3_stage(core, "xbc_in", "w_mix", XBC_TILES, ("w_mix", HY_TILES + XBC_TILES),
                        [core.h, ctx_tile], HY_TILES, [xbc, xbc_ctx],
                        core.prm["ssd_conv_w"], core.prm["ssd_conv_b"], [GRID, T])

            def silu_z(act, banks, n, i, s):
                return act.activation(zg[:, n, :], banks[0], ACT.Silu)

            linear_stage(core, "z_in", "w_mix", Z_TILES, ("w_out", 0), [core.h], silu_z,
                         first=HY_TILES + XBC_TILES)
            with nc.Block() as block:
                @block.scalar
                def _(act):
                    act.activation(xbc[:], xbc[:], ACT.Silu)
                    act.activation(xbc_ctx[:], xbc_ctx[:], ACT.Silu)
            dt_stage(core, wdt, ctx_tile, ssd)
        with ExitStack() as hyena:
            sb2 = lambda name, shape: hyena.enter_context(nc.sbuf_tensor(name, shape, F32))
            dft, inverse = sb2("dft", [P, TT, 6, P]), sb2("inverse", [P, 4, T])
            filters = sb2("filters", [P, 2, 6, HY])
            dft_loaded = core.sem("dft_loaded")
            with nc.Block() as block:
                @block.sync
                def _(sp):
                    sp.dma_start(dft[:], core.dram["dft"]).then_inc(dft_loaded, 16)
                    sp.dma_start(inverse[:], core.dram["inverse"]).then_inc(dft_loaded, 16)
                    sp.wait_ge(dft_loaded, 32)
            filter_stage(core, dft, filters)
            for o in range(2):
                hyena_stage(core, o, u, dft, inverse, filters)
        with ExitStack() as scan:
            sb2 = lambda name, shape: scan.enter_context(nc.sbuf_tensor(name, shape, F32))
            ssd.state = sb2("ssd_state", [P, 2, TT, HEADS, HEAD])
            ssd.xdt = sb2("ssd_xdt", [P, TT, 2, HEADS, HEAD])
            ssd_state_stage(core, ssd, xbc, xbc_ctx)
            ssd_scan_stage(core, ssd, xbc, zg)
        mixer_norm_stage(core, u, xbc)

    def gated(part):
        def drain(dve, banks, n, i, s):
            at = bass.ds(n + part * KD, 1)
            return dve.scalar_tensor_tensor(core.x[:, n, :], banks[0], core.mod[:, at, 0], core.x[:, n, :],
                                            ALU.mult, ALU.add)
        return drain

    linear_stage(core, "mix_out", "w_out", KD, ("w_mlp1", 0), [core.h], gated(2), "vector")
    rms_stage(core, "norm_mlp", core.x, core.h, KD, core.gain[:, 2 * KD:3 * KD], core.mod[:, 3 * KD:4 * KD, 0])
    with nc.sbuf_tensor("hidden", [P, MLP_TILES, T], F32) as hidden:
        base = core.drained.base

        def relu(act, banks, n, i, s):
            return act.activation(hidden[:, n, :], banks[0], ACT.Relu)

        def square(block):
            @block.vector
            def _(dve):
                with dve.Fori(0, MLP_TILES // RING) as i:
                    for s in range(RING):
                        dve.wait_ge(core.drained.sem, i * RING + (base + s + 1))
                        v = hidden[:, i * RING + s, :]
                        dve.tensor_tensor(v, v, v, ALU.mult)

        linear_stage(core, "mlp1", "w_mlp1", MLP_TILES, ("w_mlp2", 0), [core.h], relu, helper=square)
        linear_stage(core, "mlp2", "w_mlp2", KD, ("w_in_2", 0), [hidden], gated(5), "vector", kc=4)
    rms_stage(core, "norm_first", core.x, core.x, KD, core.prm["final1"])


def s5_setup_stage(core, s5):
    nc, dram = core.nc, core.dram
    s = {n: core.sem(f"s5_{n}") for n in ("loaded", "c_loaded", "cleared", "dt", "rate", "exp", "bounded", "sine")}
    W = HT * 64
    with ExitStack() as own:
        sb = lambda name, shape: own.enter_context(nc.sbuf_tensor(f"s5_{name}", shape, F32))
        rep = sb("rep", [P, 5, W])
        dt, e, trig, k = sb("dt", [P, W]), sb("e", [P, W]), sb("trig", [P, 2, W]), sb("k", [P, 2, W])
        kr, ki, t1, t2, inv = (sb(n, [P, W]) for n in ("kr", "ki", "t1", "t2", "inv"))
        sdt = sb("sdt", [P, PAIRS])
        sk = sb("sk", [P, PAIRS])
        with nc.Block() as block:
            @block.sync
            def _(sp):
                sp.dma_start(rep[:], dram["s5_rep"]).then_inc(s["loaded"], 16)
                sp.wait_ge(s["cleared"], 1)
                for g in range(2):
                    for part in range(2):
                        sp.dma_start(s5.c[g * 64:(g + 1) * 64, part, :, g * 16:(g + 1) * 16],
                                     dram["s5_c"][part, g * 64:(g + 1) * 64]).then_inc(s["c_loaded"], 16)

            @block.scalar
            def _(act):
                act.activation(sdt[:], core.prm["log_dt"], ACT.Exp).then_inc(s["dt"], 1)
                act.wait_ge(s["loaded"], 16)
                act.activation(dt[:], rep[:, 2, :], ACT.Exp).then_inc(s["dt"], 1)
                act.wait_ge(s["rate"], 1)
                act.activation(s5.r[:], s5.r[:], ACT.Exp)
                act.wait_ge(s["rate"], 2)
                act.activation(e[:], e[:], ACT.Exp).then_inc(s["exp"], 1)
                act.wait_ge(s["bounded"], 1)
                act.activation(trig[:], trig[:], ACT.Sin).then_inc(s["sine"], 1)

            @block.vector
            def _(dve):
                step = lambda ins: core.dve.step(dve, ins)
                mul = lambda out, a, b: step(dve.tensor_tensor(out, a, b, ALU.mult))
                dve.memset(s5.c[:], 0.0).then_inc(s["cleared"], 1)
                dve.wait_ge(s["dt"], 1)
                dve.tensor_tensor(s5.r[:], core.prm["lam_re"], sdt[:], ALU.mult).then_inc(s["rate"], 1)
                mul(s5.turn[:], core.prm["lam_im"], sdt[:])
                step(dve.tensor_scalar(s5.turn[:], s5.turn[:], 1 / (2 * math.pi), None, ALU.mult))
                step(dve.tensor_scalar(sk[:], s5.turn[:], MAGIC, None, ALU.add))
                step(dve.tensor_scalar(sk[:], sk[:], -MAGIC, None, ALU.add))
                step(dve.tensor_tensor(s5.turn[:], s5.turn[:], sk[:], ALU.subtract))
                dve.wait_ge(s["dt"], 2)
                dve.tensor_tensor(e[:], rep[:, 0, :], dt[:], ALU.mult).then_inc(s["rate"], 1)
                mul(trig[:, 0, :], rep[:, 1, :], dt[:])
                step(dve.tensor_scalar(trig[:, 1, :], trig[:, 0, :], math.pi / 2, None, ALU.add))
                sine_steps(core, dve, trig[:], k[:], s["bounded"])
                mul(t1[:], rep[:, 0, :], rep[:, 0, :])
                mul(t2[:], rep[:, 1, :], rep[:, 1, :])
                step(dve.tensor_tensor(inv[:], t1[:], t2[:], ALU.add))
                step(dve.reciprocal(inv[:], inv[:]))
                dve.wait_ge(s["exp"], 1)
                dve.wait_ge(s["sine"], 1)
                re, im = k[:, 0, :], k[:, 1, :]
                mul(re, e[:], trig[:, 1, :])
                step(dve.tensor_scalar(re, re, -1.0, None, ALU.add))
                mul(im, e[:], trig[:, 0, :])
                mul(t1[:], re, rep[:, 0, :])
                mul(t2[:], im, rep[:, 1, :])
                step(dve.tensor_tensor(kr[:], t1[:], t2[:], ALU.add))
                mul(kr[:], kr[:], inv[:])
                mul(t1[:], im, rep[:, 0, :])
                mul(t2[:], re, rep[:, 1, :])
                step(dve.tensor_tensor(ki[:], t1[:], t2[:], ALU.subtract))
                mul(ki[:], ki[:], inv[:])
                for part, (a, b, op) in enumerate(((kr, ki, ALU.subtract), (ki, kr, ALU.add))):
                    mul(t1[:], a[:], rep[:, 3, :])
                    mul(t2[:], b[:], rep[:, 4, :])
                    step(dve.tensor_tensor(t1[:], t1[:], t2[:], op))
                    for g in range(2):
                        step(dve.tensor_scalar(s5.b[:, :, part, g, :], t1[:].rearrange("p (f e) -> p f e", e=64),
                                               core.cst["group"][:, g:g + 1], None, ALU.mult))
                dve.wait_ge(s["c_loaded"], 64)
                step(dve.tensor_scalar(s5.c[:, 1], s5.c[:, 1], -1.0, None, ALU.mult))
                dve.tensor_scalar(s5.c[:, 2], s5.c[:, 0], -1.0, None, ALU.mult)


MAGIC = 12582912.0


def local_mixers_stage(core, s5, proj, conv):
    nc, ps = core.nc, core.ps
    s = {n: core.sem(f"mix_{n}") for n in ("glu", "diag", "conv", "convolved", "phase", "trig", "bu", "turned",
                                           "rotated", "scan_r", "scan_i", "out_c", "out_s", "y", "skip", "summed")}
    pad = CONV31 - 1
    with ExitStack() as own:
        sb = lambda name, shape: own.enter_context(nc.sbuf_tensor(f"mix_{name}", shape, F32))
        c = sb("c", [P, HT, pad + T])
        diag = sb("diag", [P, 2, CONV31, P])
        phase, whole, trig = sb("phase", [P, 2, 2, T]), sb("whole", [P, 2, T]), sb("trig", [P, 2, 2, T])
        p1, p2, bt, v = sb("p1", [P, 2, T]), sb("p2", [P, 2, T]), sb("bt", [P, 2, T]), sb("v", [P, 2, 2, T])
        oc, os = sb("oc", [P, 2, 2, T]), sb("os", [P, 2, 2, T])
        with nc.Block() as block:
            @block.gpsimd
            def _(pool):
                step = lambda ins: core.pool.step(pool, ins)

                def make_diag(f):
                    if f >= 2:
                        pool.wait_ge(s["conv"], f - 1)
                    taps = core.prm["conv_w"][:, f * CONV31:(f + 1) * CONV31]
                    pool.tensor_tensor(diag[:, f % 2], spread(core.cst["ident"], 1, CONV31), spread(taps, 2, P),
                                       ALU.mult).then_inc(s["diag"], 1)

                def make_phase(n):
                    if n >= 2:
                        pool.wait_ge(s["trig"], n - 1)
                    ph, turn = phase[:, n % 2], s5.turn[:, n:n + 1]
                    pool.tensor_scalar(ph[:, 0, :], core.cst["iota"], turn, None, ALU.mult)
                    step(pool.tensor_scalar(ph[:, 1, :], core.cst["iota"], turn, 0.25, ALU.mult, ALU.add))
                    step(pool.tensor_scalar(whole[:], ph, MAGIC, -MAGIC, ALU.add, ALU.add))
                    pool.tensor_tensor(ph, ph, whole[:], ALU.subtract).then_inc(s["phase"], 1)

                make_diag(0)
                make_phase(0)
                make_phase(1)
                for n in range(PAIRS):
                    if n % 4 == 1 and n // 4 + 1 < HT:
                        make_diag(n // 4 + 1)
                    if n + 2 < PAIRS:
                        make_phase(n + 2)
                    pool.wait_ge(s["scan_i"], n + 1)
                    if n >= 2:
                        pool.wait_ge(s["y"], n - 1)
                    pool.tensor_tensor(os[:, n % 2], v[:, n % 2], spread(trig[:, n % 2, 0, :], 1, 2),
                                       ALU.mult).then_inc(s["out_s"], 1)

            @block.scalar
            def _(act):
                for n in range(PAIRS):
                    act.wait_ge(s["phase"], n + 1)
                    if n >= 2:
                        act.wait_ge(s["out_c"], n - 1)
                        act.wait_ge(s["out_s"], n - 1)
                    act.activation(trig[:, n % 2], phase[:, n % 2], ACT.Sin, scale=TWO_PI).then_inc(s["trig"], 1)
                    if n % 4 == 3:
                        f = n // 4
                        act.wait_ge(s["conv"], f + 1)
                        act.activation(conv[:, f, :], ps[:, 6 + f % 2, 0:T], ACT.Identity,
                                       bias=core.prm["conv_b"][:, f:f + 1]).then_inc(s["convolved"], 1)

            @block.tensor
            def _(pe):
                def outputs(n):
                    f, q = n // 4, n % 4
                    if q == 0 and f >= 2:
                        pe.wait_ge(s["skip"], f - 1)
                    pe.wait_ge(s["out_c"], n + 1)
                    pe.wait_ge(s["out_s"], n + 1)
                    terms = ((0, oc, 0), (2, os, 1), (1, os, 0), (1, oc, 1))
                    for m, (part, src, half) in enumerate(terms):
                        mm = pe.matmul(ps[32 * q:32 * q + 32, 2 + f % 2, 0:T], s5.c[:, part, n, :],
                                       src[:, n % 2, half, :], start=m == 0, stop=m == 3)
                    mm.then_inc(s["y"], 1)

                for n in range(PAIRS):
                    f, q = n // 4, n % 4
                    if n >= 2:
                        pe.wait_ge(s["turned"], n - 1)
                    rows = slice(32 * q, 32 * q + 32)
                    for part in range(2):
                        mm = pe.matmul(ps[:, n % 2, part * T:(part + 1) * T],
                                       s5.b[rows, f, part].rearrange("p g e -> p (g e)"),
                                       proj[rows, 2 * HT + f, :], start=True, stop=True)
                    mm.then_inc(s["bu"], 1)
                    if n:
                        outputs(n - 1)
                    if q == 2:
                        pe.wait_ge(s["diag"], f + 1)
                        pe.wait_ge(s["glu"], 1)
                        if f >= 2:
                            pe.wait_ge(s["convolved"], f - 1)
                        for k in range(CONV31):
                            mm = pe.matmul(ps[:, 6 + f % 2, 0:T], diag[:, f % 2, k, :], c[:, f, k:k + T],
                                           start=k == 0, stop=k == CONV31 - 1)
                        mm.then_inc(s["conv"], 1)
                outputs(PAIRS - 1)

            @block.vector
            def _(dve):
                dve.memset(c[:, :, 0:pad], 0.0)
                dve.tensor_tensor(c[:, :, pad:], proj[:, 0:HT, :], proj[:, HT:2 * HT, :], ALU.mult).then_inc(s["glu"], 1)

                def skip(f):
                    dve.wait_ge(s["y"], 4 * f + 4)
                    u = proj[:, 2 * HT + f, :]
                    dve.scalar_tensor_tensor(u, u, core.prm["ssm_d"][:, f:f + 1], ps[:, 2 + f % 2, 0:T],
                                             ALU.mult, ALU.add).then_inc(s["skip"], 1)

                for n in range(PAIRS):
                    dve.wait_ge(s["bu"], n + 1)
                    dve.wait_ge(s["trig"], n + 1)
                    bu = ps[:, n % 2, :].rearrange("p (a t) -> p a t", a=2)
                    cos, sin = (spread(trig[:, n % 2, a, :], 1, 2) for a in (1, 0))
                    dve.tensor_tensor(p1[:], bu, cos, ALU.mult)
                    dve.tensor_tensor(p2[:], bu, sin, ALU.mult).then_inc(s["turned"], 1)
                    dve.wait_ge(s["turned"], n + 1)
                    dve.tensor_tensor(bt[:, 0, :], p1[:, 0, :], p2[:, 1, :], ALU.add).then_inc(s["rotated"], 1)
                    dve.tensor_tensor(bt[:, 1, :], p1[:, 1, :], p2[:, 0, :], ALU.subtract).then_inc(s["rotated"], 1)
                    if n >= 2:
                        dve.wait_ge(s["out_s"], n - 1)
                    rate = s5.r[:, n:n + 1].broadcast_to([P, T])
                    for a, done in enumerate(("scan_r", "scan_i")):
                        dve.wait_ge(s["rotated"], 2 * n + a + 1)
                        dve.tensor_tensor_scan(v[:, n % 2, a, :], rate, bt[:, a, :], 0.0, ALU.mult,
                                               ALU.add).then_inc(s[done], 1)
                    dve.wait_ge(s["scan_r"], n + 1)
                    dve.wait_ge(s["scan_i"], n + 1)
                    if n >= 2:
                        dve.wait_ge(s["y"], n - 1)
                    dve.tensor_tensor(oc[:, n % 2], v[:, n % 2], cos, ALU.mult).then_inc(s["out_c"], 1)
                    if n % 4 == 1 and n > 4:
                        skip(n // 4 - 1)
                skip(HT - 1)


def glu_stage(core, y, next_w):
    nc, ps = core.nc, core.ps
    used = core.used
    s = {n: core.sem(f"glu_{n}") for n in ("gelu", "sigmoid")}
    with nc.sbuf_tensor("glu_gate", [P, HT, T], F32) as gate, nc.Block() as block:
        @block.sync
        def _(sp):
            stream(core, sp, "w_glu", RING, next_w)

        @block.scalar
        def _(act):
            act.activation(y, y, ACT.Gelu_apprx_tanh).then_inc(s["gelu"], 1)
            for m in range(RING):
                act.wait_ge(used.sem, used.base + m + 1)
                act.activation(gate[:, 2 * m:2 * m + 2, :], ps[:, 2 * m:2 * m + 2, 0:T],
                               ACT.Sigmoid).then_inc(s["sigmoid"], 1)

        @block.tensor
        def _(pe):
            pe.wait_ge(s["gelu"], 1)
            for m in range(RING):
                pe.wait_ge(core.landed[m], 16 * (used.base // RING + 1))
                for n in range(2):
                    for k in range(HT):
                        mm = pe.matmul(ps[:, 2 * m + n, 0:T], core.ring[:, m, n * HT + k, :], y[:, k, :],
                                       start=k == 0, stop=k == HT - 1)
                mm.then_inc(used.sem, 1)

        @block.vector
        def _(dve):
            dve.wait_ge(s["sigmoid"], RING)
            dve.tensor_tensor(y, y, gate[:], ALU.mult)
    used.base += RING


def group_norm_stage(core, c, y):
    nc, ps = core.nc, core.ps
    s = {n: core.sem(f"gn_{n}") for n in ("sums", "squared", "centred", "rooted", "scaled", "silu", "ssm_out", "conv_out")}
    width = HT * P
    with ExitStack() as own:
        sb = lambda name, shape: own.enter_context(nc.sbuf_tensor(f"gn_{name}", shape, F32))
        sq, std = sb("sq", [P, HT, T]), sb("std", [P, 3, T])
        with nc.Block() as block:
            @block.tensor
            def _(pe):
                def total(bank, src):
                    for t in range(HT):
                        mm = pe.matmul(ps[:, bank, 0:T], core.ones[:], src[:, t, :], start=t == 0, stop=t == HT - 1)
                    mm.then_inc(s["sums"], 1)
                total(0, c)
                for n in range(3):
                    pe.wait_ge(s["squared"], n + 1)
                    total(n + 1, sq)

            @block.scalar
            def _(act):
                eps = core.small[:, EPS_COL:EPS_COL + 1]

                def root(n):
                    act.wait_ge(s["sums"], n + 2)
                    act.activation(std[:, n, :], ps[:, n + 1, 0:T], ACT.Sqrt, bias=eps,
                                   scale=1.0 / width).then_inc(s["rooted"], 1)
                act.activation(sq[:], y, ACT.Square).then_inc(s["squared"], 1)
                root(0)
                act.wait_ge(s["centred"], 1)
                act.activation(sq[:], c, ACT.Square).then_inc(s["squared"], 1)
                root(1)
                for t in range(HT):
                    act.wait_ge(s["scaled"], t + 1)
                    act.activation(c[:, t, :], c[:, t, :], ACT.Silu, bias=core.prm["ln_b"][:, t:t + 1]).then_inc(s["silu"], 1)
                act.wait_ge(s["silu"], HT)
                act.activation(sq[:], c, ACT.Square).then_inc(s["squared"], 1)
                root(2)

            @block.vector
            def _(dve):
                dve.wait_ge(s["sums"], 1)
                dve.scalar_tensor_tensor(c, spread(ps[:, 0, 0:T], 1, HT), -1.0 / width, c, ALU.mult,
                                         ALU.add).then_inc(s["centred"], 1)
                for n, (src, dst, gain) in enumerate(((y, core.h[:, HT:, :], "grp_ssm"), (c, c, "ln_g"),
                                                      (c, core.h[:, 0:HT, :], "grp_conv"))):
                    dve.wait_ge(s["rooted"], n + 1)
                    core.dve.step(dve, dve.reciprocal(std[:, n, :], std[:, n, :]))
                    for t in range(HT):
                        dve.scalar_tensor_tensor(dst[:, t, :], src[:, t, :], core.prm[gain][:, t:t + 1], std[:, n, :],
                                                 ALU.mult, ALU.mult).then_inc(s[("ssm_out", "scaled", "conv_out")[n]], 1)


def values_stage(core, mem, v, next_w):
    nc, ps = core.nc, core.ps
    used, drained = core.used, core.drained
    with nc.Block() as block:
        @block.sync
        def _(sp):
            stream(core, sp, "w_v", 16, next_w)

        @block.tensor
        def _(pe):
            with pe.Fori(0, 2) as i:
                for b in range(2):
                    for s in range(RING):
                        piece_landed(core, pe, s, i * 2, b)
                        if s == 0:
                            pe.wait_ge(drained.sem, i * 2 + (drained.base + b - 1))
                        w = core.ring[:, s].rearrange("p k m -> p (k m)").rearrange("p (k n) -> p k n", k=4)
                        for k in range(4):
                            for m in range(TT):
                                mm = pe.matmul(ps[:, 2 * b + m, :], mem[:, 4 * s + k, m * P:(m + 1) * P], w[:, k, :],
                                               start=(s, k) == (0, 0), stop=(s, k) == (3, 3))
                        mm.then_inc(used.sem, 1)

        @block.scalar
        def _(act):
            with act.Fori(0, 2) as i:
                for b in range(2):
                    act.wait_ge(used.sem, i * 8 + (used.base + 4 * b + 4))
                    act.activation(v[:, :, i * 2 + b, :], ps[:, 2 * b:2 * b + 2, :], ACT.Copy).then_inc(drained.sem, 1)
    used.base += 16
    drained.base += 4


def attention_stage(core, q, k, v):
    nc, ps = core.nc, core.ps
    s = {n: core.sem(f"att_{n}") for n in ("scores", "max", "exp", "scaled", "turned", "probs", "out", "taken")}
    units = [(h, t) for h in range(MEM_HEADS) for t in range(TT)]
    scale = 1.0 / math.sqrt(D // MEM_HEADS)
    with ExitStack() as own:
        sb = lambda name, shape: own.enter_context(nc.sbuf_tensor(f"att_{name}", shape, F32))
        p, pt = sb("p", [P, 8, T]), sb("pt", [P, TT, MEM_HEADS, T])
        top, total = sb("top", [P, 8]), sb("total", [P, 8])
        with nc.Block() as block:
            @block.tensor
            def _(pe):
                for n, (h, t) in enumerate(units):
                    for d in range(4):
                        mm = pe.matmul(ps[:, n, 0:T], q[:, 4 * h + d, t * P:(t + 1) * P], k[:, 4 * h + d, :],
                                       start=d == 0, stop=d == 3)
                    mm.then_inc(s["scores"], 1)
                for n in range(8):
                    pe.wait_ge(s["scaled"], n + 1)
                    for m in range(TT):
                        mm = pe.transpose(ps[:, n, m * P:(m + 1) * P], p[:, n, m * P:(m + 1) * P], core.cst["ident"])
                    mm.then_inc(s["turned"], 1)
                for n in range(KD):
                    h = n // 4
                    pe.wait_ge(s["probs"], 8)
                    if n >= 8:
                        pe.wait_ge(s["taken"], n - 7)
                    for m in range(TT):
                        mm = pe.matmul(ps[:, n % 8, 0:T], v[:, m, n // 4, (n % 4) * P:(n % 4 + 1) * P], pt[:, m, h, :],
                                       start=m == 0, stop=m == TT - 1)
                    mm.then_inc(s["out"], 1)

            @block.scalar
            def _(act):
                for n in range(8):
                    act.wait_ge(s["max"], n + 1)
                    act.activation(p[:, n, :], ps[:, n, 0:T], ACT.Exp, bias=top[:, n:n + 1], scale=scale,
                                   accum_out=total[:, n:n + 1]).then_inc(s["exp"], 1)
                for n in range(KD):
                    act.wait_ge(s["out"], n + 1)
                    act.activation(core.h[:, n, :], ps[:, n % 8, 0:T], ACT.Copy).then_inc(s["taken"], 1)

            @block.vector
            def _(dve):
                for n in range(8):
                    dve.wait_ge(s["scores"], n + 1)
                    core.dve.step(dve, dve.reduce_max(top[:, n:n + 1], ps[:, n, 0:T], AX_X))
                    dve.tensor_scalar(top[:, n:n + 1], top[:, n:n + 1], -scale, None, ALU.mult).then_inc(s["max"], 1)
                for n in range(8):
                    dve.wait_ge(s["exp"], n + 1)
                    core.dve.step(dve, dve.reciprocal(total[:, n:n + 1], total[:, n:n + 1]))
                    dve.tensor_scalar(p[:, n, :], p[:, n, :], total[:, n:n + 1], None, ALU.mult).then_inc(s["scaled"], 1)
                for n, (h, t) in enumerate(units):
                    dve.wait_ge(s["turned"], n + 1)
                    dve.tensor_copy(pt[:, :, h, t * P:(t + 1) * P],
                                    ps[:, n, 0:T].rearrange("p (m l) -> p m l", m=TT)).then_inc(s["probs"], 1)


def top_experts_stage(core, q, keys, turned):
    nc, ps = core.nc, core.ps
    s = {n: core.sem(f"top_{n}") for n in ("scores", "copied", "shifted", "exp", "ready", "turned", "taken")}
    with ExitStack() as own:
        sb = lambda name, shape, dt=F32: own.enter_context(nc.sbuf_tensor(f"top_{name}", shape, dt))
        sc = sb("sc", [P, TT, 2, PEER_HEADS, KEYS])
        val, idx = sb("val", [P, TT, 2, PEER_HEADS, TOPK]), sb("idx", [P, TT, 2, PEER_HEADS, TOPK], U32)
        idf = sb("idf", [P, TT, 2, PEER_HEADS, TOPK])
        cand = sb("cand", [P, TT, PEER_HEADS, TOPK * TOPK])
        best, pos = sb("best", [P, TT, PEER_HEADS, TOPK]), sb("pos", [P, TT, PEER_HEADS, TOPK], U32)
        half, halff = sb("half", [P, 2, TT, PEER_HEADS, TOPK], U32), sb("halff", [P, 2, TT, PEER_HEADS, TOPK])
        pick = sb("pick", [P, PEER_HEADS, TOPK, TOPK])
        chosen = sb("chosen", [P, TT, 3, PEER_HEADS, TOPK])
        total = sb("total", [P, TT, PEER_HEADS])
        with nc.Block() as block:
            @block.tensor
            def _(pe):
                for t in range(TT):
                    for a in range(2):
                        rows = slice(a * 64, a * 64 + 64)
                        for h in range(PEER_HEADS):
                            mm = pe.matmul(ps[:, 4 * t + 2 * a + h // 4, (h % 4) * P:(h % 4 + 1) * P],
                                           q[rows, h, t * P:(t + 1) * P], keys[rows, h, :], start=True, stop=True)
                        mm.then_inc(s["scores"], 1)
                for t in range(TT):
                    pe.wait_ge(s["ready"], t + 1)
                    for n in range(3):
                        mm = pe.transpose(ps[:, t, n * P:(n + 1) * P],
                                          chosen[:, t, n].rearrange("p h k -> p (h k)"), core.cst["ident"])
                    mm.then_inc(s["turned"], 1)

            @block.scalar
            def _(act):
                for t in range(TT):
                    for a in range(2):
                        act.wait_ge(s["scores"], 2 * t + a + 1)
                        act.activation(sc[:, t, a].rearrange("p (b h) n -> p b (h n)", b=2),
                                       ps[:, 4 * t + 2 * a:4 * t + 2 * a + 2, :], ACT.Copy).then_inc(s["copied"], 1)
                act.wait_ge(s["shifted"], 1)
                act.activation(chosen[:, :, 2], chosen[:, :, 2], ACT.Exp).then_inc(s["exp"], 1)
                for t in range(TT):
                    act.wait_ge(s["turned"], t + 1)
                    act.activation(turned[:, :, t * P:(t + 1) * P], ps[:, t, 0:3 * P].rearrange("p (n l) -> p n l", n=3),
                                   ACT.Copy)

            @block.vector
            def _(dve):
                step = lambda ins: core.dve.step(dve, ins)

                def top16(units, src, values, index):
                    for lo in (0, 8):
                        for u in units:
                            ins = dve.max(values(u)[:, lo:lo + 8], src(u))
                        step(ins)
                        for u in units:
                            ins = dve.max_index(index(u)[:, lo:lo + 8], values(u)[:, lo:lo + 8], src(u))
                        step(ins)
                        if lo == 0:
                            for u in units:
                                ins = dve.match_replace(src(u), values(u)[:, 0:8], src(u), -3.0e38)
                            step(ins)

                dve.wait_ge(s["copied"], 4)
                top16([(t, a, h) for t in range(TT) for a in range(2) for h in range(PEER_HEADS)],
                      lambda u: sc[:, u[0], u[1], u[2], :], lambda u: val[:, u[0], u[1], u[2], :],
                      lambda u: idx[:, u[0], u[1], u[2], :])
                step(dve.tensor_copy(idf[:], idx[:]))
                for t in range(TT):
                    pairs = cand[:, t].rearrange("p h (a b) -> p h a b", b=TOPK)
                    ins = dve.tensor_tensor(pairs, spread(val[:, t, 0], 3, TOPK), spread(val[:, t, 1], 2, TOPK), ALU.add)
                step(ins)
                top16([(t, h) for t in range(TT) for h in range(PEER_HEADS)],
                      lambda u: cand[:, u[0], u[1], :], lambda u: best[:, u[0], u[1], :],
                      lambda u: pos[:, u[0], u[1], :])
                dve.tensor_scalar(half[:, 0], pos[:], 4, None, ALU.logical_shift_right)
                step(dve.tensor_scalar(half[:, 1], pos[:], 15, None, ALU.bitwise_and))
                step(dve.tensor_copy(halff[:], half[:]))
                for t in range(TT):
                    ins = dve.tensor_tensor(chosen[:, t, 2], best[:, t],
                                            best[:, t, :, 0:1].broadcast_to([P, PEER_HEADS, TOPK]), ALU.subtract)
                ins.then_inc(s["shifted"], 1)
                ranks = core.cst["iota"][:, 0:TOPK].unsqueeze(1).unsqueeze(1).broadcast_to([P, PEER_HEADS, TOPK, TOPK])
                for t in range(TT):
                    for a in range(2):
                        step(dve.tensor_tensor(pick[:], ranks, spread(halff[:, a, t], 3, TOPK), ALU.is_equal))
                        step(dve.tensor_tensor(pick[:], pick[:], spread(idf[:, t, a], 2, TOPK), ALU.mult))
                        step(dve.tensor_reduce(chosen[:, t, a], pick[:], AX_X, ALU.add))
                dve.wait_ge(s["exp"], 1)
                for t in range(TT):
                    step(dve.tensor_reduce(total[:, t], chosen[:, t, 2], AX_X, ALU.add))
                step(dve.reciprocal(total[:], total[:]))
                for t in range(TT):
                    dve.tensor_tensor(chosen[:, t, 2], chosen[:, t, 2], spread(total[:, t], 2, TOPK),
                                      ALU.mult).then_inc(s["ready"], 1)


def gates_stage(core, turned, gates):
    nc, ps = core.nc, core.ps
    GROUP = 8
    s = {n: core.sem(f"gates_{n}") for n in ("left", "right", "made", "stored")}
    keys = core.cst["iota"][:, 0:KEYS]
    with ExitStack() as own:
        sb = lambda name, shape: own.enter_context(nc.sbuf_tensor(f"gates_{name}", shape, F32))
        left, right = sb("left", [P, GROUP, KEYS]), sb("right", [P, GROUP, KEYS])
        rounds = T // GROUP
        with nc.Block() as block:
            @block.tensor
            def _(pe):
                with pe.Fori(0, rounds) as i:
                    for b in range(2):
                        pe.wait_ge(s["stored"], i * 2 + (b + 1))
                        for j in range(4):
                            n = 4 * b + j
                            pe.wait_ge(s["right"], i * GROUP + (n + 1))
                            mm = pe.matmul(ps[:, b, j * P:(j + 1) * P], left[:, n, :], right[:, n, :],
                                           start=True, stop=True)
                        mm.then_inc(s["made"], 1)

            @block.scalar
            def _(act):
                act.sem_inc(s["stored"], 2)
                with act.Fori(0, rounds) as i:
                    for b in range(2):
                        act.wait_ge(s["made"], i * 2 + (b + 1))
                        act.activation(gates[:, :, bass.ds(i * GROUP + 4 * b, 4)].rearrange("p j t -> p t j"),
                                       ps[:, b, :].rearrange("p (t j) -> p t j", t=4), ACT.Copy).then_inc(s["stored"], 1)

            @block.vector
            def _(dve):
                with dve.Fori(0, rounds) as i:
                    for n in range(GROUP):
                        if n % 4 == 0:
                            dve.wait_ge(s["stored"], i * 2 + (n // 4 + 1))
                        at = bass.ds(i * GROUP + n, 1)
                        dve.tensor_scalar(left[:, n, :], keys, turned[:, 0, at], None, ALU.is_equal)
                        dve.tensor_scalar(right[:, n, :], keys, turned[:, 1, at], turned[:, 2, at], ALU.is_equal,
                                          ALU.mult).then_inc(s["right"], 1)


def added(core):
    def drain(dve, banks, n, i, s):
        return dve.tensor_tensor(core.x[:, n, :], core.x[:, n, :], banks[0], ALU.add)
    return drain


def copied_to(tile, func=ACT.Copy):
    def drain(act, banks, n, i, s):
        return act.activation(tile[:, n, :], banks[0], func)
    return drain


def second_block(core):
    nc = core.nc

    class S5:
        pass

    rms_stage(core, "norm_mix2", core.x, core.h, KD, core.prm["norm_mix"])
    with ExitStack() as mixers:
        sb = lambda name, shape: mixers.enter_context(nc.sbuf_tensor(name, shape, F32))
        proj, conv = sb("proj", [P, 3 * HT, T]), sb("conv", [P, HT, T])
        for part, (func, next_w) in enumerate(((ACT.Copy, ("w_in_2", HT)), (ACT.Sigmoid, ("w_in_2", 2 * HT)),
                                               (ACT.Copy, ("w_glu", 0)))):
            linear_stage(core, f"in2_{part}", "w_in_2", HT, next_w, [core.h],
                         copied_to(proj[:, part * HT:(part + 1) * HT, :], func), first=part * HT)
        s5 = S5()
        s5.b, s5.c = sb("s5_b", [P, HT, 2, 2, 64]), sb("s5_cc", [P, 3, PAIRS, 32])
        s5.r, s5.turn = sb("s5_r", [P, PAIRS]), sb("s5_turn", [P, PAIRS])
        s5_setup_stage(core, s5)
        local_mixers_stage(core, s5, proj, conv)
        y = proj[:, 2 * HT:, :]
        glu_stage(core, y, ("w_out_2", 0))
        group_norm_stage(core, conv[:], y)
    with ExitStack() as attention:
        sb = lambda name, shape: attention.enter_context(nc.sbuf_tensor(name, shape, F32))
        q, k, v = sb("q", [P, KD, T]), sb("k", [P, KD, T]), sb("v", [P, TT, 4, BANK])
        mem = sb("mem", [P, KD, T])
        linear_stage(core, "mix2_out", "w_out_2", KD, ("w_q", 0), [core.h], added(core), "vector",
                     loads=[(mem[:], "mem")])
        rms_stage(core, "norm_q", core.x, core.h, KD, core.prm["norm_mem"])
        linear_stage(core, "mem_q", "w_q", KD, ("w_k", 0), [core.h], copied_to(q))
        rms_stage(core, "norm_mem", mem, mem, KD, core.prm["mem_norm"])
        linear_stage(core, "mem_k", "w_k", KD, ("w_v", 0), [mem], copied_to(k))
        values_stage(core, mem, v, ("w_o", 0))
        attention_stage(core, q, k, v)
    linear_stage(core, "mem_out", "w_o", KD, ("w_peer_q", 0), [core.h], added(core), "vector")
    rms_stage(core, "norm_ffn", core.x, core.h, KD, core.prm["norm_ffn"])
    with nc.sbuf_tensor("turned", [P, 3, T], F32) as turned:
        with ExitStack() as choice:
            sb = lambda name, shape: choice.enter_context(nc.sbuf_tensor(name, shape, F32))
            q, keys = sb("peer_q", [P, PEER_HEADS, T]), sb("peer_keys", [P, PEER_HEADS, KEYS])
            linear_stage(core, "peer_q", "w_peer_q", PEER_HEADS, ("w_u", 0), [core.h], copied_to(q),
                         loads=[(keys[:], "peer_keys")])
            top_experts_stage(core, q, keys, turned)
        with nc.sbuf_tensor("gates", [P, KEYS, T], F32) as gates:
            gates_stage(core, turned, gates)
            gelu_done = core.sem("experts_gelu")
            base = core.used.base
            with nc.sbuf_tensor("expert_act", [P, RING, T], F32) as expert_act:
                def gelus(block):
                    @block.scalar
                    def _(act):
                        with act.Fori(0, KEYS // RING) as i:
                            for s in range(RING):
                                act.wait_ge(core.used.sem, i * RING + (base + s + 1))
                                act.activation(expert_act[:, s, :], core.ps[:, s, 0:T],
                                               ACT.Gelu_apprx_tanh).then_inc(gelu_done, 1)

                def gate_experts(dve, banks, n, i, s):
                    dve.wait_ge(gelu_done, i * RING + (s + 1))
                    return dve.tensor_tensor(gates[:, n, :], gates[:, n, :], expert_act[:, s, :], ALU.mult)

                linear_stage(core, "expert_up", "w_u", KEYS, ("w_v_tab", 0), [core.h], gate_experts, "vector", gelus)
            linear_stage(core, "expert_down", "w_v_tab", KD, None, [gates], added(core), "vector", kc=8)
    rms_stage(core, "norm_last", core.x, core.x, KD, core.prm["final2"])


def second_layout(a, d):
    d["mem"] = feature_major(a["mem_2"][0])
    d["w_in_2"] = pieces(a["w_in_2"][0])
    glu = a["ssm_glu_w_2"][0].reshape(HT, P, RING, 2, P)
    d["w_glu"] = glu.transpose(2, 1, 3, 0, 4).reshape(RING, P, PIECE)
    d["w_out_2"] = pieces(a["w_out_2"][0])
    d["w_q"] = pieces(a["w_q_mem_2"][0])
    kv = a["w_kv_mem_2"][0]
    d["w_k"] = pieces(kv[:, :D])
    d["w_v"] = kv[:, D:].reshape(4, 4, P, 4, BANK).transpose(3, 0, 2, 1, 4).reshape(16, P, PIECE)
    d["w_o"] = pieces(a["w_o_mem_2"][0])
    d["w_peer_q"] = pieces(a["peer_w_q_2"][0])
    d["peer_keys"] = a["peer_keys_2"][0].transpose(1, 3, 0, 2).reshape(P, PEER_HEADS, KEYS)
    by_second_key = lambda w: w.reshape(KEYS, KEYS, D).transpose(1, 0, 2).reshape(KEYS * KEYS, D)
    d["w_u"] = pieces(by_second_key(a["peer_u_2"][0]).T)
    d["w_v_tab"] = pieces(by_second_key(a["peer_v_2"][0]))
    over = lambda v: np.broadcast_to(v.reshape(HT, 8, 1, 64), (HT, 8, 16, 64))
    rep = [over(a["ssm_lam_re_2"][0]), over(a["ssm_lam_im_2"][0]),
           over(np.repeat(a["ssm_log_dt_2"][0], 64).reshape(-1, 64)),
           a["ssm_b_re_2"][0].reshape(HT, 8, 64, 16).transpose(0, 1, 3, 2),
           a["ssm_b_im_2"][0].reshape(HT, 8, 64, 16).transpose(0, 1, 3, 2)]
    d["s5_rep"] = np.stack([v.transpose(1, 2, 0, 3).reshape(P, HT * 64) for v in rep], axis=1)
    c = np.stack([a["ssm_c_re_2"][0], a["ssm_c_im_2"][0]]).reshape(2, PAIRS, 2, 16, 64)
    d["s5_c"] = c.transpose(0, 2, 4, 1, 3).reshape(2, P, PAIRS, 16)


def two_block_kernel(nc, dram, out):
    with ExitStack() as ctx:
        core = Core(nc, ctx, dram)
        first_block(core)
        stored = core.sem("result_stored")
        second_block(core)
        with nc.Block() as block:
            @block.sync
            def _(sp):
                sp.dma_start(out, core.x[:]).then_inc(stored, 16)
                sp.wait_ge(stored, 16)



def shape_constants():
    consts = np.zeros((P, N_CONST), np.float32)
    r = np.arange(P)
    at = lambda n: slice(CONST_AT[n], CONST_AT[n] + CONST_COLS[n])
    consts[:, at("ident")] = np.eye(P)
    consts[:, at("tri_f")] = r[:, None] <= r[None, :]
    consts[:, at("tri_b")] = r[:, None] >= r[None, :]
    consts[:, at("iota")] = np.arange(T)
    consts[:, at("group")] = (r[:, None] // 16) % 2 == np.arange(2)
    f32 = np.float32
    t = np.linspace(0.0, 1.0, T, dtype=f32)[:, None]
    bands = 16
    w = (f32(2.0 * math.pi) * np.arange(T, dtype=f32)[:, None] / f32(T)).astype(f32)
    f = np.linspace(1e-4, bands - 1, bands, dtype=f32)[None, :]
    feats = np.concatenate([t, np.cos(f * w), -np.sin(f * w)], axis=-1).astype(f32)
    deltas = np.linspace(math.log(1e-2) / 1.5, math.log(1e-2) / 0.3, HY, dtype=f32)
    window = np.exp(-t * np.abs(deltas)).astype(f32)
    n = 2 * T
    tt, ff = np.arange(T)[:, None], np.arange(T)[None, :]
    angle = 2 * np.pi * ((tt * ff) % n) / n
    cos, sin = np.cos(angle), -np.sin(angle)
    nyquist = (-1.0) ** np.arange(T)
    cos_n, sin_n = cos[:, :P].copy(), sin[:, :P].copy()
    cos_n[:, 0] = sin_n[:, 0] = nyquist
    sin0 = sin[:, :P].copy()
    sin0[:, 0] = 0
    mats = np.stack([cos[:, :P], cos[:, P:], cos_n, sin_n, sin0, sin[:, P:]], axis=1)
    dft = mats.reshape(TT, P, 6, P).transpose(1, 0, 2, 3)
    ci, si = cos.T * 2 / n, sin.T * 2 / n
    ci[0] /= 2
    si[0] = nyquist / n
    inverse = np.concatenate([ci, si]).reshape(4, P, T).transpose(1, 0, 2)
    as32 = lambda a: np.ascontiguousarray(a, dtype=np.float32)
    return {"consts": consts, "feats": as32(feats.T), "dft": as32(dft), "inverse": as32(inverse),
            "window": as32(window.reshape(TT, P, HY).transpose(1, 0, 2))}


def columns(v):
    v = np.asarray(v)
    return v.reshape(-1, P).T


def pieces(w):
    K, N = w.shape
    a = w.reshape(K // D, KD, P, N // P, P).transpose(3, 0, 2, 1, 4)
    return a.reshape(N // P * (K // D), P, PIECE)


def feature_major(x):
    return x.reshape(T, KD, P).transpose(2, 1, 0)


def lay_out(i):
    a = {n: np.asarray(v) for n, v in i.items()}
    w_in = a["w_in"][0]
    o0, o1 = HY_TILES * P, (HY_TILES + XBC_TILES) * P
    o2 = o1 + 2 * HEADS
    d = {
        "x": feature_major(a["x"][0]), "ctx": feature_major(a["ctx"][0]),
        "w_ada": pieces(a["w_ada"][0]),
        "w_mix": pieces(np.concatenate([w_in[:, :o1], w_in[:, o2:]], axis=1)),
        "w_dt": w_in[:, o1:o2].reshape(KD, P, 2 * HEADS).transpose(1, 0, 2),
        "w_out": pieces(a["w_out"][0]), "w_mlp1": pieces(a["w_mlp1"][0]), "w_mlp2": pieces(a["w_mlp2"][0]),
        "filt_w1": a["filt_w1"][0], "filt_w2": a["filt_w2"][0], "filt_w3": a["filt_w3"][0],
    }
    rows = lambda v: np.broadcast_to(v.reshape(1, -1), (P, v.size))
    state = lambda v: v.reshape(PAIRS, P).T
    filt = np.stack([np.pad(a[n][0], (0, P - 64)) for n in ("filt_freq", "filt_b1", "filt_b2", "filt_b2")], axis=1)
    cols = {
        "cond": np.stack([a["c"][0], a["c_ctx"]], axis=1).reshape(KD, P, 2).transpose(1, 0, 2).reshape(P, 2 * KD),
        "b_ada": columns(a["b_ada"]), "norm1": columns(a["norm1_w"]),
        "hy_conv_w": columns(a["hy_conv_w"]), "hy_conv_b": columns(a["hy_conv_b"]),
        "hy_bias": columns(a["hy_bias"]), "hy_norm": columns(a["hy_norm_w"]),
        "ssd_conv_w": columns(a["ssd_conv_w"]), "ssd_conv_b": columns(a["ssd_conv_b"]),
        "ssd_d": columns(np.repeat(a["ssd_d"][0], HEAD)), "ssd_norm": columns(a["ssd_norm_w"]),
        "norm2": columns(a["norm2_w"]), "final1": columns(a["final_norm_w"]),
        "norm_mix": columns(a["norm_mix_g_2"]), "conv_b": columns(a["conv_b_2"]),
        "ln_g": columns(a["conv_ln_g_2"]), "ln_b": columns(a["conv_ln_b_2"]),
        "grp_conv": columns(a["grp_norm_conv_g_2"]), "grp_ssm": columns(a["grp_norm_ssm_g_2"]),
        "norm_mem": columns(a["norm_mem_g_2"]), "mem_norm": columns(a["mem_norm_g_2"]),
        "norm_ffn": columns(a["norm_ffn_g_2"]), "final2": columns(a["final_norm_g_2"]),
        "ssm_d": columns(a["ssm_d_2"]), "lam_re": state(a["ssm_lam_re_2"][0]),
        "lam_im": state(a["ssm_lam_im_2"][0]), "log_dt": state(np.repeat(a["ssm_log_dt_2"][0], 64)),
        "dt_bias": rows(a["dt_bias"][0]), "a_log": rows(a["a_log"][0]),
        "conv_w": a["conv_w_2"][0].reshape(CONV31, HT, P).transpose(2, 1, 0).reshape(P, -1),
        "filt": filt,
    }
    d["params"] = np.concatenate([cols[n] for n in PARAM_COLS], axis=1)
    second_layout(a, d)
    d = {n: np.ascontiguousarray(v) for n, v in d.items()}
    d.update(shape_constants())
    return d


def kernel(**inputs):
    from concourse import bacc
    from concourse.bass_utils import run_bass_kernel_spmd

    arrays = lay_out(inputs)
    nc = bacc.Bacc("TRN2", target_bir_lowering=False, num_devices=1, dynamic_dma_scratch_size=1024)
    dram = {n: nc.dram_tensor(f"in_{n}", v.shape, mybir.dt.from_np(v.dtype), kind="ExternalInput").ap()
            for n, v in arrays.items()}
    out = nc.dram_tensor("out", (P, KD, T), F32, kind="ExternalOutput").ap()
    two_block_kernel(nc, dram, out)
    r = run_bass_kernel_spmd(nc, [{f"in_{n}": v for n, v in arrays.items()}], core_ids=[0])
    return r.results[0]["out"].transpose(2, 1, 0).reshape(1, T, D)
```

```python
import math
from contextlib import ExitStack

import numpy as np

import concourse.bass as bass
from concourse import mybir

F32 = mybir.dt.float32
F32R = mybir.dt.float32r
U32 = mybir.dt.uint32
ALU = mybir.AluOpType
ACT = mybir.ActivationFunctionType
AX_X = mybir.AxisListType.X

P = 128
T = 256
TT = T // P
D = 2048
KD = D // P
EPS = 1e-6
RING = 4
HALF = 8
SLOTS = 4
QUARTER = 4
BANK = 512

HY = 1024
HT = HY // P
HY_TILES = 3 * HT
XBC_TILES = 12
Z_TILES = 8
GRID = 64
HEADS = 16
HEAD = 64
MLP_TILES = 64
EPS_COL, ZERO_COL, QUARTER_COL = 0, 1, 2

CONV31 = 31
PAIRS = 32
MEM_HEADS = 4
PEER_HEADS = 8
KEYS = 128
TOPK = 16
TWO_PI = 6.283185

PARAM_COLS = dict(
    cond=2 * KD, b_ada=6 * KD, norm1=KD, hy_conv_w=3 * HY_TILES, hy_conv_b=HY_TILES,
    hy_bias=2 * HT, hy_norm=HT, ssd_conv_w=3 * XBC_TILES, ssd_conv_b=XBC_TILES, ssd_d=HT,
    ssd_norm=HT, norm2=KD, final1=KD, norm_mix=KD, conv_b=HT, ln_g=HT, ln_b=HT, grp_conv=HT,
    grp_ssm=HT, norm_mem=KD, mem_norm=KD, norm_ffn=KD, final2=KD, ssm_d=HT, lam_re=PAIRS,
    lam_im=PAIRS, log_dt=PAIRS, dt_bias=2 * HEADS, a_log=2 * HEADS, conv_w=CONV31 * HT,
    filt=4,
)
PARAM_AT, N_PARAM = {}, 0
for _name, _n in PARAM_COLS.items():
    PARAM_AT[_name] = N_PARAM
    N_PARAM += _n

CONST_COLS = dict(ident=P, tri_f=P, tri_b=P, iota=T, group=2, halves=2)
CONST_AT, N_CONST = {}, 0
for _name, _n in CONST_COLS.items():
    CONST_AT[_name] = N_CONST
    N_CONST += _n


def spread(ap, axis, n):
    v = ap.unsqueeze(axis)
    shape = list(v.shape)
    shape[axis] = n
    return v.broadcast_to(shape)


class Signal:

    def __init__(self, sem):
        self.sem, self.base = sem, 0


class Chain:

    def __init__(self, sem):
        self.sem, self.n, self.per, self.i = sem, 0, 0, None

    def step(self, eng, ins):
        ins.then_inc(self.sem, 1)
        self.n += 1
        eng.wait_ge(self.sem, self.n if self.i is None else self.i * self.per + self.n)

    def loop(self, i, per, start=None):
        self.n = self.n if start is None else start
        self.i, self.per, self.start = i, per, self.n

    def end(self, iterations):
        assert self.n - self.start == self.per, (self.n - self.start, self.per)
        self.n += self.per * (iterations - 1)
        self.i = None


class Core:

    def __init__(self, nc, ctx, dram):
        self.nc, self.dram, self.ctx = nc, dram, ctx
        self.sb = lambda name, shape, dt=F32: ctx.enter_context(nc.sbuf_tensor(name, shape, dt))
        self.ring = self.sb("ring", [P, RING, HALF, P])
        self.hi = self.sb("weights_hi", [P, SLOTS, QUARTER, P], F32R)
        self.lo = self.sb("weights_lo", [P, SLOTS, QUARTER, P], F32R)
        self.params = self.sb("params", [P, N_PARAM])
        self.consts = self.sb("consts", [P, N_CONST])
        self.ones = self.sb("ones", [P, P])
        self.small = self.sb("small", [P, 4])
        self.mod = self.sb("mod", [P, 6 * KD, 2])
        self.gain = self.sb("gain", [P, 3 * KD])
        self.x = self.sb("x", [P, KD, T])
        self.ps = ctx.enter_context(nc.psum_tensor("ps", [P, 8, BANK], F32))
        self.landed = [self.sem(f"weights_landed{s}") for s in range(RING)]
        self.rounded, self.split, self.multiplied = (self.sem(f"weights_{n}") for n in ("rounded", "split", "multiplied"))
        self.moved, self.summed, self.shaped = (self.sem(f"tile_{n}") for n in ("moved", "summed", "shaped"))
        self.quarters, self.tiles, self.moves, self.shapes = 0, 0, 0, 0
        self.norm_signals = [Signal(self.sem(f"norm_{n}")) for n in ("squared", "summed", "rooted", "scaled")]
        self.hyena_signals = {n: self.sem(f"hyena_{n}") for n in ("turned", "token", "spectrum", "product", "result")}
        self.dve = Chain(self.sem("vector_step"))
        self.act = Chain(self.sem("scalar_step"))
        self.pool = Chain(self.sem("gpsimd_step"))
        self.prm = {n: self.params[:, PARAM_AT[n]:PARAM_AT[n] + c] for n, c in PARAM_COLS.items()}
        self.cst = {n: self.consts[:, CONST_AT[n]:CONST_AT[n] + c] for n, c in CONST_COLS.items()}

    def sem(self, name):
        return self.ctx.enter_context(self.nc.semaphore(name))

    def block(self, w, n):
        return self.dram[w][n].rearrange("p (k m) -> p k m", k=HALF)


def stream(core, sp, w, count, next_w, first=0):
    rounds = count // RING
    if rounds > 1:
        with sp.Fori(0, rounds - 1) as i:
            for s in range(RING):
                sp.wait_ge(core.split, i * (2 * RING) + (core.quarters + 2 * s + 2))
                sp.dma_start(core.ring[:, s], core.block(w, i * RING + (first + RING + s))).then_inc(core.landed[s], 16)
    for s in range(RING):
        sp.wait_ge(core.split, core.quarters + 2 * (count - RING + s) + 2)
        if next_w is not None:
            sp.dma_start(core.ring[:, s], core.block(next_w[0], next_w[1] + s)).then_inc(core.landed[s], 16)


def make_hi(core, act, g, i, per):
    slot, at = g // 2 % RING, g % 2 * QUARTER
    if g % 2 == 0:
        act.wait_ge(core.landed[slot], i * (2 * per) + 16 * (core.quarters // 8 + g // 8 + 1))
    act.wait_ge(core.multiplied, i * per + (core.quarters + g + 1))
    act.activation(core.hi[:, g % SLOTS], core.ring[:, slot, at:at + QUARTER], ACT.Copy).then_inc(core.rounded, 1)


def make_lo(core, dve, g, i, per):
    slot, at = g // 2 % RING, g % 2 * QUARTER
    dve.wait_ge(core.rounded, i * per + (core.quarters + g + 1))
    dve.tensor_tensor(core.lo[:, g % SLOTS], core.ring[:, slot, at:at + QUARTER],
                      core.hi[:, g % SLOTS].bitcast(F32), ALU.subtract).then_inc(core.split, 1)


def split_and_take(core, eng, make, take, rounds, unroll, quarters, source=None):
    per, ahead = unroll * quarters, min(SLOTS, quarters)

    def body(i, last):
        for s in range(unroll):
            for g in range(s * quarters + ahead, (s + 1) * quarters + ahead):
                if g < per or not last:
                    make(core, eng, g, i, per)
            take(eng, i * unroll + s, i, s)

    for g in range(ahead):
        if source is not None:
            source(eng, g)
        make(core, eng, g, 0, per)
    if rounds > 1:
        with eng.Fori(0, rounds - 1) as i:
            body(i, False)
    body(rounds - 1, True)


def rms_stage(core, name, src, dst, tiles, gain, bias=None):
    nc, ps = core.nc, core.ps
    squared, summed, rooted, scaled = core.norm_signals
    with ExitStack() as own:
        sq = own.enter_context(nc.sbuf_tensor(f"{name}_sq", [P, tiles, T], F32))
        std = own.enter_context(nc.sbuf_tensor(f"{name}_std", [P, T], F32))
        rstd = own.enter_context(nc.sbuf_tensor(f"{name}_rstd", [P, T], F32))
        group = tiles // 4
        with nc.Block() as block:
            @block.scalar
            def _(act):
                for g in range(4):
                    at = slice(g * group, (g + 1) * group)
                    act.activation(sq[:, at, :], src[:, at, :], ACT.Square).then_inc(squared.sem, 1)
                act.wait_ge(summed.sem, summed.base + 1)
                act.activation(std[:], ps[:, 0, 0:T], ACT.Sqrt, bias=core.small[:, EPS_COL:EPS_COL + 1],
                               scale=1.0 / (tiles * P)).then_inc(rooted.sem, 1)
                if bias is not None:
                    for t in range(tiles):
                        act.wait_ge(scaled.sem, scaled.base + t + 1)
                        act.activation(dst[:, t, :], dst[:, t, :], ACT.Identity, bias=bias[:, t:t + 1])

            @block.tensor
            def _(pe):
                for t in range(tiles):
                    if t % group == 0:
                        pe.wait_ge(squared.sem, squared.base + t // group + 1)
                    mm = pe.matmul(ps[:, 0, 0:T], core.ones[:], sq[:, t, :], start=t == 0, stop=t == tiles - 1)
                mm.then_inc(summed.sem, 1)

            @block.vector
            def _(dve):
                dve.wait_ge(rooted.sem, rooted.base + 1)
                core.dve.step(dve, dve.reciprocal(rstd[:], std[:]))
                for t in range(tiles):
                    dve.scalar_tensor_tensor(dst[:, t, :], src[:, t, :], gain[:, t:t + 1], rstd[:],
                                             ALU.mult, ALU.mult).then_inc(scaled.sem, 1)
    for signal, n in ((squared, 4), (summed, 1), (rooted, 1), (scaled, tiles)):
        signal.base += n


def start_stage(core, ctx_tile, const_loads):
    nc, ps, dram = core.nc, core.ps, core.dram
    loaded, made, split_c, ready = (core.sem(n) for n in ("inputs_loaded", "silu_made", "silu_split", "silu_ready"))
    tables = core.sem("tables_loaded")
    blocks = 6 * D // BANK
    turned = core.sem("mod_turned")
    with ExitStack() as own:
        silu_c = own.enter_context(nc.sbuf_tensor("silu_c", [P, KD, 2], F32))
        zeros = own.enter_context(nc.sbuf_tensor("zeros", [P, KD, P], F32))
        c4 = own.enter_context(nc.sbuf_tensor("silu_parts", [P, KD, P], F32R))
        rows = own.enter_context(nc.sbuf_tensor("mod_rows", [4, 2, BANK], F32))
        block = own.enter_context(nc.Block())
        mod_sums = ps[:, 4, 0:12 * KD].rearrange("p (n c) -> p n c", c=2)
        rounds = blocks // 2

        @block.sync
        def _(sp):
            sp.dma_start(core.params[:], dram["params"]).then_inc(loaded, 16)
            for s in range(RING):
                sp.dma_start(core.ring[:, s], core.block("w_ada", s)).then_inc(core.landed[s], 16)
            stream(core, sp, "w_ada", blocks * HALF, ("w_mix", 0))

        @block.scalar
        def _(act):
            act.wait_ge(loaded, 16)
            act.activation(silu_c[:], core.prm["cond"].rearrange("p (k c) -> p k c", c=2), ACT.Silu).then_inc(made, 1)
            act.wait_ge(split_c, 1)
            act.wait_ge(made, 1)
            act.activation(c4[:, :, 0:2], silu_c[:], ACT.Copy).then_inc(made, 1)
            split_and_take(core, act, make_hi, lambda act, n, i, s: None, rounds, 2, KD)

        @block.gpsimd
        def _(pool):
            pool.dma_start(core.consts[:], dram["consts"]).then_inc(tables, 16)
            pool.dma_start(core.x[:], dram["x"]).then_inc(tables, 16)
            pool.dma_start(ctx_tile[:], dram["ctx"]).then_inc(tables, 16)
            for tile, name in const_loads:
                pool.dma_start(tile, dram[name]).then_inc(tables, 16)
            pool.wait_ge(tables, 16 * (3 + len(const_loads)))

        @block.vector
        def _(dve):
            dve.sem_inc(core.multiplied, SLOTS)
            dve.sem_inc(core.summed, 2)
            dve.memset(core.ones[:], 1.0)
            for col, value in ((EPS_COL, EPS), (ZERO_COL, 0.0), (QUARTER_COL, 0.25)):
                dve.memset(core.small[:, col:col + 1], value)
            core.dve.step(dve, dve.memset(zeros[:], 0.0))
            dve.tensor_copy(c4[:], zeros[:]).then_inc(split_c, 1)
            dve.wait_ge(made, 2)
            dve.tensor_tensor(c4[:, :, 2:4], silu_c[:], c4[:, :, 0:2].bitcast(F32), ALU.subtract).then_inc(ready, 1)

            def take(dve, n, i, s):
                dve.wait_ge(core.multiplied, i * (2 * KD) + (SLOTS + (s + 1) * KD))
                dve.tensor_copy(rows[:, s], ps[0:4, s, :]).then_inc(core.summed, 1)

            split_and_take(core, dve, make_lo, take, rounds, 2, KD)
            dve.wait_ge(turned, blocks)
            core.dve.step(dve, dve.tensor_tensor(core.mod[:], mod_sums, spread(core.prm["b_ada"], 2, 2), ALU.add))
            for n, (norm, part, who) in enumerate((("norm1", 1, 0), ("norm1", 1, 1), ("norm2", 4, 0))):
                dve.scalar_tensor_tensor(core.gain[:, n * KD:(n + 1) * KD], core.mod[:, part * KD:(part + 1) * KD, who],
                                         1.0, core.prm[norm], ALU.add, ALU.mult)

        @block.tensor
        def _(pe):
            def multiply(i, b, ks):
                for k in ks:
                    pe.wait_ge(core.split, i * (2 * KD) + (b * KD + k + 1))
                    for m, w in enumerate((core.hi, core.lo)):
                        mm = pe.matmul(ps[:, b % 2, :], c4[:, k, :], w[:, k % SLOTS].rearrange("p k m -> p (k m)"),
                                       start=(m, k) == (0, 0), stop=(m, k) == (1, KD - 1))
                    mm.then_inc(core.multiplied, 1)

            def turn(i, b):
                pe.wait_ge(core.summed, i * 2 + (b + 3))
                for j in range(BANK // P):
                    mm = pe.matmul(mod_sums[:, i * 8 + (b * 4 + j), :], rows[:, b % 2, j * P:(j + 1) * P],
                                   core.cst["halves"][0:4, :], start=True, stop=True)
                mm.then_inc(turned, 1)

            first, rest = range(KD // 2), range(KD // 2, KD)
            pe.wait_ge(ready, 1)
            multiply(0, 0, range(KD))
            pe.wait_ge(tables, 16 * (3 + len(const_loads)))
            with pe.Fori(0, rounds - 1) as i:
                for b in range(2):
                    multiply(i, b + 1, first)
                    turn(i, b)
                    multiply(i, b + 1, rest)
            multiply(rounds - 1, 1, first)
            turn(rounds - 1, 0)
            multiply(rounds - 1, 1, rest)
            turn(rounds - 1, 1)
    core.quarters += blocks * KD
    core.tiles += blocks


def split_stage(core, src, dst, tiles):
    nc, group = core.nc, 4
    base = core.shapes
    with nc.Block() as block:
        @block.scalar
        def _(act):
            for t in range(0, tiles, group):
                act.activation(dst[:, t:t + group, 0, :], src[:, t:t + group, :], ACT.Copy).then_inc(core.shaped, 1)

        @block.vector
        def _(dve):
            for t in range(0, tiles, group):
                dve.wait_ge(core.shaped, base + t // group + 1)
                dve.tensor_tensor(dst[:, t:t + group, 1, :], src[:, t:t + group, :],
                                  dst[:, t:t + group, 0, :].bitcast(F32), ALU.subtract)
    core.shapes += tiles // group


def linear_stage(core, name, w, tiles, next_w, rhs, into=None, shape=None, finish=None, first=0, quarters=4,
                 sources=None, loads=(), steps=0):
    nc, ps = core.nc, core.ps
    unroll = 2 * SLOTS // quarters
    rounds, per = tiles // unroll, 2 * SLOTS
    loaded = core.sem(f"{name}_loaded") if loads else None
    chained = core.dve.n
    Q, N, M, S = core.quarters, core.tiles, core.moves, core.shapes
    with ExitStack() as own:
        sums = own.enter_context(nc.sbuf_tensor(f"{name}_sums", [P, 2, len(rhs), T], F32)) if into is None else None
        block = own.enter_context(nc.Block())

        def slots(n, s):
            return [into(n)] if into is not None else [sums[:, s % 2, j, :] for j in range(len(rhs))]

        @block.sync
        def _(sp):
            for tile, source in loads:
                sp.dma_start(tile, core.dram[source]).then_inc(loaded, 16)
            stream(core, sp, w, tiles * quarters // 2, next_w, first)
            if loads:
                sp.wait_ge(loaded, 16 * len(loads))

        @block.scalar
        def _(act):
            def source(act, q):
                at = slice(q * QUARTER, (q + 1) * QUARTER)
                for r, src in zip(rhs, sources):
                    act.activation(r[:, at, 0, :], src[:, at, :], ACT.Copy)

            def take(act, n, i, s):
                act.wait_ge(core.multiplied, i * per + (Q + SLOTS + (s + 1) * quarters))
                for j, slot in enumerate(slots(n, s)):
                    ins = act.activation(slot, ps[:, s % 2 + 2 * j, T:2 * T], ACT.Copy)
                ins.then_inc(core.moved, 1)
                if shape is not None:
                    act.wait_ge(core.summed, i * unroll + (N + s + 3))
                    shape(act, n, slots(n, s)).then_inc(core.shaped, 1)
            split_and_take(core, act, make_hi, take, rounds, unroll, quarters, source if sources else None)

        @block.vector
        def _(dve):
            def source(dve, q):
                dve.wait_ge(core.rounded, Q + q + 1)
                at = slice(q * QUARTER, (q + 1) * QUARTER)
                for r, src in zip(rhs, sources):
                    dve.tensor_tensor(r[:, at, 1, :], src[:, at, :], r[:, at, 0, :].bitcast(F32), ALU.subtract)

            def take(dve, n, i, s):
                if s == 0 and steps:
                    core.dve.loop(i, steps * unroll, chained)
                dve.wait_ge(core.moved, i * unroll + (M + s + 1))
                for j, slot in enumerate(slots(n, s)):
                    ins = dve.tensor_tensor(slot, slot, ps[:, s % 2 + 2 * j, 0:T], ALU.add)
                ins.then_inc(core.summed, 1)
                if shape is not None:
                    dve.wait_ge(core.shaped, i * unroll + (S + s + 1))
                elif finish is not None:
                    dve.wait_ge(core.summed, i * unroll + (N + s + 3))
                if finish is not None:
                    finish(dve, n, slots(n, s))
            split_and_take(core, dve, make_lo, take, rounds, unroll, quarters, source if sources else None)
            if steps:
                core.dve.end(rounds)

        @block.tensor
        def _(pe):
            with pe.Fori(0, rounds) as i:
                for s in range(unroll):
                    pe.wait_ge(core.summed, i * unroll + (N + s + 1))
                    for q in range(quarters):
                        g = s * quarters + q
                        pe.wait_ge(core.split, i * per + (Q + g + 1))
                        for k in range(QUARTER):
                            at, last = q * QUARTER + k, (q, k) == (quarters - 1, QUARTER - 1)
                            for part in ((core.lo, core.hi) if last else (core.hi, core.lo)):
                                for j, r in enumerate(rhs):
                                    if part is core.hi:
                                        out, moving = ps[:, s % 2 + 2 * j, :], r[:, at].rearrange("p a t -> p (a t)")
                                    else:
                                        out, moving = ps[:, s % 2 + 2 * j, 0:T], r[:, at, 0, :]
                                    mm = pe.matmul(out, part[:, g % SLOTS, k, :], moving,
                                                   start=at == 0 and part is core.hi, stop=last and part is core.hi)
                        mm.then_inc(core.multiplied, 1)
    core.quarters += tiles * quarters
    core.tiles += tiles
    core.moves += tiles
    if shape is not None:
        core.shapes += tiles


def conv3_stage(core, name, w, tiles, next_w, rhs, first, dests, taps, bias, rows, sources):
    def centre(act, n, slots):
        for dst, u in zip(dests, slots):
            ins = act.activation(dst[:, n, :], u, ACT.Identity, bias=bias[:, bass.ds(n, 1)],
                                 scale=taps[:, bass.ds(n + tiles, 1)])
        return ins

    def neighbours(dve, n, slots):
        for dst, slot, g in zip(dests, slots, rows):
            u = slot.rearrange("p (r t) -> p r t", t=g)
            y = dst[:, n, :].rearrange("p (r t) -> p r t", t=g)
            core.dve.step(dve, dve.scalar_tensor_tensor(
                y[:, :, 1:g], u[:, :, 0:g - 1], taps[:, bass.ds(n, 1)], y[:, :, 1:g], ALU.mult, ALU.add))
            dve.scalar_tensor_tensor(
                y[:, :, 0:g - 1], u[:, :, 1:g], taps[:, bass.ds(n + 2 * tiles, 1)], y[:, :, 0:g - 1],
                ALU.mult, ALU.add)

    linear_stage(core, name, w, tiles, next_w, rhs, shape=centre, finish=neighbours, first=first * 2,
                 sources=sources, steps=len(rhs))


def dt_stage(core, wdt, h_parts, ctx_parts, ssd):
    nc, ps = core.nc, core.ps
    names = ("rounded", "split", "sums", "abs", "exp", "grown", "log", "a", "da", "cum", "to_end")
    s = {n: core.sem(f"dt_{n}") for n in names}
    H2 = 2 * HEADS
    with ExitStack() as own:
        sb = lambda name: own.enter_context(nc.sbuf_tensor(f"dt_{name}", [P, 4, H2], F32))
        v, e, u, lnu, zero, den, rest = (sb(n) for n in ("v", "e", "u", "lnu", "zero", "den", "rest"))
        av = sb("av")
        a_row = own.enter_context(nc.sbuf_tensor("a_row", [P, H2], F32))
        w = own.enter_context(nc.sbuf_tensor("wdt_parts", [P, KD, 2, H2], F32R))
        with nc.Block() as block:
            @block.tensor
            def _(pe):
                pe.wait_ge(s["split"], 1)
                for q in range(4):
                    src = h_parts if q < 2 else ctx_parts
                    at = slice((q % 2) * P, (q % 2 + 1) * P)
                    out = ps[:, 0, 2 * q * H2:2 * (q + 1) * H2]
                    for k in range(KD):
                        if k:
                            pe.matmul(out[:, 0:H2], src[:, k, 1, at], w[:, k, 0, :], start=False, stop=False)
                        mm = pe.matmul(out, src[:, k, 0, at], w[:, k].rearrange("p a h -> p (a h)"), start=k == 0,
                                       stop=k == KD - 1)
                        if k == 0:
                            pe.matmul(out[:, 0:H2], src[:, k, 1, at], w[:, k, 0, :], start=False, stop=False)
                mm.then_inc(s["sums"], 1)
                pe.wait_ge(s["da"], 1)
                for q in range(4):
                    for d, tri in enumerate(("tri_f", "tri_b")):
                        at = slice(d * HEADS, (d + 1) * HEADS)
                        pe.matmul(ps[:, 1, q * H2 + d * HEADS:q * H2 + (d + 1) * HEADS], core.cst[tri],
                                  ssd.da[:, q, at], start=True, stop=True)
                mm = pe.matmul(ps[:, 2, 0:4 * H2], core.ones[:], ssd.da[:], start=True, stop=True)
                mm.then_inc(s["cum"], 1)

            @block.scalar
            def _(act):
                act.activation(w[:, :, 0, :], wdt[:], ACT.Copy).then_inc(s["rounded"], 1)
                act.activation(a_row[:], core.prm["a_log"], ACT.Exp).then_inc(s["a"], 1)
                act.wait_ge(s["abs"], 1)
                act.activation(e[:], av[:], ACT.Exp, scale=-1.0).then_inc(s["exp"], 1)
                act.wait_ge(s["grown"], 1)
                act.activation(lnu[:], u[:], ACT.Ln).then_inc(s["log"], 1)
                act.wait_ge(s["to_end"], 1)
                act.activation(ssd.etot[:], ps[:, 2, 0:4 * H2].rearrange("p (q h) -> p q h", q=4), ACT.Exp)
                act.activation(ssd.to_end[:], ssd.to_end[:], ACT.Exp)

            @block.vector
            def _(dve):
                step = lambda ins: core.dve.step(dve, ins)
                dve.wait_ge(s["rounded"], 1)
                dve.tensor_tensor(w[:, :, 1, :], wdt[:], w[:, :, 0, :].bitcast(F32), ALU.subtract).then_inc(s["split"], 1)
                sums = ps[:, 0, 0:8 * H2].rearrange("p (q a h) -> p q a h", q=4, a=2)
                dve.wait_ge(s["sums"], 1)
                step(dve.tensor_tensor(v[:], sums[:, :, 0, :], spread(core.prm["dt_bias"], 1, 4), ALU.add))
                step(dve.tensor_tensor(v[:], v[:], sums[:, :, 1, :], ALU.add))
                step(dve.tensor_scalar(rest[:], v[:], -1.0, None, ALU.mult))
                dve.tensor_tensor(av[:], v[:], rest[:], ALU.max).then_inc(s["abs"], 1)
                dve.wait_ge(s["exp"], 1)
                dve.tensor_scalar(u[:], e[:], 1.0, None, ALU.add).then_inc(s["grown"], 1)
                dve.wait_ge(s["grown"], 1)
                step(dve.tensor_scalar(den[:], u[:], -1.0, None, ALU.add))
                step(dve.tensor_scalar(zero[:], den[:], 0.0, None, ALU.is_equal))
                step(dve.tensor_tensor(den[:], den[:], zero[:], ALU.add))
                step(dve.reciprocal(den[:], den[:]))
                dve.wait_ge(s["log"], 1)
                step(dve.tensor_tensor(den[:], den[:], lnu[:], ALU.mult))
                step(dve.tensor_tensor(den[:], den[:], zero[:], ALU.add))
                step(dve.tensor_tensor(den[:], den[:], e[:], ALU.mult))
                step(dve.scalar_tensor_tensor(ssd.dt[:], v[:], 0.0, den[:], ALU.max, ALU.add))
                dve.wait_ge(s["a"], 1)
                dve.scalar_tensor_tensor(ssd.da[:], ssd.dt[:], -1.0, spread(a_row[:], 1, 4),
                                         ALU.mult, ALU.mult).then_inc(s["da"], 1)
                dve.wait_ge(s["cum"], 1)
                step(dve.tensor_copy(ssd.cum[:], ps[:, 1, 0:4 * H2].rearrange("p (q h) -> p q h", q=4)))
                dve.tensor_tensor(ssd.to_end[:], ps[:, 2, 0:4 * H2].rearrange("p (q h) -> p q h", q=4),
                                  ssd.cum[:], ALU.subtract).then_inc(s["to_end"], 1)


def sine_steps(core, dve, x, k, bound_done):
    magic = 12582912.0
    c1, c2 = 6.28125, 2 * math.pi - 6.28125
    step = lambda ins: core.dve.step(dve, ins)
    step(dve.tensor_scalar(k, x, 1 / (2 * math.pi), magic, ALU.mult, ALU.add))
    step(dve.tensor_scalar(k, k, -magic, None, ALU.add))
    step(dve.scalar_tensor_tensor(x, k, -c1, x, ALU.mult, ALU.add))
    step(dve.scalar_tensor_tensor(x, k, -c2, x, ALU.mult, ALU.add))
    dve.tensor_scalar(x, x, 3.1415925, -3.1415925, ALU.min, ALU.max).then_inc(bound_done, 1)


COS0, COS1, COS_N, SIN_N, SIN0, SIN1 = range(6)
KA0, KA1, KN0, KN1, KB0, KB1 = range(6)


def filter_stage(core, dft, filters):
    nc, ps, dram = core.nc, core.ps, core.dram
    names = ("in", "fw3", "arg", "bounded", "sine", "taps", "tapped", "abs", "abs_sum", "norm", "even_odd",
             "spectrum", "stored")
    s = {n: core.sem(f"filt_{n}") for n in names}
    with ExitStack() as own:
        sb = lambda name, shape: own.enter_context(nc.sbuf_tensor(f"filt_{name}", shape, F32))
        fw1, fw2, hdn = sb("w1", [33, 64]), sb("w2", [64, 64]), sb("hdn", [64, T])
        fw3, window = sb("w3", [64, 2, HY]), sb("window", [P, TT, HY])
        tmp, norm = sb("tmp", [P, 4, BANK]), sb("norm", [P, HY])
        h = sb("taps", [P, TT, 2, HY])
        x, k, feats = tmp[0:64, 0, 0:T], tmp[0:64, 0, T:2 * T], tmp[0:33, 1, 0:T]
        freq, b1, b2 = (core.prm["filt"][0:64, n:n + 1] for n in range(3))
        with nc.Block() as block:
            @block.sync
            def _(sp):
                sp.dma_start(feats, dram["feats"]).then_inc(s["in"], 16)
                sp.dma_start(fw1[:], dram["filt_w1"]).then_inc(s["in"], 16)
                sp.dma_start(fw2[:], dram["filt_w2"]).then_inc(s["in"], 16)
                sp.dma_start(window[:], dram["window"]).then_inc(s["in"], 16)
                w3 = dram["filt_w3"].rearrange("k (o a c) -> k o a c", o=2, a=2)
                sp.dma_start(fw3[:], w3[:, 0]).then_inc(s["fw3"], 16)
                sp.wait_ge(s["taps"], 1)
                sp.dma_start(fw3[:], w3[:, 1]).then_inc(s["fw3"], 16)

            @block.tensor
            def _(pe):
                pe.wait_ge(s["in"], 64)
                pe.matmul(ps[0:64, 0, 0:T], fw1[:], feats, start=True, stop=True).then_inc(s["arg"], 1)
                pe.wait_ge(s["sine"], 1)
                pe.matmul(ps[0:64, 0, 0:T], fw2[:], hdn[:], start=True, stop=True).then_inc(s["arg"], 1)
                pe.wait_ge(s["sine"], 2)
                for o in range(2):
                    pe.wait_ge(s["fw3"], 16 * (o + 1))
                    if o:
                        pe.wait_ge(s["stored"], 10)
                    for b in range(8):
                        t, a, c = b // 4, b // 2 % 2, b % 2
                        mm = pe.matmul(ps[:, b, :], hdn[:, t * P:(t + 1) * P], fw3[:, a, c * BANK:(c + 1) * BANK],
                                       start=True, stop=True)
                    mm.then_inc(s["taps"], 1)
                    pe.wait_ge(s["tapped"], o + 1)
                    for c in range(2):
                        pe.wait_ge(s["abs"], 2 * o + c + 1)
                        for j in range(4):
                            mm = pe.matmul(ps[:, c, :], core.ones[:], tmp[:, j, :], start=j == 0, stop=j == 3)
                        mm.then_inc(s["abs_sum"], 1)
                    pe.wait_ge(s["even_odd"], o + 1)
                    for n, (mat, side) in enumerate(((COS0, 0), (COS1, 0), (COS_N, 0), (SIN0, 1), (SIN1, 1))):
                        for c in range(2):
                            m = 2 * n + c
                            if m >= 4:
                                pe.wait_ge(s["stored"], 10 * o + m - 3)
                            for t in range(TT):
                                mm = pe.matmul(ps[:, 4 + m % 4, :], dft[:, t, mat, :],
                                               h[:, t, side, c * BANK:(c + 1) * BANK], start=t == 0, stop=t == TT - 1)
                            mm.then_inc(s["spectrum"], 1)

            @block.scalar
            def _(act):
                for n in range(2):
                    act.wait_ge(s["bounded"], n + 1)
                    act.activation(hdn[:], x, ACT.Sin).then_inc(s["sine"], 1)
                for o in range(2):
                    act.wait_ge(s["tapped"], o + 1)
                    for c in range(2):
                        if o or c:
                            act.wait_ge(s["abs_sum"], 2 * o + c)
                        if o and not c:
                            act.wait_ge(s["even_odd"], o)
                        act.activation(tmp[:], h[:, :, :, c * BANK:(c + 1) * BANK].rearrange("p a b c -> p (a b) c"),
                                       ACT.Abs).then_inc(s["abs"], 1)
                    act.wait_ge(s["stored"], 10 * o + 4)
                    act.activation(filters[:, o, KN1, :], filters[:, o, KA1, :], ACT.Copy)

            @block.vector
            def _(dve):
                step = lambda ins: core.dve.step(dve, ins)
                for n, bias in enumerate((b1, b2)):
                    dve.wait_ge(s["arg"], n + 1)
                    if n:
                        dve.wait_ge(s["sine"], n)
                    step(dve.tensor_scalar(x, ps[0:64, 0, 0:T], bias, freq, ALU.add, ALU.mult))
                    sine_steps(core, dve, x, k, s["bounded"])
                for o in range(2):
                    dve.wait_ge(s["taps"], o + 1)
                    if o:
                        dve.wait_ge(s["spectrum"], 10)
                    for b in range(8):
                        t, a, c = b // 4, b // 2 % 2, b % 2
                        at = slice(c * BANK, (c + 1) * BANK)
                        ins = dve.tensor_tensor(h[:, t, a, at], ps[:, b, :], window[:, t, at], ALU.mult)
                    step(ins)
                    dve.memset(h[0:1, 0, 1, :], 0.0).then_inc(s["tapped"], 1)
                    for c in range(2):
                        at = slice(c * BANK, (c + 1) * BANK)
                        dve.wait_ge(s["abs_sum"], 2 * o + c + 1)
                        step(dve.tensor_scalar(norm[:, at], ps[:, c, :], EPS, None, ALU.add))
                        step(dve.reciprocal(norm[:, at], norm[:, at]))
                    sums = tmp[:].rearrange("p j c -> p (j c)").rearrange("p (t c) -> p t c", t=TT)
                    dve.wait_ge(s["tapped"], o + 1)
                    step(dve.tensor_tensor(sums, h[:, :, 0, :], h[:, :, 1, :], ALU.add))
                    step(dve.tensor_tensor(h[:, :, 1, :], h[:, :, 0, :], h[:, :, 1, :], ALU.subtract))
                    dve.tensor_copy(h[:, :, 0, :], sums).then_inc(s["even_odd"], 1)
                    for n, part in enumerate((KA0, KA1, KN0, KB0, KB1)):
                        for c in range(2):
                            m = 2 * n + c
                            at = slice(c * BANK, (c + 1) * BANK)
                            dve.wait_ge(s["spectrum"], 10 * o + m + 1)
                            dve.tensor_tensor(filters[:, o, part, at], ps[:, 4 + m % 4, :], norm[:, at],
                                              ALU.mult).then_inc(s["stored"], 1)


def hyena_stage(core, o, u, dft, inverse, filters):
    nc, ps = core.nc, core.ps
    per = {"turned": 4, "token": 4, "spectrum": 2, "product": 12, "result": 2}
    s = core.hyena_signals
    after = {n: o * c for n, c in per.items()}
    with ExitStack() as own:
        sb = lambda name, shape: own.enter_context(nc.sbuf_tensor(f"hy{o}_{name}", shape, F32))
        z, y = sb("z", [P, TT, HY]), sb("y", [P, 4, BANK])
        t1, t2 = sb("t1", [P, 2, BANK]), sb("t2", [P, 2, BANK])
        with nc.Block() as block:
            @block.tensor
            def _(pe):
                for b in range(4):
                    t, c = b // 2, b % 2
                    for j in range(4):
                        mm = pe.transpose(ps[:, b, j * P:(j + 1) * P], u[:, 4 * c + j, t * P:(t + 1) * P],
                                          core.cst["ident"])
                    mm.then_inc(s["turned"], 1)
                pe.wait_ge(s["token"], after["token"] + 4)
                for c in range(2):
                    if c:
                        pe.wait_ge(s["product"], after["product"] + 6)
                    for b, mat in enumerate((COS0, COS1, SIN_N, SIN1)):
                        for t in range(TT):
                            mm = pe.matmul(ps[:, 4 + b, :], dft[:, t, mat, :], z[:, t, c * BANK:(c + 1) * BANK],
                                           start=t == 0, stop=t == TT - 1)
                    mm.then_inc(s["spectrum"], 1)
                    pe.wait_ge(s["product"], after["product"] + 6 * c + 6)
                    for j in range(4):
                        for f in range(4):
                            mm = pe.matmul(ps[:, 2 * c + j // 2, (j % 2) * T:(j % 2 + 1) * T],
                                           y[:, f, j * P:(j + 1) * P], inverse[:, f, :], start=f == 0, stop=f == 3)
                    mm.then_inc(s["result"], 1)

            @block.scalar
            def _(act):
                for b in range(4):
                    t, c = b // 2, b % 2
                    act.wait_ge(s["turned"], after["turned"] + b + 1)
                    act.activation(z[:, t, c * BANK:(c + 1) * BANK], ps[:, b, :], ACT.Copy).then_inc(s["token"], 1)

            @block.vector
            def _(dve):
                step = lambda ins: core.dve.step(dve, ins)
                za, zb = ps[:, 4:6, :], ps[:, 6:8, :]

                def gate(c):
                    dve.wait_ge(s["result"], after["result"] + c + 1)
                    for j in range(4):
                        n = 4 * c + j
                        bank = ps[:, 2 * c + j // 2, (j % 2) * T:(j % 2 + 1) * T]
                        step(dve.scalar_tensor_tensor(u[:, n, :], u[:, n, :],
                                                      core.prm["hy_bias"][:, o * HT + n:o * HT + n + 1], bank,
                                                      ALU.mult, ALU.add))
                    at = slice(4 * c, 4 * c + 4)
                    gates = slice((o + 1) * HT + 4 * c, (o + 1) * HT + 4 * c + 4)
                    step(dve.tensor_tensor(u[:, at, :], u[:, at, :], u[:, gates, :], ALU.mult))

                for c in range(2):
                    at = slice(c * BANK, (c + 1) * BANK)
                    dve.wait_ge(s["spectrum"], after["spectrum"] + c + 1)
                    if c:
                        dve.wait_ge(s["result"], after["result"] + 1)
                    k = lambda n: filters[:, o, n:n + 2, at]
                    dve.tensor_tensor(t1[:], za, k(KA0), ALU.mult).then_inc(s["product"], 1)
                    dve.tensor_tensor(t2[:], zb, k(KB0), ALU.mult).then_inc(s["product"], 1)
                    dve.wait_ge(s["product"], after["product"] + 6 * c + 2)
                    dve.tensor_tensor(y[:, 0:2, :], t1[:], t2[:], ALU.subtract).then_inc(s["product"], 1)
                    dve.wait_ge(s["product"], after["product"] + 6 * c + 3)
                    dve.tensor_tensor(t1[:], za, k(KB0), ALU.mult).then_inc(s["product"], 1)
                    dve.tensor_tensor(t2[:], zb, k(KN0), ALU.mult).then_inc(s["product"], 1)
                    dve.wait_ge(s["product"], after["product"] + 6 * c + 5)
                    dve.tensor_tensor(y[:, 2:4, :], t1[:], t2[:], ALU.add).then_inc(s["product"], 1)
                gate(0)
                gate(1)


def ssd_state_stage(core, ssd, xbc, xbc_ctx):
    nc, ps = core.nc, core.ps
    F, B = 0, 1
    s = {n: core.sem(f"state_{n}") for n in ("turned", "token", "xdt", "weighted", "sum", "taken")}
    NX = HEADS * HEAD
    jobs = [(2, F), (3, F), (3, B), (2, B), (0, F), (1, B)]
    extra = [(0, B), (1, F)]
    with ExitStack() as own:
        sb = lambda name, shape: own.enter_context(nc.sbuf_tensor(f"st_{name}", shape, F32))
        tok = sb("tok", [P, 4, NX + 2 * P])
        ctx_xdt, xw = sb("ctx_xdt", [P, HEADS, HEAD]), sb("xw", [P, 2, HEADS, HEAD])
        with nc.Block() as block:
            tiles = [(0, 4), (4, 4), (8, 2)]

            @block.tensor
            def _(pe):
                n = 0
                for q in (2, 3, 0, 1):
                    src = xbc if q < 2 else xbc_ctx
                    at = slice((q % 2) * P, (q % 2 + 1) * P)
                    for first, count in tiles:
                        if n >= 4:
                            pe.wait_ge(s["token"], n - 3)
                        for j in range(count):
                            mm = pe.transpose(ps[:, n % 4, j * P:(j + 1) * P], src[:, first + j, at], core.cst["ident"])
                        mm.then_inc(s["turned"], 1)
                        n += 1
                for j, (q, d) in enumerate(jobs):
                    pe.wait_ge(s["weighted"], j + 1)
                    if j >= 2:
                        pe.wait_ge(s["taken"], j - 1)
                    if j == 0:
                        pe.wait_ge(s["token"], 12)
                    for g in range(2):
                        mm = pe.matmul(ps[:, 4 + 2 * (j % 2) + g, :], tok[:, q, NX + g * P:NX + (g + 1) * P],
                                       xw[:, j % 2, 8 * g:8 * g + 8, :].rearrange("p h e -> p (h e)"),
                                       start=True, stop=True)
                    mm.then_inc(s["sum"], 1)

            @block.scalar
            def _(act):
                n = 0
                for q in (2, 3, 0, 1):
                    for first, count in tiles:
                        act.wait_ge(s["turned"], n + 1)
                        act.activation(tok[:, q, first * P:(first + count) * P], ps[:, n % 4, 0:count * P],
                                       ACT.Copy).then_inc(s["token"], 1)
                        n += 1

            @block.vector
            def _(dve):
                step = lambda ins: core.dve.step(dve, ins)
                ready = {2: 3, 3: 6, 0: 9, 1: 12}
                heads = lambda d: slice(d * HEADS, (d + 1) * HEADS)

                def take(j):
                    q, d = jobs[j]
                    dve.wait_ge(s["sum"], j + 1)
                    sums = ps[:, 4 + 2 * (j % 2):6 + 2 * (j % 2), :].rearrange("p g (h e) -> p (g h) e", e=HEAD)
                    etot = lambda q, d: spread(ssd.etot[:, q, heads(d)], 2, HEAD)
                    first = {F: 0, B: 1}[d]
                    dst = ssd.state[:, d, first if q >= 2 else 1 - first]
                    if j in (0, 2):
                        ins = dve.tensor_tensor(dst, sums, etot(5 - q, d), ALU.mult)
                    elif j in (1, 3):
                        ins = dve.tensor_tensor(dst, dst, sums, ALU.add)
                    else:
                        step(dve.tensor_tensor(dst, ssd.state[:, d, first], etot(q, d), ALU.mult))
                        ins = dve.tensor_tensor(dst, dst, sums, ALU.add)
                    ins.then_inc(s["taken"], 1)
                    dve.wait_ge(s["taken"], j + 1)

                for j, (q, d) in enumerate(jobs + extra):
                    dve.wait_ge(s["token"], ready[q])
                    x = tok[:, q, 0:NX].rearrange("p (h e) -> p h e", e=HEAD)
                    xdt = ctx_xdt[:] if q >= 2 else ssd.xdt[:, q, d]
                    step(dve.tensor_tensor(xdt, x, spread(ssd.dt[:, q, heads(d)], 2, HEAD), ALU.mult))
                    if j < len(jobs):
                        if j >= 2:
                            take(j - 2)
                        dve.tensor_tensor(xw[:, j % 2], xdt, spread(ssd.to_end[:, q, heads(d)], 2, HEAD),
                                          ALU.mult).then_inc(s["weighted"], 1)
                        dve.wait_ge(s["weighted"], j + 1)
                take(4)
                take(5)


def ssd_scan_stage(core, ssd, xbc, gate):
    nc, ps = core.nc, core.ps
    s = {n: core.sem(f"scan_{n}") for n in ("cb", "cum", "diff", "grown", "decay", "kernel", "turned_c", "y", "cbm")}
    units = [(c, h4) for c in range(TT) for h4 in range(4)]
    with ExitStack() as own:
        sb = lambda name, shape: own.enter_context(nc.sbuf_tensor(f"scan_{name}", shape, F32))
        cbm = sb("cbm", [P, TT, 2, 2, P])
        grown, decay = sb("grown", [P, 2, 2, 4, P]), sb("decay", [P, 2, 2, 4, P])
        with nc.Block() as block:
            @block.tensor
            def _(pe):
                for c in range(TT):
                    at = slice(c * P, (c + 1) * P)
                    for g in range(2):
                        mm = pe.matmul(ps[:, 2, (2 * c + g) * P:(2 * c + g + 1) * P], xbc[:, 8 + g, at],
                                       xbc[:, 10 + g, at], start=True, stop=True)
                mm.then_inc(s["cb"], 1)

                def sums(u):
                    c, h4 = units[u]
                    if u == 1:
                        pe.wait_ge(s["cbm"], 8)
                    if u >= 2:
                        pe.wait_ge(s["grown"], 2 * u - 2)
                    for d, tri in enumerate(("tri_f", "tri_b")):
                        for h in range(4):
                            hd = d * HEADS + 4 * h4 + h
                            mm = pe.matmul(ps[:, 2 * (u % 2) + d, h * P:(h + 1) * P],
                                           ssd.da[:, c, hd:hd + 1].broadcast_to([P, P]), core.cst[tri],
                                           start=True, stop=True)
                        mm.then_inc(s["cum"], 1)

                sums(0)
                for u, (c, h4) in enumerate(units):
                    if u + 1 < len(units):
                        sums(u + 1)
                    pe.wait_ge(s["kernel"], 2 * u + 2)
                    pe.wait_ge(s["turned_c"], 2 * u + 2)
                    for h in range(4):
                        head = 4 * h4 + h
                        ft, row = head // 2, (head % 2) * HEAD
                        out = ps[row:row + HEAD, 4 + ft // 2, (ft % 2) * T + c * P:(ft % 2) * T + (c + 1) * P]
                        for d in range(2):
                            pe.matmul(out, ssd.xdt[:, c, d, head, :], decay[:, u % 2, d, h, :],
                                      start=d == 0, stop=False)
                            mm = pe.matmul(out, ssd.state[:, d, c, head, :], grown[:, u % 2, d, h, :],
                                           start=False, stop=d == 1)
                    mm.then_inc(s["y"], 1)

            @block.scalar
            def _(act):
                for u in range(len(units)):
                    if u >= 2:
                        act.wait_ge(s["y"], u - 1)
                    for d in range(2):
                        act.wait_ge(s["diff"], 2 * u + d + 1)
                        act.activation(grown[:, u % 2, d].rearrange("p h l -> p (h l)"),
                                       ps[:, 2 * (u % 2) + d, :],
                                       ACT.Exp).then_inc(s["grown"], 1)
                    for d in range(2):
                        act.activation(decay[:, u % 2, d], decay[:, u % 2, d], ACT.Exp).then_inc(s["decay"], 1)

            @block.vector
            def _(dve):
                dve.wait_ge(s["cb"], 1)
                for c in range(TT):
                    for g in range(2):
                        for d, tri in enumerate(("tri_f", "tri_b")):
                            dve.tensor_tensor(cbm[:, c, g, d, :], ps[:, 2, (2 * c + g) * P:(2 * c + g + 1) * P],
                                              core.cst[tri], ALU.mult).then_inc(s["cbm"], 1)
                dve.wait_ge(s["cbm"], 8)

                def diffs(u):
                    c, h4 = units[u]
                    if u >= 2:
                        dve.wait_ge(s["y"], u - 1)
                    for d in range(2):
                        dve.wait_ge(s["cum"], 2 * u + d + 1)
                        for h in range(4):
                            hd = d * HEADS + 4 * h4 + h
                            ins = dve.tensor_scalar(decay[:, u % 2, d, h, :], ps[:, 2 * (u % 2) + d, h * P:(h + 1) * P],
                                                    ssd.cum[:, c, hd:hd + 1], 0.0, ALU.subtract, ALU.min)
                        ins.then_inc(s["diff"], 1)

                diffs(0)
                for u, (c, h4) in enumerate(units):
                    if u + 1 < len(units):
                        diffs(u + 1)
                    g = h4 // 2
                    for d in range(2):
                        slot = grown[:, u % 2, d]
                        dve.wait_ge(s["grown"], 2 * u + d + 1)
                        dve.tensor_tensor(slot, slot, spread(xbc[:, 10 + g, c * P:(c + 1) * P], 1, 4),
                                          ALU.mult).then_inc(s["turned_c"], 1)
                    for d in range(2):
                        slot = decay[:, u % 2, d]
                        dve.wait_ge(s["decay"], 2 * u + d + 1)
                        dve.tensor_tensor(slot, slot, spread(cbm[:, c, g, d, :], 1, 4), ALU.mult).then_inc(s["kernel"], 1)
                dve.wait_ge(s["y"], len(units))
                for ft in range(HT):
                    ins = dve.scalar_tensor_tensor(xbc[:, ft, :], xbc[:, ft, :], core.prm["ssd_d"][:, ft:ft + 1],
                                                   ps[:, 4 + ft // 2, (ft % 2) * T:(ft % 2 + 1) * T],
                                                   ALU.mult, ALU.add)
                core.dve.step(dve, ins)
                dve.tensor_tensor(xbc[:, 0:HT, :], xbc[:, 0:HT, :], gate[:], ALU.mult)


def mixer_norm_stage(core, z, y, h):
    nc, ps = core.nc, core.ps
    s = {n: core.sem(f"mixnorm_{n}") for n in ("squared", "summed", "rooted")}
    with ExitStack() as own:
        sb = lambda name, shape: own.enter_context(nc.sbuf_tensor(f"mn_{name}", shape, F32))
        sq, std = sb("sq", [P, 2 * HT, T]), sb("std", [P, HT + 2, T])
        with nc.Block() as block:
            @block.scalar
            def _(act):
                act.activation(sq[:, 0:HT, :], z[:, 0:HT, :], ACT.Square).then_inc(s["squared"], 1)
                act.activation(sq[:, HT:, :], y[:, 0:HT, :], ACT.Square).then_inc(s["squared"], 1)
                act.wait_ge(s["summed"], 1)
                eps = core.small[:, EPS_COL:EPS_COL + 1]
                act.activation(std[:, 0:HT, :].rearrange("p (b j) t -> p b (j t)", j=2), ps[:, 0:4, :], ACT.Sqrt,
                               bias=eps, scale=1.0 / P).then_inc(s["rooted"], 1)
                act.wait_ge(s["summed"], 2)
                act.activation(std[:, HT:, :], ps[:, 4:6, 0:T], ACT.Sqrt, bias=eps,
                               scale=2.0 / HY).then_inc(s["rooted"], 1)

            @block.tensor
            def _(pe):
                pe.wait_ge(s["squared"], 1)
                for b in range(4):
                    mm = pe.matmul(ps[:, b, :], core.ones[:], sq[:, 2 * b:2 * b + 2, :].rearrange("p j t -> p (j t)"),
                                   start=True, stop=True)
                mm.then_inc(s["summed"], 1)
                pe.wait_ge(s["squared"], 2)
                for g in range(2):
                    for j in range(4):
                        mm = pe.matmul(ps[:, 4 + g, 0:T], core.ones[:], sq[:, HT + 4 * g + j, :],
                                       start=j == 0, stop=j == 3)
                mm.then_inc(s["summed"], 1)

            @block.vector
            def _(dve):
                for half, (at, src, gain) in enumerate(((slice(0, HT), z, "hy_norm"), (slice(HT, HT + 2), y, "ssd_norm"))):
                    dve.wait_ge(s["rooted"], half + 1)
                    core.dve.step(dve, dve.reciprocal(std[:, at, :], std[:, at, :]))
                    for t in range(HT):
                        r = std[:, t, :] if half == 0 else std[:, HT + t // 4, :]
                        dve.scalar_tensor_tensor(h[:, half * HT + t, :], src[:, t, :],
                                                 core.prm[gain][:, t:t + 1], r, ALU.mult, ALU.mult)


def gated(core, part):
    def finish(dve, n, slots):
        at = bass.ds(n + part * KD, 1)
        dve.scalar_tensor_tensor(core.x[:, n, :], slots[0], core.mod[:, at, 0], core.x[:, n, :], ALU.mult, ALU.add)
    return finish


def first_block(core):
    nc = core.nc


    class Ssd:
        pass

    with ExitStack() as mixer:
        sb = lambda name, shape, dt=F32: mixer.enter_context(nc.sbuf_tensor(name, shape, dt))
        u, xbc, zg = sb("u", [P, HY_TILES, T]), sb("xbc", [P, XBC_TILES, T]), sb("zg", [P, Z_TILES, T])
        xbc_ctx = sb("xbc_ctx", [P, XBC_TILES, T])
        ssd = Ssd()
        ssd.dt, ssd.da, ssd.cum, ssd.to_end, ssd.etot = (sb(f"ssd_{n}", [P, 4, 2 * HEADS])
                                                         for n in ("dt", "da", "cum", "to_end", "etot"))
        with ExitStack() as projections:
            sb2 = lambda name, shape, dt=F32: projections.enter_context(nc.sbuf_tensor(name, shape, dt))
            wdt = sb2("wdt", [P, KD, 2 * HEADS])
            h_parts, ctx_parts = (sb2(n, [P, KD, 2, T], F32R) for n in ("h_parts", "ctx_parts"))
            with nc.sbuf_tensor("context", [P, KD, T], F32) as ctx_tile:
                start_stage(core, ctx_tile, [(wdt[:], "w_dt")])
                shift = core.mod[:, 0:KD, :]
                rms_stage(core, "norm_ctx", ctx_tile, ctx_tile, KD, core.gain[:, KD:2 * KD], shift[:, :, 1])
                split_stage(core, ctx_tile, ctx_parts, KD)
            with nc.sbuf_tensor("h_mix", [P, KD, T], F32) as h:
                rms_stage(core, "norm_x", core.x, h, KD, core.gain[:, 0:KD], shift[:, :, 0])
                conv3_stage(core, "hy_in", "w_mix", HY_TILES, ("w_mix", 2 * HY_TILES), [h_parts], 0, [u],
                            core.prm["hy_conv_w"], core.prm["hy_conv_b"], [GRID], [h])
            conv3_stage(core, "xbc_in", "w_mix", XBC_TILES, ("w_mix", 2 * (HY_TILES + XBC_TILES)),
                        [h_parts, ctx_parts], HY_TILES, [xbc, xbc_ctx],
                        core.prm["ssd_conv_w"], core.prm["ssd_conv_b"], [GRID, T], None)

            def silu_z(act, n, slots):
                return act.activation(zg[:, n, :], slots[0], ACT.Silu)

            linear_stage(core, "z_in", "w_mix", Z_TILES, ("w_out", 0), [h_parts], shape=silu_z,
                         first=2 * (HY_TILES + XBC_TILES))
            with nc.Block() as block:
                @block.scalar
                def _(act):
                    act.activation(xbc[:], xbc[:], ACT.Silu)
                    act.activation(xbc_ctx[:], xbc_ctx[:], ACT.Silu)
            dt_stage(core, wdt, h_parts, ctx_parts, ssd)
        with ExitStack() as hyena:
            sb2 = lambda name, shape: hyena.enter_context(nc.sbuf_tensor(name, shape, F32))
            dft, inverse = sb2("dft", [P, TT, 6, P]), sb2("inverse", [P, 4, T])
            filters = sb2("filters", [P, 2, 6, HY])
            dft_loaded = core.sem("dft_loaded")
            with nc.Block() as block:
                @block.sync
                def _(sp):
                    sp.dma_start(dft[:], core.dram["dft"]).then_inc(dft_loaded, 16)
                    sp.dma_start(inverse[:], core.dram["inverse"]).then_inc(dft_loaded, 16)
                    sp.wait_ge(dft_loaded, 32)
            filter_stage(core, dft, filters)
            for o in range(2):
                hyena_stage(core, o, u, dft, inverse, filters)
        with ExitStack() as scan:
            sb2 = lambda name, shape: scan.enter_context(nc.sbuf_tensor(name, shape, F32))
            ssd.state = sb2("ssd_state", [P, 2, TT, HEADS, HEAD])
            ssd.xdt = sb2("ssd_xdt", [P, TT, 2, HEADS, HEAD])
            ssd_state_stage(core, ssd, xbc, xbc_ctx)
            ssd_scan_stage(core, ssd, xbc, zg)
        parts = sb("mix_parts", [P, KD, 2, T], F32R)
        h = sb("h_mixed", [P, KD, T])
        mixer_norm_stage(core, u, xbc, h)
        linear_stage(core, "mix_out", "w_out", KD, ("w_mlp1", 0), [parts], finish=gated(core, 2), sources=[h])
    with nc.sbuf_tensor("mlp_parts", [P, KD, 2, T], F32R) as parts:
        with nc.sbuf_tensor("h_mlp", [P, KD, T], F32) as h:
            rms_stage(core, "norm_mlp", core.x, h, KD, core.gain[:, 2 * KD:3 * KD], core.mod[:, 3 * KD:4 * KD, 0])
            split_stage(core, h, parts, KD)
        with nc.sbuf_tensor("hidden", [P, MLP_TILES, 2, T], F32R) as hidden:
            def squared_relu(dve, n, slots):
                v, hi = slots[0], hidden[:, n, 0, :]
                core.dve.step(dve, dve.scalar_tensor_tensor(v, v, 0.0, v, ALU.max, ALU.mult))
                core.dve.step(dve, dve.tensor_copy(hi, v))
                dve.tensor_tensor(hidden[:, n, 1, :], v, hi.bitcast(F32), ALU.subtract)

            linear_stage(core, "mlp1", "w_mlp1", MLP_TILES, ("w_mlp2", 0), [parts], finish=squared_relu, steps=2)
            chunks = MLP_TILES // KD
            for c in range(chunks):
                linear_stage(core, f"mlp2_{c}", "w_mlp2", KD, ("w_mlp2", (c + 1) * 2 * KD) if c + 1 < chunks else ("w_in_2", 0),
                             [hidden[:, c * KD:(c + 1) * KD]], finish=gated(core, 5), first=c * 2 * KD)
    rms_stage(core, "norm_first", core.x, core.x, KD, core.prm["final1"])


def s5_setup_stage(core, s5):
    nc, dram = core.nc, core.dram
    s = {n: core.sem(f"s5_{n}") for n in ("loaded", "c_loaded", "cleared", "dt", "rate", "exp", "bounded", "sine")}
    W = HT * 64
    with ExitStack() as own:
        sb = lambda name, shape: own.enter_context(nc.sbuf_tensor(f"s5_{name}", shape, F32))
        rep = sb("rep", [P, 5, W])
        dt, e, trig, k = sb("dt", [P, W]), sb("e", [P, W]), sb("trig", [P, 2, W]), sb("k", [P, 2, W])
        kr, ki, t1, t2, inv = (sb(n, [P, W]) for n in ("kr", "ki", "t1", "t2", "inv"))
        sdt = sb("sdt", [P, PAIRS])
        sk = sb("sk", [P, PAIRS])
        with nc.Block() as block:
            @block.sync
            def _(sp):
                sp.dma_start(rep[:], dram["s5_rep"]).then_inc(s["loaded"], 16)
                sp.wait_ge(s["cleared"], 1)
                for g in range(2):
                    for part in range(2):
                        sp.dma_start(s5.c[g * 64:(g + 1) * 64, part, :, g * 16:(g + 1) * 16],
                                     dram["s5_c"][part, g * 64:(g + 1) * 64]).then_inc(s["c_loaded"], 16)

            @block.scalar
            def _(act):
                act.activation(sdt[:], core.prm["log_dt"], ACT.Exp).then_inc(s["dt"], 1)
                act.wait_ge(s["loaded"], 16)
                act.activation(dt[:], rep[:, 2, :], ACT.Exp).then_inc(s["dt"], 1)
                act.wait_ge(s["rate"], 1)
                act.activation(s5.r[:], s5.r[:], ACT.Exp)
                act.wait_ge(s["rate"], 2)
                act.activation(e[:], e[:], ACT.Exp).then_inc(s["exp"], 1)
                act.wait_ge(s["bounded"], 1)
                act.activation(trig[:], trig[:], ACT.Sin).then_inc(s["sine"], 1)

            @block.vector
            def _(dve):
                step = lambda ins: core.dve.step(dve, ins)
                mul = lambda out, a, b: step(dve.tensor_tensor(out, a, b, ALU.mult))
                dve.memset(s5.c[:], 0.0).then_inc(s["cleared"], 1)
                dve.wait_ge(s["dt"], 1)
                dve.tensor_tensor(s5.r[:], core.prm["lam_re"], sdt[:], ALU.mult).then_inc(s["rate"], 1)
                mul(s5.turn[:], core.prm["lam_im"], sdt[:])
                step(dve.tensor_scalar(s5.turn[:], s5.turn[:], 1 / (2 * math.pi), None, ALU.mult))
                step(dve.tensor_scalar(sk[:], s5.turn[:], MAGIC, None, ALU.add))
                step(dve.tensor_scalar(sk[:], sk[:], -MAGIC, None, ALU.add))
                step(dve.tensor_tensor(s5.turn[:], s5.turn[:], sk[:], ALU.subtract))
                dve.wait_ge(s["dt"], 2)
                dve.tensor_tensor(e[:], rep[:, 0, :], dt[:], ALU.mult).then_inc(s["rate"], 1)
                mul(trig[:, 0, :], rep[:, 1, :], dt[:])
                step(dve.tensor_scalar(trig[:, 1, :], trig[:, 0, :], math.pi / 2, None, ALU.add))
                sine_steps(core, dve, trig[:], k[:], s["bounded"])
                mul(t1[:], rep[:, 0, :], rep[:, 0, :])
                mul(t2[:], rep[:, 1, :], rep[:, 1, :])
                step(dve.tensor_tensor(inv[:], t1[:], t2[:], ALU.add))
                step(dve.reciprocal(inv[:], inv[:]))
                dve.wait_ge(s["exp"], 1)
                dve.wait_ge(s["sine"], 1)
                re, im = k[:, 0, :], k[:, 1, :]
                mul(re, e[:], trig[:, 1, :])
                step(dve.tensor_scalar(re, re, -1.0, None, ALU.add))
                mul(im, e[:], trig[:, 0, :])
                mul(t1[:], re, rep[:, 0, :])
                mul(t2[:], im, rep[:, 1, :])
                step(dve.tensor_tensor(kr[:], t1[:], t2[:], ALU.add))
                mul(kr[:], kr[:], inv[:])
                mul(t1[:], im, rep[:, 0, :])
                mul(t2[:], re, rep[:, 1, :])
                step(dve.tensor_tensor(ki[:], t1[:], t2[:], ALU.subtract))
                mul(ki[:], ki[:], inv[:])
                for part, (a, b, op) in enumerate(((kr, ki, ALU.subtract), (ki, kr, ALU.add))):
                    mul(t1[:], a[:], rep[:, 3, :])
                    mul(t2[:], b[:], rep[:, 4, :])
                    step(dve.tensor_tensor(t1[:], t1[:], t2[:], op))
                    for g in range(2):
                        step(dve.tensor_scalar(s5.b[:, :, part, g, :], t1[:].rearrange("p (f e) -> p f e", e=64),
                                               core.cst["group"][:, g:g + 1], None, ALU.mult))
                dve.wait_ge(s["c_loaded"], 64)
                step(dve.tensor_scalar(s5.c[:, 1], s5.c[:, 1], -1.0, None, ALU.mult))
                dve.tensor_scalar(s5.c[:, 2], s5.c[:, 0], -1.0, None, ALU.mult)


MAGIC = 12582912.0


def local_mixers_stage(core, s5, proj, conv):
    nc, ps = core.nc, core.ps
    s = {n: core.sem(f"mix_{n}") for n in ("glu", "diag", "conv", "convolved", "turns", "phase", "trig", "bu", "turned",
                                           "rotated", "scan_r", "scan_i", "out_c", "out_s", "y", "skip", "summed")}
    pad = CONV31 - 1
    with ExitStack() as own:
        sb = lambda name, shape: own.enter_context(nc.sbuf_tensor(f"mix_{name}", shape, F32))
        c = sb("c", [P, HT, pad + T])
        diag = sb("diag", [P, 2, CONV31, P])
        phase, whole, trig = sb("phase", [P, 2, 2, T]), sb("whole", [P, 2, T]), sb("trig", [P, 2, 2, T])
        p1, p2, bt, v = sb("p1", [P, 2, T]), sb("p2", [P, 2, T]), sb("bt", [P, 2, T]), sb("v", [P, 2, 2, T])
        oc, os = sb("oc", [P, 2, 2, T]), sb("os", [P, 2, 2, T])
        with nc.Block() as block:
            @block.gpsimd
            def _(pool):
                def make_diag(f):
                    if f >= 2:
                        pool.wait_ge(s["conv"], f - 1)
                    taps = core.prm["conv_w"][:, f * CONV31:(f + 1) * CONV31]
                    pool.tensor_tensor(diag[:, f % 2], spread(core.cst["ident"], 1, CONV31), spread(taps, 2, P),
                                       ALU.mult).then_inc(s["diag"], 1)

                make_diag(0)
                for n in range(PAIRS):
                    if n % 4 == 1 and n // 4 + 1 < HT:
                        make_diag(n // 4 + 1)
                    pool.wait_ge(s["scan_i"], n + 1)
                    if n >= 2:
                        pool.wait_ge(s["y"], n - 1)
                    pool.tensor_tensor(os[:, n % 2], v[:, n % 2], spread(trig[:, n % 2, 0, :], 1, 2),
                                       ALU.mult).then_inc(s["out_s"], 1)

            @block.scalar
            def _(act):
                def make_turns(n):
                    if n >= 2:
                        act.wait_ge(s["trig"], n - 1)
                    ph, turn = phase[:, n % 2], s5.turn[:, n:n + 1]
                    act.activation(ph[:, 0, :], core.cst["iota"], ACT.Identity, scale=turn,
                                   bias=core.small[:, ZERO_COL:ZERO_COL + 1])
                    act.activation(ph[:, 1, :], core.cst["iota"], ACT.Identity, scale=turn,
                                   bias=core.small[:, QUARTER_COL:QUARTER_COL + 1]).then_inc(s["turns"], 1)

                make_turns(0)
                make_turns(1)
                for n in range(PAIRS):
                    act.wait_ge(s["phase"], n + 1)
                    if n >= 2:
                        act.wait_ge(s["out_c"], n - 1)
                        act.wait_ge(s["out_s"], n - 1)
                    act.activation(trig[:, n % 2], phase[:, n % 2], ACT.Sin, scale=TWO_PI).then_inc(s["trig"], 1)
                    if n + 2 < PAIRS:
                        make_turns(n + 2)
                    if n % 4 == 3:
                        f = n // 4
                        act.wait_ge(s["conv"], f + 1)
                        act.activation(conv[:, f, :], ps[:, 6 + f % 2, 0:T], ACT.Identity,
                                       bias=core.prm["conv_b"][:, f:f + 1]).then_inc(s["convolved"], 1)

            @block.tensor
            def _(pe):
                def outputs(n):
                    f, q = n // 4, n % 4
                    if q == 0 and f >= 2:
                        pe.wait_ge(s["skip"], f - 1)
                    pe.wait_ge(s["out_c"], n + 1)
                    pe.wait_ge(s["out_s"], n + 1)
                    terms = ((0, oc, 0), (2, os, 1), (1, os, 0), (1, oc, 1))
                    for m, (part, src, half) in enumerate(terms):
                        mm = pe.matmul(ps[32 * q:32 * q + 32, 2 + f % 2, 0:T], s5.c[:, part, n, :],
                                       src[:, n % 2, half, :], start=m == 0, stop=m == 3)
                    mm.then_inc(s["y"], 1)

                for n in range(PAIRS):
                    f, q = n // 4, n % 4
                    if n >= 2:
                        pe.wait_ge(s["turned"], n - 1)
                    rows = slice(32 * q, 32 * q + 32)
                    for part in range(2):
                        mm = pe.matmul(ps[:, n % 2, part * T:(part + 1) * T],
                                       s5.b[rows, f, part].rearrange("p g e -> p (g e)"),
                                       proj[rows, 2 * HT + f, :], start=True, stop=True)
                    mm.then_inc(s["bu"], 1)
                    if q == 0:
                        pe.wait_ge(s["diag"], f + 1)
                        pe.wait_ge(s["glu"], 1)
                        if f >= 2:
                            pe.wait_ge(s["convolved"], f - 1)
                    for k in range(8 * q, min(8 * q + 8, CONV31)):
                        mm = pe.matmul(ps[:, 6 + f % 2, 0:T], diag[:, f % 2, k, :], c[:, f, k:k + T],
                                       start=k == 0, stop=k == CONV31 - 1)
                    if q == 3:
                        mm.then_inc(s["conv"], 1)
                    if n:
                        outputs(n - 1)
                outputs(PAIRS - 1)

            @block.vector
            def _(dve):
                dve.memset(c[:, :, 0:pad], 0.0)
                dve.tensor_tensor(c[:, :, pad:], proj[:, 0:HT, :], proj[:, HT:2 * HT, :], ALU.mult).then_inc(s["glu"], 1)

                def skip(f):
                    dve.wait_ge(s["y"], 4 * f + 4)
                    u = proj[:, 2 * HT + f, :]
                    dve.scalar_tensor_tensor(u, u, core.prm["ssm_d"][:, f:f + 1], ps[:, 2 + f % 2, 0:T],
                                             ALU.mult, ALU.add).then_inc(s["skip"], 1)

                def make_phase(n):
                    dve.wait_ge(s["turns"], n + 1)
                    if n:
                        dve.wait_ge(s["phase"], n)
                    ph = phase[:, n % 2]
                    core.dve.step(dve, dve.tensor_scalar(whole[:], ph, MAGIC, -MAGIC, ALU.add, ALU.add))
                    dve.tensor_tensor(ph, ph, whole[:], ALU.subtract).then_inc(s["phase"], 1)

                make_phase(0)
                make_phase(1)
                for n in range(PAIRS):
                    dve.wait_ge(s["bu"], n + 1)
                    dve.wait_ge(s["trig"], n + 1)
                    bu = ps[:, n % 2, :].rearrange("p (a t) -> p a t", a=2)
                    cos, sin = (spread(trig[:, n % 2, a, :], 1, 2) for a in (1, 0))
                    dve.tensor_tensor(p1[:], bu, cos, ALU.mult)
                    dve.tensor_tensor(p2[:], bu, sin, ALU.mult).then_inc(s["turned"], 1)
                    dve.wait_ge(s["turned"], n + 1)
                    dve.tensor_tensor(bt[:, 0, :], p1[:, 0, :], p2[:, 1, :], ALU.add).then_inc(s["rotated"], 1)
                    dve.tensor_tensor(bt[:, 1, :], p1[:, 1, :], p2[:, 0, :], ALU.subtract).then_inc(s["rotated"], 1)
                    if n + 2 < PAIRS:
                        make_phase(n + 2)
                    if n >= 2:
                        dve.wait_ge(s["out_s"], n - 1)
                    rate = s5.r[:, n:n + 1].broadcast_to([P, T])
                    for a, done in enumerate(("scan_r", "scan_i")):
                        dve.wait_ge(s["rotated"], 2 * n + a + 1)
                        dve.tensor_tensor_scan(v[:, n % 2, a, :], rate, bt[:, a, :], 0.0, ALU.mult,
                                               ALU.add).then_inc(s[done], 1)
                    dve.wait_ge(s["scan_r"], n + 1)
                    dve.wait_ge(s["scan_i"], n + 1)
                    if n >= 2:
                        dve.wait_ge(s["y"], n - 1)
                    dve.tensor_tensor(oc[:, n % 2], v[:, n % 2], cos, ALU.mult).then_inc(s["out_c"], 1)
                    if n % 4 == 1 and n > 4:
                        skip(n // 4 - 1)
                skip(HT - 1)


def glu_stage(core, y, parts, next_w):
    with core.nc.Block() as block:
        @block.scalar
        def _(act):
            act.activation(y, y, ACT.Gelu_apprx_tanh)

    def gate(dve, n, slots):
        dve.tensor_tensor(y[:, n, :], y[:, n, :], slots[0], ALU.mult)

    linear_stage(core, "glu", "w_glu", HT, next_w, [parts],
                 shape=lambda act, n, slots: act.activation(slots[0], slots[0], ACT.Sigmoid), finish=gate,
                 quarters=2, sources=[y])


def group_norm_stage(core, c, y, h):
    nc, ps = core.nc, core.ps
    s = {n: core.sem(f"gn_{n}") for n in ("sums", "squared", "centred", "rooted", "scaled", "silu", "ssm_out", "conv_out")}
    width = HT * P
    with ExitStack() as own:
        sb = lambda name, shape: own.enter_context(nc.sbuf_tensor(f"gn_{name}", shape, F32))
        sq, std = sb("sq", [P, HT, T]), sb("std", [P, 3, T])
        with nc.Block() as block:
            @block.tensor
            def _(pe):
                def total(bank, src):
                    for t in range(HT):
                        mm = pe.matmul(ps[:, bank, 0:T], core.ones[:], src[:, t, :], start=t == 0, stop=t == HT - 1)
                    mm.then_inc(s["sums"], 1)
                total(0, c)
                for n in range(3):
                    pe.wait_ge(s["squared"], n + 1)
                    total(n + 1, sq)

            @block.scalar
            def _(act):
                eps = core.small[:, EPS_COL:EPS_COL + 1]

                def root(n):
                    act.wait_ge(s["sums"], n + 2)
                    act.activation(std[:, n, :], ps[:, n + 1, 0:T], ACT.Sqrt, bias=eps,
                                   scale=1.0 / width).then_inc(s["rooted"], 1)
                act.activation(sq[:], y, ACT.Square).then_inc(s["squared"], 1)
                root(0)
                act.wait_ge(s["centred"], 1)
                act.activation(sq[:], c, ACT.Square).then_inc(s["squared"], 1)
                root(1)
                for t in range(HT):
                    act.wait_ge(s["scaled"], t + 1)
                    act.activation(c[:, t, :], c[:, t, :], ACT.Silu, bias=core.prm["ln_b"][:, t:t + 1]).then_inc(s["silu"], 1)
                act.wait_ge(s["silu"], HT)
                act.activation(sq[:], c, ACT.Square).then_inc(s["squared"], 1)
                root(2)

            @block.vector
            def _(dve):
                dve.wait_ge(s["sums"], 1)
                dve.scalar_tensor_tensor(c, spread(ps[:, 0, 0:T], 1, HT), -1.0 / width, c, ALU.mult,
                                         ALU.add).then_inc(s["centred"], 1)
                for n, (src, dst, gain) in enumerate(((y, h[:, HT:, :], "grp_ssm"), (c, c, "ln_g"),
                                                      (c, h[:, 0:HT, :], "grp_conv"))):
                    dve.wait_ge(s["rooted"], n + 1)
                    core.dve.step(dve, dve.reciprocal(std[:, n, :], std[:, n, :]))
                    for t in range(HT):
                        dve.scalar_tensor_tensor(dst[:, t, :], src[:, t, :], core.prm[gain][:, t:t + 1], std[:, n, :],
                                                 ALU.mult, ALU.mult).then_inc(s[("ssm_out", "scaled", "conv_out")[n]], 1)


def values_stage(core, mem, v, next_w):
    nc, ps = core.nc, core.ps
    Q, N = core.quarters, core.tiles
    blocks = D // BANK
    rounds = blocks // 2
    with nc.Block() as block:
        @block.sync
        def _(sp):
            stream(core, sp, "w_v", blocks * HALF, next_w)

        @block.scalar
        def _(act):
            split_and_take(core, act, make_hi, lambda act, n, i, s: None, rounds, 2, KD)

        @block.vector
        def _(dve):
            def take(dve, n, i, s):
                dve.wait_ge(core.multiplied, i * (2 * KD) + (Q + SLOTS + (s + 1) * KD))
                dve.tensor_copy(v[:, :, n, :], ps[:, 2 * s:2 * s + 2, :]).then_inc(core.summed, 1)
            split_and_take(core, dve, make_lo, take, rounds, 2, KD)

        @block.tensor
        def _(pe):
            with pe.Fori(0, rounds) as i:
                for b in range(2):
                    pe.wait_ge(core.summed, i * 2 + (N + b + 1))
                    for k in range(KD):
                        pe.wait_ge(core.split, i * (2 * KD) + (Q + b * KD + k + 1))
                        hi, lo = (w[:, k % SLOTS].rearrange("p k m -> p (k m)") for w in (core.hi, core.lo))
                        for m in range(TT):
                            rows = slice(m * P, (m + 1) * P)
                            for j, (part, w) in enumerate(((0, hi), (0, lo), (1, hi))):
                                mm = pe.matmul(ps[:, 2 * b + m, :], mem[:, k, part, rows], w,
                                               start=(j, k) == (0, 0), stop=(j, k) == (2, KD - 1))
                        mm.then_inc(core.multiplied, 1)
    core.quarters += blocks * KD
    core.tiles += blocks


def attention_stage(core, q, k, v, out):
    nc, ps = core.nc, core.ps
    s = {n: core.sem(f"att_{n}") for n in ("scores", "max", "exp", "scaled", "turned", "probs", "out", "rounded", "taken")}
    units = [(h, t) for h in range(MEM_HEADS) for t in range(TT)]
    scale = 1.0 / math.sqrt(D // MEM_HEADS)
    with ExitStack() as own:
        sb = lambda name, shape: own.enter_context(nc.sbuf_tensor(f"att_{name}", shape, F32))
        p, pt = sb("p", [P, 8, T]), sb("pt", [P, TT, MEM_HEADS, T])
        top, total = sb("top", [P, 8]), sb("total", [P, 8])
        with nc.Block() as block:
            @block.tensor
            def _(pe):
                for n, (h, t) in enumerate(units):
                    for d in range(4):
                        mm = pe.matmul(ps[:, n, 0:T], q[:, 4 * h + d, t * P:(t + 1) * P], k[:, 4 * h + d, :],
                                       start=d == 0, stop=d == 3)
                    mm.then_inc(s["scores"], 1)
                for n in range(8):
                    pe.wait_ge(s["scaled"], n + 1)
                    for m in range(TT):
                        mm = pe.transpose(ps[:, n, m * P:(m + 1) * P], p[:, n, m * P:(m + 1) * P], core.cst["ident"])
                    mm.then_inc(s["turned"], 1)
                for n in range(KD):
                    h = n // 4
                    pe.wait_ge(s["probs"], 8)
                    if n >= 8:
                        pe.wait_ge(s["taken"], n - 7)
                    for m in range(TT):
                        mm = pe.matmul(ps[:, n % 8, 0:T], v[:, m, n // 4, (n % 4) * P:(n % 4 + 1) * P], pt[:, m, h, :],
                                       start=m == 0, stop=m == TT - 1)
                    mm.then_inc(s["out"], 1)

            @block.scalar
            def _(act):
                for n in range(8):
                    act.wait_ge(s["max"], n + 1)
                    act.activation(p[:, n, :], ps[:, n, 0:T], ACT.Exp, bias=top[:, n:n + 1], scale=scale,
                                   accum_out=total[:, n:n + 1]).then_inc(s["exp"], 1)
                for n in range(KD):
                    act.wait_ge(s["out"], n + 1)
                    act.activation(out[:, n, 0, :], ps[:, n % 8, 0:T], ACT.Copy).then_inc(s["rounded"], 1)

            @block.vector
            def _(dve):
                for n in range(8):
                    dve.wait_ge(s["scores"], n + 1)
                    core.dve.step(dve, dve.reduce_max(top[:, n:n + 1], ps[:, n, 0:T], AX_X))
                    dve.tensor_scalar(top[:, n:n + 1], top[:, n:n + 1], -scale, None, ALU.mult).then_inc(s["max"], 1)
                for n in range(8):
                    dve.wait_ge(s["exp"], n + 1)
                    core.dve.step(dve, dve.reciprocal(total[:, n:n + 1], total[:, n:n + 1]))
                    dve.tensor_scalar(p[:, n, :], p[:, n, :], total[:, n:n + 1], None, ALU.mult).then_inc(s["scaled"], 1)
                for n, (h, t) in enumerate(units):
                    dve.wait_ge(s["turned"], n + 1)
                    dve.tensor_copy(pt[:, :, h, t * P:(t + 1) * P],
                                    ps[:, n, 0:T].rearrange("p (m l) -> p m l", m=TT)).then_inc(s["probs"], 1)
                for n in range(KD):
                    dve.wait_ge(s["rounded"], n + 1)
                    dve.tensor_tensor(out[:, n, 1, :], ps[:, n % 8, 0:T], out[:, n, 0, :].bitcast(F32),
                                      ALU.subtract).then_inc(s["taken"], 1)


def top_experts_stage(core, q, keys, turned):
    nc, ps = core.nc, core.ps
    s = {n: core.sem(f"top_{n}") for n in ("scores", "copied", "shifted", "exp", "ready", "turned", "taken")}
    with ExitStack() as own:
        sb = lambda name, shape, dt=F32: own.enter_context(nc.sbuf_tensor(f"top_{name}", shape, dt))
        sc = sb("sc", [P, TT, 2, PEER_HEADS, KEYS])
        val, idx = sb("val", [P, TT, 2, PEER_HEADS, TOPK]), sb("idx", [P, TT, 2, PEER_HEADS, TOPK], U32)
        idf = sb("idf", [P, TT, 2, PEER_HEADS, TOPK])
        cand = sb("cand", [P, TT, PEER_HEADS, TOPK * TOPK])
        best, pos = sb("best", [P, TT, PEER_HEADS, TOPK]), sb("pos", [P, TT, PEER_HEADS, TOPK], U32)
        half, halff = sb("half", [P, 2, TT, PEER_HEADS, TOPK], U32), sb("halff", [P, 2, TT, PEER_HEADS, TOPK])
        pick = sb("pick", [P, PEER_HEADS, TOPK, TOPK])
        chosen = sb("chosen", [P, TT, 3, PEER_HEADS, TOPK])
        total = sb("total", [P, TT, PEER_HEADS])
        with nc.Block() as block:
            @block.tensor
            def _(pe):
                for t in range(TT):
                    for a in range(2):
                        rows = slice(a * 64, a * 64 + 64)
                        for h in range(PEER_HEADS):
                            mm = pe.matmul(ps[:, 4 * t + 2 * a + h // 4, (h % 4) * P:(h % 4 + 1) * P],
                                           q[rows, h, t * P:(t + 1) * P], keys[rows, h, :], start=True, stop=True)
                        mm.then_inc(s["scores"], 1)
                for t in range(TT):
                    pe.wait_ge(s["ready"], t + 1)
                    for n in range(3):
                        mm = pe.transpose(ps[:, t, n * P:(n + 1) * P],
                                          chosen[:, t, n].rearrange("p h k -> p (h k)"), core.cst["ident"])
                    mm.then_inc(s["turned"], 1)

            @block.scalar
            def _(act):
                for t in range(TT):
                    for a in range(2):
                        act.wait_ge(s["scores"], 2 * t + a + 1)
                        act.activation(sc[:, t, a].rearrange("p (b h) n -> p b (h n)", b=2),
                                       ps[:, 4 * t + 2 * a:4 * t + 2 * a + 2, :], ACT.Copy).then_inc(s["copied"], 1)
                act.wait_ge(s["shifted"], 1)
                act.activation(chosen[:, :, 2], chosen[:, :, 2], ACT.Exp).then_inc(s["exp"], 1)
                for t in range(TT):
                    act.wait_ge(s["turned"], t + 1)
                    act.activation(turned[:, :, t * P:(t + 1) * P], ps[:, t, 0:3 * P].rearrange("p (n l) -> p n l", n=3),
                                   ACT.Copy)

            @block.vector
            def _(dve):
                step = lambda ins: core.dve.step(dve, ins)

                def top16(units, src, values, index):
                    for lo in (0, 8):
                        for u in units:
                            ins = dve.max(values(u)[:, lo:lo + 8], src(u))
                        step(ins)
                        for u in units:
                            ins = dve.max_index(index(u)[:, lo:lo + 8], values(u)[:, lo:lo + 8], src(u))
                        step(ins)
                        if lo == 0:
                            for u in units:
                                ins = dve.match_replace(src(u), values(u)[:, 0:8], src(u), -3.0e38)
                            step(ins)

                dve.wait_ge(s["copied"], 4)
                top16([(t, a, h) for t in range(TT) for a in range(2) for h in range(PEER_HEADS)],
                      lambda u: sc[:, u[0], u[1], u[2], :], lambda u: val[:, u[0], u[1], u[2], :],
                      lambda u: idx[:, u[0], u[1], u[2], :])
                step(dve.tensor_copy(idf[:], idx[:]))
                for t in range(TT):
                    pairs = cand[:, t].rearrange("p h (a b) -> p h a b", b=TOPK)
                    ins = dve.tensor_tensor(pairs, spread(val[:, t, 0], 3, TOPK), spread(val[:, t, 1], 2, TOPK), ALU.add)
                step(ins)
                top16([(t, h) for t in range(TT) for h in range(PEER_HEADS)],
                      lambda u: cand[:, u[0], u[1], :], lambda u: best[:, u[0], u[1], :],
                      lambda u: pos[:, u[0], u[1], :])
                dve.tensor_scalar(half[:, 0], pos[:], 4, None, ALU.logical_shift_right)
                step(dve.tensor_scalar(half[:, 1], pos[:], 15, None, ALU.bitwise_and))
                step(dve.tensor_copy(halff[:], half[:]))
                for t in range(TT):
                    ins = dve.tensor_tensor(chosen[:, t, 2], best[:, t],
                                            best[:, t, :, 0:1].broadcast_to([P, PEER_HEADS, TOPK]), ALU.subtract)
                ins.then_inc(s["shifted"], 1)
                ranks = core.cst["iota"][:, 0:TOPK].unsqueeze(1).unsqueeze(1).broadcast_to([P, PEER_HEADS, TOPK, TOPK])
                for t in range(TT):
                    for a in range(2):
                        step(dve.tensor_tensor(pick[:], ranks, spread(halff[:, a, t], 3, TOPK), ALU.is_equal))
                        step(dve.tensor_tensor(pick[:], pick[:], spread(idf[:, t, a], 2, TOPK), ALU.mult))
                        step(dve.tensor_reduce(chosen[:, t, a], pick[:], AX_X, ALU.add))
                dve.wait_ge(s["exp"], 1)
                for t in range(TT):
                    step(dve.tensor_reduce(total[:, t], chosen[:, t, 2], AX_X, ALU.add))
                step(dve.reciprocal(total[:], total[:]))
                for t in range(TT):
                    dve.tensor_tensor(chosen[:, t, 2], chosen[:, t, 2], spread(total[:, t], 2, TOPK),
                                      ALU.mult).then_inc(s["ready"], 1)


def gates_stage(core, turned, gates):
    nc, ps = core.nc, core.ps
    GROUP = 8
    s = {n: core.sem(f"gates_{n}") for n in ("left_act", "left_abs", "right", "multiplied", "stored")}
    keys = core.cst["iota"][:, 0:KEYS]
    left = core.hi[:].rearrange("p s k m -> p (s k) m")
    with nc.sbuf_tensor("gates_right", [P, GROUP, KEYS], F32) as right:
        rounds = T // GROUP
        with nc.Block() as block:
            @block.tensor
            def _(pe):
                pe.sem_inc(s["multiplied"], GROUP)
                with pe.Fori(0, rounds) as i:
                    for b in range(2):
                        pe.wait_ge(s["stored"], i * 2 + (b + 1))
                        for j in range(4):
                            n = 4 * b + j
                            if j == 2:
                                pe.wait_ge(s["left_act"], i * 2 + (b + 1))
                            pe.wait_ge(s["right"], i * GROUP + (n + 1))
                            pe.matmul(ps[:, b, j * P:(j + 1) * P], left[:, n, :].bitcast(F32), right[:, n, :],
                                      start=True, stop=True).then_inc(s["multiplied"], 1)

            @block.scalar
            def _(act):
                def make_left(i, b):
                    n = 4 * (b % 2) + 2
                    act.wait_ge(s["multiplied"], i * GROUP + (4 * b + 3))
                    act.activation(left[:, n, :], keys, ACT.Abs, scale=-1.0,
                                   bias=turned[:, 0, bass.ds(i * GROUP + (4 * b + 2), 1)]).then_inc(s["left_abs"], 1)
                    act.wait_ge(s["left_abs"], i * 2 + (b + 1))
                    act.activation(left[:, n, :], left[:, n, :].bitcast(F32), ACT.Relu, scale=-1.0,
                                   bias=core.ones[:, 0:1]).then_inc(s["left_act"], 1)

                def store(i, b):
                    act.wait_ge(s["multiplied"], i * GROUP + (GROUP + 4 * b + 4))
                    act.activation(gates[:, :, bass.ds(i * GROUP + 4 * b, 4)].rearrange("p j t -> p t j"),
                                   ps[:, b, :].rearrange("p (t j) -> p t j", t=4), ACT.Copy).then_inc(s["stored"], 1)

                act.sem_inc(s["stored"], 2)
                make_left(0, 0)
                with act.Fori(0, rounds - 1) as i:
                    for b in range(2):
                        make_left(i, b + 1)
                        store(i, b)
                make_left(rounds - 1, 1)
                store(rounds - 1, 0)
                store(rounds - 1, 1)

            @block.vector
            def _(dve):
                with dve.Fori(0, rounds) as i:
                    for n in range(GROUP):
                        at = bass.ds(i * GROUP + n, 1)
                        dve.wait_ge(s["multiplied"], i * GROUP + (n + 1))
                        if n % 4 != 2:
                            dve.tensor_scalar(left[:, n, :], keys, turned[:, 0, at], None, ALU.is_equal)
                        dve.tensor_scalar(right[:, n, :], keys, turned[:, 1, at], turned[:, 2, at],
                                          ALU.is_equal, ALU.mult).then_inc(s["right"], 1)


def onto_stream(core):
    def finish(dve, n, slots):
        dve.tensor_tensor(core.x[:, n, :], core.x[:, n, :], slots[0], ALU.add)
    return finish


def second_block(core):
    nc = core.nc

    class S5:
        pass

    with ExitStack() as mixers:
        sb = lambda name, shape: mixers.enter_context(nc.sbuf_tensor(name, shape, F32))
        proj, conv = sb("proj", [P, 3 * HT, T]), sb("conv", [P, HT, T])
        with nc.sbuf_tensor("in2_parts", [P, KD, 2, T], F32R) as parts, nc.sbuf_tensor("h_in2", [P, KD, T], F32) as h:
            rms_stage(core, "norm_mix2", core.x, h, KD, core.prm["norm_mix"])
            rows = lambda part: (lambda n: proj[:, n + part * HT, :])
            linear_stage(core, "in2_0", "w_in_2", HT, ("w_in_2", 2 * HT), [parts], into=rows(0), sources=[h])
            linear_stage(core, "in2_1", "w_in_2", HT, ("w_in_2", 4 * HT), [parts], first=2 * HT,
                         shape=lambda act, n, slots: act.activation(slots[0], slots[0], ACT.Sigmoid),
                         finish=lambda dve, n, slots: dve.tensor_copy(proj[:, n + HT, :], slots[0]))
            linear_stage(core, "in2_2", "w_in_2", HT, ("w_glu", 0), [parts], first=4 * HT, into=rows(2))
        with ExitStack() as scans:
            sb2 = lambda name, shape: scans.enter_context(nc.sbuf_tensor(name, shape, F32))
            s5 = S5()
            s5.b, s5.c = sb2("s5_b", [P, HT, 2, 2, 64]), sb2("s5_cc", [P, 3, PAIRS, 32])
            s5.r, s5.turn = sb2("s5_r", [P, PAIRS]), sb2("s5_turn", [P, PAIRS])
            s5_setup_stage(core, s5)
            local_mixers_stage(core, s5, proj, conv)
        y = proj[:, 2 * HT:, :]
        with nc.sbuf_tensor("glu_parts", [P, HT, 2, T], F32R) as parts:
            glu_stage(core, y, parts, ("w_out_2", 0))
        with nc.sbuf_tensor("out2_parts", [P, KD, 2, T], F32R) as parts, nc.sbuf_tensor("h_out2", [P, KD, T], F32) as h:
            group_norm_stage(core, conv[:], y, h)
            linear_stage(core, "mix2_out", "w_out_2", KD, ("w_q", 0), [parts], finish=onto_stream(core), sources=[h])
    with ExitStack() as attention:
        sb = lambda name, shape, dt=F32: attention.enter_context(nc.sbuf_tensor(name, shape, dt))
        q, k, v = sb("q", [P, KD, T]), sb("k", [P, KD, T]), sb("v", [P, TT, 4, BANK])
        parts, h, mem = sb("att_parts", [P, KD, 2, T], F32R), sb("h_att", [P, KD, T]), sb("mem", [P, KD, T])
        rms_stage(core, "norm_q", core.x, h, KD, core.prm["norm_mem"])
        linear_stage(core, "mem_q", "w_q", KD, ("w_k", 0), [parts], into=lambda n: q[:, n, :], sources=[h],
                     loads=[(mem[:], "mem")])
        rms_stage(core, "norm_mem", mem, mem, KD, core.prm["mem_norm"])
        linear_stage(core, "mem_k", "w_k", KD, ("w_v", 0), [parts], into=lambda n: k[:, n, :], sources=[mem])
        values_stage(core, parts, v, ("w_o", 0))
        attention_stage(core, q, k, v, parts)
        linear_stage(core, "mem_out", "w_o", KD, ("w_peer_q", 0), [parts], finish=onto_stream(core))
    with nc.sbuf_tensor("expert_parts", [P, KD, 2, T], F32R) as parts, nc.sbuf_tensor("turned", [P, 3, T], F32) as turned:
        with ExitStack() as choice:
            sb = lambda name, shape: choice.enter_context(nc.sbuf_tensor(name, shape, F32))
            q, keys = sb("peer_q", [P, PEER_HEADS, T]), sb("peer_keys", [P, PEER_HEADS, KEYS])
            with nc.sbuf_tensor("h_ffn", [P, KD, T], F32) as h:
                rms_stage(core, "norm_ffn", core.x, h, KD, core.prm["norm_ffn"])
                linear_stage(core, "peer_q", "w_peer_q", PEER_HEADS, ("w_u", 0), [parts], into=lambda n: q[:, n, :],
                             sources=[h], loads=[(keys[:], "peer_keys")])
            top_experts_stage(core, q, keys, turned)
        with nc.sbuf_tensor("gates", [P, KEYS, T], F32) as gates:
            gates_stage(core, turned, gates)

            def gate_experts(dve, n, slots):
                dve.tensor_tensor(gates[:, n, :], gates[:, n, :], slots[0], ALU.mult)

            linear_stage(core, "expert_up", "w_u", KEYS, ("w_v_tab", 0), [parts], finish=gate_experts,
                         shape=lambda act, n, slots: act.activation(slots[0], slots[0], ACT.Gelu_apprx_tanh))
            chunks = KEYS // KD
            for c in range(chunks):
                linear_stage(core, f"expert_down_{c}", "w_v_tab", KD,
                             ("w_v_tab", (c + 1) * 2 * KD) if c + 1 < chunks else None, [parts],
                             finish=onto_stream(core), first=c * 2 * KD, sources=[gates[:, c * KD:(c + 1) * KD, :]])
    rms_stage(core, "norm_last", core.x, core.x, KD, core.prm["final2"])


def second_layout(a, d):
    d["mem"] = feature_major(a["mem_2"][0])
    d["w_in_2"] = blocks(a["w_in_2"][0])
    d["w_glu"] = blocks(a["ssm_glu_w_2"][0])
    d["w_out_2"] = blocks(a["w_out_2"][0])
    d["w_q"] = blocks(a["w_q_mem_2"][0])
    kv = a["w_kv_mem_2"][0]
    d["w_k"] = blocks(kv[:, :D])
    d["w_v"] = row_blocks(kv[:, D:])
    d["w_o"] = blocks(a["w_o_mem_2"][0])
    d["w_peer_q"] = blocks(a["peer_w_q_2"][0])
    d["peer_keys"] = a["peer_keys_2"][0].transpose(1, 3, 0, 2).reshape(P, PEER_HEADS, KEYS)
    by_second_key = lambda w: w.reshape(KEYS, KEYS, D).transpose(1, 0, 2).reshape(KEYS * KEYS, D)
    d["w_u"] = blocks(by_second_key(a["peer_u_2"][0]).T)
    d["w_v_tab"] = blocks(by_second_key(a["peer_v_2"][0]), D)
    over = lambda v: np.broadcast_to(v.reshape(HT, 8, 1, 64), (HT, 8, 16, 64))
    rep = [over(a["ssm_lam_re_2"][0]), over(a["ssm_lam_im_2"][0]),
           over(np.repeat(a["ssm_log_dt_2"][0], 64).reshape(-1, 64)),
           a["ssm_b_re_2"][0].reshape(HT, 8, 64, 16).transpose(0, 1, 3, 2),
           a["ssm_b_im_2"][0].reshape(HT, 8, 64, 16).transpose(0, 1, 3, 2)]
    d["s5_rep"] = np.stack([v.transpose(1, 2, 0, 3).reshape(P, HT * 64) for v in rep], axis=1)
    c = np.stack([a["ssm_c_re_2"][0], a["ssm_c_im_2"][0]]).reshape(2, PAIRS, 2, 16, 64)
    d["s5_c"] = c.transpose(0, 2, 4, 1, 3).reshape(2, P, PAIRS, 16)


def two_block_kernel(nc, dram, out):
    with ExitStack() as ctx:
        core = Core(nc, ctx, dram)
        first_block(core)
        stored = core.sem("result_stored")
        second_block(core)
        with nc.Block() as block:
            @block.sync
            def _(sp):
                sp.dma_start(out, core.x[:]).then_inc(stored, 16)
                sp.wait_ge(stored, 16)



def shape_constants():
    consts = np.zeros((P, N_CONST), np.float32)
    r = np.arange(P)
    at = lambda n: slice(CONST_AT[n], CONST_AT[n] + CONST_COLS[n])
    consts[:, at("ident")] = np.eye(P)
    consts[:, at("tri_f")] = r[:, None] <= r[None, :]
    consts[:, at("tri_b")] = r[:, None] >= r[None, :]
    consts[:, at("iota")] = np.arange(T)
    consts[:4, at("halves")] = np.arange(4)[:, None] % 2 == np.arange(2)
    consts[:, at("group")] = (r[:, None] // 16) % 2 == np.arange(2)
    f32 = np.float32
    t = np.linspace(0.0, 1.0, T, dtype=f32)[:, None]
    bands = 16
    w = (f32(2.0 * math.pi) * np.arange(T, dtype=f32)[:, None] / f32(T)).astype(f32)
    f = np.linspace(1e-4, bands - 1, bands, dtype=f32)[None, :]
    feats = np.concatenate([t, np.cos(f * w), -np.sin(f * w)], axis=-1).astype(f32)
    deltas = np.linspace(math.log(1e-2) / 1.5, math.log(1e-2) / 0.3, HY, dtype=f32)
    window = np.exp(-t * np.abs(deltas)).astype(f32)
    n = 2 * T
    tt, ff = np.arange(T)[:, None], np.arange(T)[None, :]
    angle = 2 * np.pi * ((tt * ff) % n) / n
    cos, sin = np.cos(angle), -np.sin(angle)
    nyquist = (-1.0) ** np.arange(T)
    cos_n, sin_n = cos[:, :P].copy(), sin[:, :P].copy()
    cos_n[:, 0] = sin_n[:, 0] = nyquist
    sin0 = sin[:, :P].copy()
    sin0[:, 0] = 0
    mats = np.stack([cos[:, :P], cos[:, P:], cos_n, sin_n, sin0, sin[:, P:]], axis=1)
    dft = mats.reshape(TT, P, 6, P).transpose(1, 0, 2, 3)
    ci, si = cos.T * 2 / n, sin.T * 2 / n
    ci[0] /= 2
    si[0] = nyquist / n
    inverse = np.concatenate([ci, si]).reshape(4, P, T).transpose(1, 0, 2)
    as32 = lambda a: np.ascontiguousarray(a, dtype=np.float32)
    return {"consts": consts, "feats": as32(feats.T), "dft": as32(dft), "inverse": as32(inverse),
            "window": as32(window.reshape(TT, P, HY).transpose(1, 0, 2))}


def columns(v):
    v = np.asarray(v)
    return v.reshape(-1, P).T


def blocks(w, chunk=None):
    K, N = w.shape
    chunk = chunk or K
    a = w.reshape(K // chunk, chunk // (HALF * P), HALF, P, N // P, P).transpose(0, 4, 1, 3, 2, 5)
    return a.reshape(-1, P, HALF * P)


def row_blocks(w):
    N = w.shape[1]
    a = w.reshape(KD // 2, 2, P, N // BANK, BANK).transpose(3, 0, 2, 1, 4)
    return a.reshape(-1, P, 2 * BANK)


def feature_major(x):
    return x.reshape(T, KD, P).transpose(2, 1, 0)


def lay_out(i):
    a = {n: np.asarray(v) for n, v in i.items()}
    w_in = a["w_in"][0]
    o0, o1 = HY_TILES * P, (HY_TILES + XBC_TILES) * P
    o2 = o1 + 2 * HEADS
    d = {
        "x": feature_major(a["x"][0]), "ctx": feature_major(a["ctx"][0]),
        "w_ada": row_blocks(a["w_ada"][0]),
        "w_mix": blocks(np.concatenate([w_in[:, :o1], w_in[:, o2:]], axis=1)),
        "w_dt": w_in[:, o1:o2].reshape(KD, P, 2 * HEADS).transpose(1, 0, 2),
        "w_out": blocks(a["w_out"][0]), "w_mlp1": blocks(a["w_mlp1"][0]), "w_mlp2": blocks(a["w_mlp2"][0], D),
        "filt_w1": a["filt_w1"][0], "filt_w2": a["filt_w2"][0], "filt_w3": a["filt_w3"][0],
    }
    rows = lambda v: np.broadcast_to(v.reshape(1, -1), (P, v.size))
    state = lambda v: v.reshape(PAIRS, P).T
    filt = np.stack([np.pad(a[n][0], (0, P - 64)) for n in ("filt_freq", "filt_b1", "filt_b2", "filt_b2")], axis=1)
    cols = {
        "cond": np.stack([a["c"][0], a["c_ctx"]], axis=1).reshape(KD, P, 2).transpose(1, 0, 2).reshape(P, 2 * KD),
        "b_ada": columns(a["b_ada"]), "norm1": columns(a["norm1_w"]),
        "hy_conv_w": columns(a["hy_conv_w"]), "hy_conv_b": columns(a["hy_conv_b"]),
        "hy_bias": columns(a["hy_bias"]), "hy_norm": columns(a["hy_norm_w"]),
        "ssd_conv_w": columns(a["ssd_conv_w"]), "ssd_conv_b": columns(a["ssd_conv_b"]),
        "ssd_d": columns(np.repeat(a["ssd_d"][0], HEAD)), "ssd_norm": columns(a["ssd_norm_w"]),
        "norm2": columns(a["norm2_w"]), "final1": columns(a["final_norm_w"]),
        "norm_mix": columns(a["norm_mix_g_2"]), "conv_b": columns(a["conv_b_2"]),
        "ln_g": columns(a["conv_ln_g_2"]), "ln_b": columns(a["conv_ln_b_2"]),
        "grp_conv": columns(a["grp_norm_conv_g_2"]), "grp_ssm": columns(a["grp_norm_ssm_g_2"]),
        "norm_mem": columns(a["norm_mem_g_2"]), "mem_norm": columns(a["mem_norm_g_2"]),
        "norm_ffn": columns(a["norm_ffn_g_2"]), "final2": columns(a["final_norm_g_2"]),
        "ssm_d": columns(a["ssm_d_2"]), "lam_re": state(a["ssm_lam_re_2"][0]),
        "lam_im": state(a["ssm_lam_im_2"][0]), "log_dt": state(np.repeat(a["ssm_log_dt_2"][0], 64)),
        "dt_bias": rows(a["dt_bias"][0]), "a_log": rows(a["a_log"][0]),
        "conv_w": a["conv_w_2"][0].reshape(CONV31, HT, P).transpose(2, 1, 0).reshape(P, -1),
        "filt": filt,
    }
    d["params"] = np.concatenate([cols[n] for n in PARAM_COLS], axis=1)
    second_layout(a, d)
    d = {n: np.ascontiguousarray(v) for n, v in d.items()}
    d.update(shape_constants())
    return d


def kernel(**inputs):
    from concourse import bacc
    from concourse.bass_utils import run_bass_kernel_spmd

    arrays = lay_out(inputs)
    nc = bacc.Bacc("TRN2", target_bir_lowering=False, num_devices=1, dynamic_dma_scratch_size=1024)
    dram = {n: nc.dram_tensor(f"in_{n}", v.shape, mybir.dt.from_np(v.dtype), kind="ExternalInput").ap()
            for n, v in arrays.items()}
    out = nc.dram_tensor("out", (P, KD, T), F32, kind="ExternalOutput").ap()
    two_block_kernel(nc, dram, out)
    r = run_bass_kernel_spmd(nc, [{f"in_{n}": v for n, v in arrays.items()}], core_ids=[0])
    return r.results[0]["out"].transpose(2, 1, 0).reshape(1, T, D)
```

```python
import math
from contextlib import ExitStack

import numpy as np

import concourse.bass as bass
from concourse import mybir

F32 = mybir.dt.float32
F32R = mybir.dt.float32r
U32 = mybir.dt.uint32
ALU = mybir.AluOpType
ACT = mybir.ActivationFunctionType
AX_X = mybir.AxisListType.X

P = 128
T = 256
TT = T // P
D = 2048
KD = D // P
EPS = 1e-6
RING = 4
HALF = 8
SLOTS = 4
QUARTER = 4
BANK = 512

HY = 1024
HT = HY // P
HY_TILES = 3 * HT
XBC_TILES = 12
Z_TILES = 8
GRID = 64
HEADS = 16
HEAD = 64
MLP_TILES = 64
EPS_COL, ZERO_COL, QUARTER_COL = 0, 1, 2

CONV31 = 31
PAIRS = 32
MEM_HEADS = 4
PEER_HEADS = 8
KEYS = 128
TOPK = 16
TWO_PI = 6.283185

PARAM_COLS = dict(
    cond=2 * KD, b_ada=6 * KD, norm1=KD, hy_conv_w=3 * HY_TILES, hy_conv_b=HY_TILES,
    hy_bias=2 * HT, hy_norm=HT, ssd_conv_w=3 * XBC_TILES, ssd_conv_b=XBC_TILES, ssd_d=HT,
    ssd_norm=HT, norm2=KD, final1=KD, norm_mix=KD, conv_b=HT, ln_g=HT, ln_b=HT, grp_conv=HT,
    grp_ssm=HT, norm_mem=KD, mem_norm=KD, norm_ffn=KD, final2=KD, ssm_d=HT, lam_re=PAIRS,
    lam_im=PAIRS, log_dt=PAIRS, dt_bias=2 * HEADS, a_log=2 * HEADS, conv_w=CONV31 * HT,
    filt=4,
)
PARAM_AT, N_PARAM = {}, 0
for _name, _n in PARAM_COLS.items():
    PARAM_AT[_name] = N_PARAM
    N_PARAM += _n

CONST_COLS = dict(ident=P, tri_f=P, tri_b=P, iota=T, group=2, halves=2, fold=2 * HEADS)
CONST_AT, N_CONST = {}, 0
for _name, _n in CONST_COLS.items():
    CONST_AT[_name] = N_CONST
    N_CONST += _n


def spread(ap, axis, n):
    v = ap.unsqueeze(axis)
    shape = list(v.shape)
    shape[axis] = n
    return v.broadcast_to(shape)


class Signal:

    def __init__(self, sem):
        self.sem, self.base = sem, 0


class Chain:

    def __init__(self, sem):
        self.sem, self.n, self.per, self.i = sem, 0, 0, None

    def step(self, eng, ins):
        ins.then_inc(self.sem, 1)
        self.n += 1
        eng.wait_ge(self.sem, self.n if self.i is None else self.i * self.per + self.n)

    def loop(self, i, per, start=None):
        self.n = self.n if start is None else start
        self.i, self.per, self.start = i, per, self.n

    def end(self, iterations):
        assert self.n - self.start == self.per, (self.n - self.start, self.per)
        self.n += self.per * (iterations - 1)
        self.i = None


class Core:

    def __init__(self, nc, ctx, dram):
        self.nc, self.dram, self.ctx = nc, dram, ctx
        self.sb = lambda name, shape, dt=F32: ctx.enter_context(nc.sbuf_tensor(name, shape, dt))
        self.ring = self.sb("ring", [P, RING, HALF, P])
        self.hi = self.sb("weights_hi", [P, SLOTS, QUARTER, P], F32R)
        self.lo = self.sb("weights_lo", [P, SLOTS, QUARTER, P], F32R)
        self.params = self.sb("params", [P, N_PARAM])
        self.consts = self.sb("consts", [P, N_CONST])
        self.ones = self.sb("ones", [P, P])
        self.small = self.sb("small", [P, 4])
        self.mod = self.sb("mod", [P, 6 * KD, 2])
        self.gain = self.sb("gain", [P, 3 * KD])
        self.x = self.sb("x", [P, KD, T])
        self.ps = ctx.enter_context(nc.psum_tensor("ps", [P, 8, BANK], F32))
        self.landed = [self.sem(f"weights_landed{s}") for s in range(RING)]
        self.rounded, self.split, self.multiplied = (self.sem(f"weights_{n}") for n in ("rounded", "split", "multiplied"))
        self.moved, self.summed, self.shaped = (self.sem(f"tile_{n}") for n in ("moved", "summed", "shaped"))
        self.source_rounded, self.source_split = self.sem("source_rounded"), self.sem("source_split")
        self.quarters, self.tiles, self.moves, self.shapes, self.sources = 0, 0, 0, 0, 0
        self.begun = False
        self.norm_signals = [Signal(self.sem(f"norm_{n}")) for n in ("squared", "summed", "rooted", "scaled")]
        self.hyena_signals = {n: self.sem(f"hyena_{n}") for n in ("turned", "token", "spectrum", "product", "result")}
        self.dve = Chain(self.sem("vector_step"))
        self.act = Chain(self.sem("scalar_step"))
        self.pool = Chain(self.sem("gpsimd_step"))
        self.prm = {n: self.params[:, PARAM_AT[n]:PARAM_AT[n] + c] for n, c in PARAM_COLS.items()}
        self.cst = {n: self.consts[:, CONST_AT[n]:CONST_AT[n] + c] for n, c in CONST_COLS.items()}

        self.squares = self.consts[:, CONST_AT["tri_f"]:CONST_AT["tri_f"] + T]

    def sem(self, name):
        return self.ctx.enter_context(self.nc.semaphore(name))

    def block(self, w, n):
        return self.dram[w][n].rearrange("p (k m) -> p k m", k=HALF)


def stream(core, sp, w, count, next_w, first, base):
    rounds = count // RING
    if rounds > 1:
        with sp.Fori(0, rounds - 1) as i:
            for s in range(RING):
                sp.wait_ge(core.split, i * (2 * RING) + (base + 2 * s + 2))
                sp.dma_start(core.ring[:, s], core.block(w, i * RING + (first + RING + s))).then_inc(core.landed[s], 16)
    for s in range(RING):
        sp.wait_ge(core.split, base + 2 * (count - RING + s) + 2)
        if next_w is not None:
            sp.dma_start(core.ring[:, s], core.block(next_w[0], next_w[1] + s)).then_inc(core.landed[s], 16)


def make_hi(core, act, g, i, per, base):
    slot, at = g // 2 % RING, g % 2 * QUARTER
    if g % 2 == 0:
        act.wait_ge(core.landed[slot], i * (2 * per) + 16 * (base // 8 + g // 8 + 1))
    act.wait_ge(core.multiplied, i * per + (base + g + 1))
    act.activation(core.hi[:, g % SLOTS], core.ring[:, slot, at:at + QUARTER], ACT.Copy).then_inc(core.rounded, 1)


def make_lo(core, dve, g, i, per, base):
    slot, at = g // 2 % RING, g % 2 * QUARTER
    dve.wait_ge(core.rounded, i * per + (base + g + 1))
    dve.tensor_tensor(core.lo[:, g % SLOTS], core.ring[:, slot, at:at + QUARTER],
                      core.hi[:, g % SLOTS].bitcast(F32), ALU.subtract).then_inc(core.split, 1)


def begin(core, eng, make, per, base, begun, source=None, quarters=SLOTS):
    for g in range(SLOTS):
        if source is not None and g < quarters:
            source(eng, g)
        if not begun:
            make(core, eng, g, 0, per, base)


def split_and_take(core, eng, make, take, rounds, unroll, quarters, base, follow):
    per = unroll * quarters

    def body(i, last):
        for s in range(unroll):
            for g in range(s * quarters + SLOTS, (s + 1) * quarters + SLOTS):
                if g < per or not last:
                    make(core, eng, g, i, per, base)
                elif follow is not None:
                    follow(g - per)
            take(eng, i * unroll + s, i, s)

    if rounds > 1:
        with eng.Fori(0, rounds - 1) as i:
            body(i, False)
    body(rounds - 1, True)


def first_of_next(core, eng, make, base):
    return lambda g: make(core, eng, g, 0, 2 * SLOTS, base)


def add_squares(core, dve, n, scratch):
    x = core.x[:, n, :]
    core.dve.step(dve, dve.tensor_tensor(scratch, x, x, ALU.mult))
    core.dve.step(dve, dve.tensor_tensor(core.squares, core.squares, scratch, ALU.add))


def rms_stage(core, name, src, dst, tiles, gain, bias=None, squares=None):
    nc, ps = core.nc, core.ps
    squared, summed, rooted, scaled = core.norm_signals
    with ExitStack() as own:
        sq = own.enter_context(nc.sbuf_tensor(f"{name}_sq", [P, tiles, T], F32)) if squares is None else None
        std = own.enter_context(nc.sbuf_tensor(f"{name}_std", [P, T], F32))
        rstd = own.enter_context(nc.sbuf_tensor(f"{name}_rstd", [P, T], F32))
        group = tiles // 4
        with nc.Block() as block:
            @block.scalar
            def _(act):
                for g in range(4 if squares is None else 0):
                    at = slice(g * group, (g + 1) * group)
                    act.activation(sq[:, at, :], src[:, at, :], ACT.Square).then_inc(squared.sem, 1)
                act.wait_ge(summed.sem, summed.base + 1)
                act.activation(std[:], ps[:, 0, 0:T], ACT.Sqrt, bias=core.small[:, EPS_COL:EPS_COL + 1],
                               scale=1.0 / (tiles * P)).then_inc(rooted.sem, 1)
                if bias is not None:
                    for t in range(tiles):
                        act.wait_ge(scaled.sem, scaled.base + t + 1)
                        act.activation(dst[:, t, :], dst[:, t, :], ACT.Identity, bias=bias[:, t:t + 1])

            @block.tensor
            def _(pe):
                if squares is not None:
                    mm = pe.matmul(ps[:, 0, 0:T], core.ones[:], squares, start=True, stop=True)
                for t in range(tiles if squares is None else 0):
                    if t % group == 0:
                        pe.wait_ge(squared.sem, squared.base + t // group + 1)
                    mm = pe.matmul(ps[:, 0, 0:T], core.ones[:], sq[:, t, :], start=t == 0, stop=t == tiles - 1)
                mm.then_inc(summed.sem, 1)

            @block.vector
            def _(dve):
                dve.wait_ge(rooted.sem, rooted.base + 1)
                core.dve.step(dve, dve.reciprocal(rstd[:], std[:]))
                for t in range(tiles):
                    dve.scalar_tensor_tensor(dst[:, t, :], src[:, t, :], gain[:, t:t + 1], rstd[:],
                                             ALU.mult, ALU.mult).then_inc(scaled.sem, 1)
    for signal, n in ((squared, 4 if squares is None else 0), (summed, 1), (rooted, 1), (scaled, tiles)):
        signal.base += n


def start_stage(core, ctx_tile, const_loads, scratch, squares):
    nc, ps, dram = core.nc, core.ps, core.dram
    loaded, made, split_c, ready = (core.sem(n) for n in ("inputs_loaded", "silu_made", "silu_split", "silu_ready"))
    tables = core.sem("tables_loaded")
    blocks = 6 * D // BANK
    turned = core.sem("mod_turned")
    with ExitStack() as own:
        silu_c = own.enter_context(nc.sbuf_tensor("silu_c", [P, KD, 2], F32))
        zeros = own.enter_context(nc.sbuf_tensor("zeros", [P, KD, P], F32))
        c4 = own.enter_context(nc.sbuf_tensor("silu_parts", [P, KD, P], F32R))
        rows = own.enter_context(nc.sbuf_tensor("mod_rows", [4, 2, BANK], F32))
        block = own.enter_context(nc.Block())
        mod_sums = ps[:, 4, 0:12 * KD].rearrange("p (n c) -> p n c", c=2)
        rounds = blocks // 2

        @block.sync
        def _(sp):
            sp.dma_start(core.params[:], dram["params"]).then_inc(loaded, 16)
            for s in range(RING):
                sp.dma_start(core.ring[:, s], core.block("w_ada", s)).then_inc(core.landed[s], 16)
            stream(core, sp, "w_ada", blocks * HALF, ("w_mix", 0), 0, 0)

        @block.scalar
        def _(act):
            act.wait_ge(loaded, 16)
            act.activation(silu_c[:], core.prm["cond"].rearrange("p (k c) -> p k c", c=2), ACT.Silu).then_inc(made, 1)
            act.wait_ge(split_c, 1)
            act.wait_ge(made, 1)
            act.activation(c4[:, :, 0:2], silu_c[:], ACT.Copy).then_inc(made, 1)
            begin(core, act, make_hi, 2 * KD, 0, False)
            split_and_take(core, act, make_hi, lambda act, n, i, s: None, rounds, 2, KD, 0,
                           first_of_next(core, act, make_hi, blocks * KD))

        @block.gpsimd
        def _(pool):
            pool.dma_start(core.consts[:], dram["consts"]).then_inc(tables, 16)
            pool.dma_start(core.x[:], dram["x"]).then_inc(tables, 16)
            pool.dma_start(ctx_tile[:], dram["ctx"]).then_inc(tables, 16)
            for tile, name in const_loads:
                pool.dma_start(tile, dram[name]).then_inc(tables, 16)
            pool.wait_ge(tables, 16 * (3 + len(const_loads)))
            step = lambda ins: core.pool.step(pool, ins)
            for j, src in enumerate((core.x, ctx_tile)):
                step(pool.tensor_tensor(scratch[:, 0:KD, :], src[:], src[:], ALU.mult))
                half = KD // 2
                while half:
                    out = scratch[:, 0:half, :] if half > 1 else squares[:, j:j + 1, :]
                    step(pool.tensor_tensor(out, scratch[:, 0:half, :], scratch[:, half:2 * half, :], ALU.add))
                    half //= 2

        @block.vector
        def _(dve):
            dve.sem_inc(core.multiplied, SLOTS)
            dve.sem_inc(core.summed, 2)
            dve.memset(core.ones[:], 1.0)
            for col, value in ((EPS_COL, EPS), (ZERO_COL, 0.0), (QUARTER_COL, 0.25)):
                dve.memset(core.small[:, col:col + 1], value)
            core.dve.step(dve, dve.memset(zeros[:], 0.0))
            dve.tensor_copy(c4[:], zeros[:]).then_inc(split_c, 1)
            dve.wait_ge(made, 2)
            dve.tensor_tensor(c4[:, :, 2:4], silu_c[:], c4[:, :, 0:2].bitcast(F32), ALU.subtract).then_inc(ready, 1)

            def take(dve, n, i, s):
                dve.wait_ge(core.multiplied, i * (2 * KD) + (SLOTS + (s + 1) * KD))
                dve.tensor_copy(rows[:, s], ps[0:4, s, :]).then_inc(core.summed, 1)

            begin(core, dve, make_lo, 2 * KD, 0, False)
            split_and_take(core, dve, make_lo, take, rounds, 2, KD, 0,
                           first_of_next(core, dve, make_lo, blocks * KD))
            dve.wait_ge(turned, blocks)
            core.dve.step(dve, dve.tensor_tensor(core.mod[:], mod_sums, spread(core.prm["b_ada"], 2, 2), ALU.add))
            for n, (norm, part, who) in enumerate((("norm1", 1, 0), ("norm1", 1, 1), ("norm2", 4, 0))):
                dve.scalar_tensor_tensor(core.gain[:, n * KD:(n + 1) * KD], core.mod[:, part * KD:(part + 1) * KD, who],
                                         1.0, core.prm[norm], ALU.add, ALU.mult)

        @block.tensor
        def _(pe):
            def multiply(i, b, ks):
                for k in ks:
                    pe.wait_ge(core.split, i * (2 * KD) + (b * KD + k + 1))
                    for m, w in enumerate((core.hi, core.lo)):
                        mm = pe.matmul(ps[:, b % 2, :], c4[:, k, :], w[:, k % SLOTS].rearrange("p k m -> p (k m)"),
                                       start=(m, k) == (0, 0), stop=(m, k) == (1, KD - 1))
                    mm.then_inc(core.multiplied, 1)

            def turn(i, b):
                pe.wait_ge(core.summed, i * 2 + (b + 3))
                for j in range(BANK // P):
                    mm = pe.matmul(mod_sums[:, i * 8 + (b * 4 + j), :], rows[:, b % 2, j * P:(j + 1) * P],
                                   core.cst["halves"][0:4, :], start=True, stop=True)
                mm.then_inc(turned, 1)

            first, rest = range(KD // 2), range(KD // 2, KD)
            pe.wait_ge(ready, 1)
            multiply(0, 0, range(KD))
            pe.wait_ge(tables, 16 * (3 + len(const_loads)))
            with pe.Fori(0, rounds - 1) as i:
                for b in range(2):
                    multiply(i, b + 1, first)
                    turn(i, b)
                    multiply(i, b + 1, rest)
            multiply(rounds - 1, 1, first)
            turn(rounds - 1, 0)
            multiply(rounds - 1, 1, rest)
            turn(rounds - 1, 1)
    core.quarters += blocks * KD
    core.tiles += blocks
    core.begun = True


def split_stage(core, src, dst, tiles):
    nc, group = core.nc, 4
    base = core.shapes
    with nc.Block() as block:
        @block.scalar
        def _(act):
            for t in range(0, tiles, group):
                act.activation(dst[:, t:t + group, 0, :], src[:, t:t + group, :], ACT.Copy).then_inc(core.shaped, 1)

        @block.vector
        def _(dve):
            for t in range(0, tiles, group):
                dve.wait_ge(core.shaped, base + t // group + 1)
                dve.tensor_tensor(dst[:, t:t + group, 1, :], src[:, t:t + group, :],
                                  dst[:, t:t + group, 0, :].bitcast(F32), ALU.subtract)
    core.shapes += tiles // group


class Layer:

    def __init__(self, w, tiles, rhs, into=None, shape=None, finish=None, first=0, quarters=4, source=None, steps=0,
                 squares=False):
        self.squares = squares
        self.w, self.tiles, self.rhs, self.into, self.shape, self.finish = w, tiles, rhs, into, shape, finish
        self.first, self.quarters, self.source, self.steps = first, quarters, source, steps
        self.unroll = 2 * SLOTS // quarters
        self.rounds, self.per = tiles // self.unroll, 2 * SLOTS


def linear_stage(core, name, layers, next_w, loads=(), begin_next=True):
    nc, ps = core.nc, core.ps
    loaded = core.sem(f"{name}_loaded") if loads else None
    squares = any(layer.squares for layer in layers)
    begun, begin_next = core.begun, begin_next and next_w is not None
    for layer in layers:
        layer.Q, layer.N, layer.M, layer.S, layer.A = core.quarters, core.tiles, core.moves, core.shapes, core.sources
        core.quarters += layer.tiles * layer.quarters
        core.tiles += layer.tiles
        core.moves += layer.tiles
        core.shapes += layer.tiles if layer.shape is not None else 0
        core.sources += layer.quarters if layer.source is not None else 0
    with ExitStack() as own:
        width = max([len(layer.rhs) for layer in layers if layer.into is None], default=0)
        sums = own.enter_context(nc.sbuf_tensor(f"{name}_sums", [P, 2, width, T], F32)) if width else None
        block = own.enter_context(nc.Block())

        def slots(layer, n, s):
            if layer.into is not None:
                return [layer.into(n)]
            return [sums[:, s % 2, j, :] for j in range(len(layer.rhs))]

        def run(eng, make, source_of, take_of):
            starts = [source_of(layer) for layer in layers]
            begin(core, eng, make, layers[0].per, layers[0].Q, begun, starts[0], layers[0].quarters)
            for layer, after, start in zip(layers, layers[1:] + [None], starts[1:] + [None]):
                def follow(g):
                    if start is not None and g < after.quarters:
                        start(eng, g)
                    make(core, eng, g, 0, after.per, after.Q)
                if after is None:
                    follow = first_of_next(core, eng, make, core.quarters) if begin_next else None
                split_and_take(core, eng, make, take_of(layer), layer.rounds, layer.unroll, layer.quarters, layer.Q,
                               follow)
                if layer.steps and make is make_lo:
                    core.dve.end(layer.rounds)

        @block.sync
        def _(sp):
            for tile, source in loads:
                sp.dma_start(tile, core.dram[source]).then_inc(loaded, 16)
            for layer, after in zip(layers, layers[1:] + [None]):
                stream(core, sp, layer.w, layer.tiles * layer.quarters // 2,
                       next_w if after is None else (after.w, after.first), layer.first, layer.Q)
            if loads:
                sp.wait_ge(loaded, 16 * len(loads))

        @block.scalar
        def _(act):
            def source_of(layer):
                def source(act, q):
                    act.wait_ge(core.multiplied, layer.Q + q + 1)
                    at = slice(q * QUARTER, (q + 1) * QUARTER)
                    act.activation(layer.rhs[0][:, at, 0, :], layer.source[:, at, :], ACT.Copy).then_inc(core.source_rounded, 1)
                return source if layer.source is not None else None

            def take_of(layer):
                def take(act, n, i, s):
                    act.wait_ge(core.multiplied, i * layer.per + (layer.Q + SLOTS + (s + 1) * layer.quarters))
                    for j, slot in enumerate(slots(layer, n, s)):
                        ins = act.activation(slot, ps[:, s % 2 + 2 * j, T:2 * T], ACT.Copy)
                    ins.then_inc(core.moved, 1)
                    if layer.shape is not None:
                        act.wait_ge(core.summed, i * layer.unroll + (layer.N + s + 3))
                        layer.shape(act, n, slots(layer, n, s)).then_inc(core.shaped, 1)
                return take
            run(act, make_hi, source_of, take_of)

        @block.vector
        def _(dve):
            if squares:
                core.dve.step(dve, dve.memset(core.squares, 0.0))

            def source_of(layer):
                def source(dve, q):
                    dve.wait_ge(core.source_rounded, layer.A + q + 1)
                    r, at = layer.rhs[0], slice(q * QUARTER, (q + 1) * QUARTER)
                    dve.tensor_tensor(r[:, at, 1, :], layer.source[:, at, :], r[:, at, 0, :].bitcast(F32),
                                      ALU.subtract).then_inc(core.source_split, 1)
                return source if layer.source is not None else None

            def take_of(layer):
                chained = core.dve.n

                def take(dve, n, i, s):
                    if s == 0 and layer.steps:
                        core.dve.loop(i, layer.steps * layer.unroll, chained)
                    dve.wait_ge(core.moved, i * layer.unroll + (layer.M + s + 1))
                    for j, slot in enumerate(slots(layer, n, s)):
                        ins = dve.tensor_tensor(slot, slot, ps[:, s % 2 + 2 * j, 0:T], ALU.add)
                    ins.then_inc(core.summed, 1)
                    if layer.shape is not None:
                        dve.wait_ge(core.shaped, i * layer.unroll + (layer.S + s + 1))
                    elif layer.finish is not None:
                        dve.wait_ge(core.summed, i * layer.unroll + (layer.N + s + 3))
                    if layer.finish is not None:
                        layer.finish(dve, n, slots(layer, n, s))
                return take
            run(dve, make_lo, source_of, take_of)

        def products(pe, layer, i, s, q):
            g = s * layer.quarters + q
            if layer.source is not None and s == 0:
                pe.wait_ge(core.source_split, layer.A + q + 1)
            pe.wait_ge(core.split, i * layer.per + (layer.Q + g + 1))
            for k in range(QUARTER):
                at, last = q * QUARTER + k, (q, k) == (layer.quarters - 1, QUARTER - 1)
                for part in ((core.lo, core.hi) if last else (core.hi, core.lo)):
                    for j, r in enumerate(layer.rhs):
                        if part is core.hi:
                            out, moving = ps[:, s % 2 + 2 * j, :], r[:, at].rearrange("p a t -> p (a t)")
                        else:
                            out, moving = ps[:, s % 2 + 2 * j, 0:T], r[:, at, 0, :]
                        mm = pe.matmul(out, part[:, g % SLOTS, k, :], moving,
                                       start=at == 0 and part is core.hi, stop=last and part is core.hi)
            mm.then_inc(core.multiplied, 1)

        @block.tensor
        def _(pe):
            for layer in layers:
                with pe.Fori(0, layer.rounds) as i:
                    for s in range(layer.unroll):
                        pe.wait_ge(core.summed, i * layer.unroll + (layer.N + s + 1))
                        for q in range(layer.quarters):
                            products(pe, layer, i, s, q)
    core.begun = begin_next


def conv3_layer(core, w, tiles, rhs, first, dests, taps, bias, rows, source=None):
    def centre(act, n, slots):
        for dst, u in zip(dests, slots):
            ins = act.activation(dst[:, n, :], u, ACT.Identity, bias=bias[:, bass.ds(n, 1)],
                                 scale=taps[:, bass.ds(n + tiles, 1)])
        return ins

    def neighbours(dve, n, slots):
        for dst, slot, g in zip(dests, slots, rows):
            u = slot.rearrange("p (r t) -> p r t", t=g)
            y = dst[:, n, :].rearrange("p (r t) -> p r t", t=g)
            core.dve.step(dve, dve.scalar_tensor_tensor(
                y[:, :, 1:g], u[:, :, 0:g - 1], taps[:, bass.ds(n, 1)], y[:, :, 1:g], ALU.mult, ALU.add))
            dve.scalar_tensor_tensor(
                y[:, :, 0:g - 1], u[:, :, 1:g], taps[:, bass.ds(n + 2 * tiles, 1)], y[:, :, 0:g - 1],
                ALU.mult, ALU.add)

    return Layer(w, tiles, rhs, shape=centre, finish=neighbours, first=first * 2, source=source, steps=len(rhs))


def dt_stage(core, wdt, h_parts, ctx_parts, ssd, xbc, xbc_ctx):
    nc, ps = core.nc, core.ps
    names = ("rounded", "split", "products", "rows", "sums", "abs", "exp", "grown", "log", "a", "da", "cum", "to_end")
    s = {n: core.sem(f"dt_{n}") for n in names}
    H2 = 2 * HEADS
    with ExitStack() as own:
        sb = lambda name: own.enter_context(nc.sbuf_tensor(f"dt_{name}", [P, 4, H2], F32))
        v, e, u, lnu, zero, den, rest = (sb(n) for n in ("v", "e", "u", "lnu", "zero", "den", "rest"))
        av = sb("av")
        a_row = own.enter_context(nc.sbuf_tensor("a_row", [P, H2], F32))
        w = own.enter_context(nc.sbuf_tensor("wdt_parts", [P, KD, 4, H2], F32R))
        rows = own.enter_context(nc.sbuf_tensor("dt_rows", [2 * H2, 2, 2, T], F32))
        with nc.Block() as block:
            @block.tensor
            def _(pe):
                pe.wait_ge(s["split"], 1)
                for j, src in enumerate((h_parts, ctx_parts)):
                    for k in range(KD):
                        mm = pe.matmul(ps[:, 3 + j, :], w[:, k].rearrange("p a h -> p (a h)"),
                                       src[:, k].rearrange("p a t -> p (a t)"), start=k == 0, stop=k == KD - 1)
                    mm.then_inc(s["products"], 1)
                for q in range(4):
                    at = slice((q % 2) * P, (q % 2 + 1) * P)
                    pe.wait_ge(s["rows"], q // 2 + 1)
                    for part in range(2):
                        mm = pe.matmul(ps[:, 0, q * H2:(q + 1) * H2], rows[:, q // 2, part, at],
                                       core.cst["fold"][0:2 * H2, :], start=part == 0, stop=part == 1)
                mm.then_inc(s["sums"], 1)
                pe.wait_ge(s["da"], 1)
                for q in range(4):
                    for d, tri in enumerate(("tri_f", "tri_b")):
                        at = slice(d * HEADS, (d + 1) * HEADS)
                        pe.matmul(ps[:, 1, q * H2 + d * HEADS:q * H2 + (d + 1) * HEADS], core.cst[tri],
                                  ssd.da[:, q, at], start=True, stop=True)
                mm = pe.matmul(ps[:, 2, 0:4 * H2], core.ones[:], ssd.da[:], start=True, stop=True)
                mm.then_inc(s["cum"], 1)

            @block.scalar
            def _(act):
                act.activation(w[:, :, 0, :], wdt[:], ACT.Copy).then_inc(s["rounded"], 1)
                act.activation(w[:, :, 2:4, :], spread(wdt[:], 2, 2), ACT.Copy).then_inc(s["rounded"], 1)
                act.activation(xbc[:], xbc[:], ACT.Silu)
                act.activation(xbc_ctx[:], xbc_ctx[:], ACT.Silu)
                act.activation(a_row[:], core.prm["a_log"], ACT.Exp).then_inc(s["a"], 1)
                act.wait_ge(s["abs"], 1)
                act.activation(e[:], av[:], ACT.Exp, scale=-1.0).then_inc(s["exp"], 1)
                act.wait_ge(s["grown"], 1)
                act.activation(lnu[:], u[:], ACT.Ln).then_inc(s["log"], 1)
                act.wait_ge(s["to_end"], 1)
                act.activation(ssd.etot[:], ps[:, 2, 0:4 * H2].rearrange("p (q h) -> p q h", q=4), ACT.Exp)
                act.activation(ssd.to_end[:], ssd.to_end[:], ACT.Exp)

            @block.vector
            def _(dve):
                step = lambda ins: core.dve.step(dve, ins)
                dve.wait_ge(s["rounded"], 2)
                dve.tensor_tensor(w[:, :, 1, :], wdt[:], w[:, :, 0, :].bitcast(F32), ALU.subtract).then_inc(s["split"], 1)
                for j in range(2):
                    dve.wait_ge(s["products"], j + 1)
                    dve.tensor_copy(rows[:, j], ps[0:2 * H2, 3 + j, :].rearrange("p (a t) -> p a t", a=2)).then_inc(s["rows"], 1)
                dve.wait_ge(s["sums"], 1)
                step(dve.tensor_tensor(v[:], ps[:, 0, 0:4 * H2].rearrange("p (q h) -> p q h", q=4),
                                       spread(core.prm["dt_bias"], 1, 4), ALU.add))
                step(dve.tensor_scalar(rest[:], v[:], -1.0, None, ALU.mult))
                dve.tensor_tensor(av[:], v[:], rest[:], ALU.max).then_inc(s["abs"], 1)
                dve.wait_ge(s["exp"], 1)
                dve.tensor_scalar(u[:], e[:], 1.0, None, ALU.add).then_inc(s["grown"], 1)
                dve.wait_ge(s["grown"], 1)
                step(dve.tensor_scalar(den[:], u[:], -1.0, None, ALU.add))
                step(dve.tensor_scalar(zero[:], den[:], 0.0, None, ALU.is_equal))
                step(dve.tensor_tensor(den[:], den[:], zero[:], ALU.add))
                step(dve.reciprocal(den[:], den[:]))
                dve.wait_ge(s["log"], 1)
                step(dve.tensor_tensor(den[:], den[:], lnu[:], ALU.mult))
                step(dve.tensor_tensor(den[:], den[:], zero[:], ALU.add))
                step(dve.tensor_tensor(den[:], den[:], e[:], ALU.mult))
                step(dve.scalar_tensor_tensor(ssd.dt[:], v[:], 0.0, den[:], ALU.max, ALU.add))
                dve.wait_ge(s["a"], 1)
                dve.scalar_tensor_tensor(ssd.da[:], ssd.dt[:], -1.0, spread(a_row[:], 1, 4),
                                         ALU.mult, ALU.mult).then_inc(s["da"], 1)
                dve.wait_ge(s["cum"], 1)
                step(dve.tensor_copy(ssd.cum[:], ps[:, 1, 0:4 * H2].rearrange("p (q h) -> p q h", q=4)))
                dve.tensor_tensor(ssd.to_end[:], ps[:, 2, 0:4 * H2].rearrange("p (q h) -> p q h", q=4),
                                  ssd.cum[:], ALU.subtract).then_inc(s["to_end"], 1)


def sine_steps(core, dve, x, k, bound_done):
    magic = 12582912.0
    c1, c2 = 6.28125, 2 * math.pi - 6.28125
    step = lambda ins: core.dve.step(dve, ins)
    step(dve.tensor_scalar(k, x, 1 / (2 * math.pi), magic, ALU.mult, ALU.add))
    step(dve.tensor_scalar(k, k, -magic, None, ALU.add))
    step(dve.scalar_tensor_tensor(x, k, -c1, x, ALU.mult, ALU.add))
    step(dve.scalar_tensor_tensor(x, k, -c2, x, ALU.mult, ALU.add))
    dve.tensor_scalar(x, x, 3.1415925, -3.1415925, ALU.min, ALU.max).then_inc(bound_done, 1)


COS0, COS1, COS_N, SIN_N, SIN0, SIN1 = range(6)
KA0, KA1, KN0, KN1, KB0, KB1 = range(6)


def filter_stage(core, dft, filters):
    nc, ps, dram = core.nc, core.ps, core.dram
    names = ("in", "fw3", "window", "arg", "bounded", "sine", "taps", "tapped", "abs", "abs_sum", "norm", "even_odd",
             "spectrum", "stored")
    s = {n: core.sem(f"filt_{n}") for n in names}
    with ExitStack() as own:
        sb = lambda name, shape: own.enter_context(nc.sbuf_tensor(f"filt_{name}", shape, F32))
        fw1, fw2, hdn = sb("w1", [33, 64]), sb("w2", [64, 64]), sb("hdn", [64, T])
        fw3, window = sb("w3", [64, 2, HY]), sb("window", [P, TT, HY])
        tmp, norm = sb("tmp", [P, 4, BANK]), sb("norm", [P, HY])
        h = sb("taps", [P, TT, 2, HY])
        x, k, feats = tmp[0:64, 0, 0:T], tmp[0:64, 0, T:2 * T], tmp[0:33, 1, 0:T]
        even = lambda o: filters[:, o, KB0:KB1 + 1, :]
        freq, b1, b2 = (core.prm["filt"][0:64, n:n + 1] for n in range(3))
        with nc.Block() as block:
            @block.sync
            def _(sp):
                sp.dma_start(feats, dram["feats"]).then_inc(s["in"], 16)
                sp.dma_start(fw1[:], dram["filt_w1"]).then_inc(s["in"], 16)
                sp.dma_start(fw2[:], dram["filt_w2"]).then_inc(s["in"], 16)
                w3 = dram["filt_w3"].rearrange("k (o a c) -> k o a c", o=2, a=2)
                sp.dma_start(fw3[:], w3[:, 0]).then_inc(s["fw3"], 16)
                sp.dma_start(window[:], dram["window"]).then_inc(s["window"], 16)
                sp.wait_ge(s["taps"], 1)
                sp.dma_start(fw3[:], w3[:, 1]).then_inc(s["fw3"], 16)

            @block.tensor
            def _(pe):
                pe.wait_ge(s["in"], 48)
                pe.matmul(ps[0:64, 0, 0:T], fw1[:], feats, start=True, stop=True).then_inc(s["arg"], 1)
                pe.wait_ge(s["sine"], 1)
                pe.matmul(ps[0:64, 0, 0:T], fw2[:], hdn[:], start=True, stop=True).then_inc(s["arg"], 1)
                pe.wait_ge(s["sine"], 2)
                for o in range(2):
                    pe.wait_ge(s["fw3"], 16 * (o + 1))
                    if o:
                        pe.wait_ge(s["stored"], 10)
                    for b in range(8):
                        t, a, c = b // 4, b // 2 % 2, b % 2
                        mm = pe.matmul(ps[:, b, :], hdn[:, t * P:(t + 1) * P], fw3[:, a, c * BANK:(c + 1) * BANK],
                                       start=True, stop=True)
                    mm.then_inc(s["taps"], 1)
                    pe.wait_ge(s["tapped"], o + 1)
                    for c in range(2):
                        pe.wait_ge(s["abs"], 2 * o + c + 1)
                        for j in range(4):
                            mm = pe.matmul(ps[:, c, :], core.ones[:], tmp[:, j, :], start=j == 0, stop=j == 3)
                        mm.then_inc(s["abs_sum"], 1)
                    for n, (mat, taps) in enumerate(((COS0, even(o)), (COS1, even(o)), (COS_N, even(o)),
                                                     (SIN0, h[:, :, 1, :]), (SIN1, h[:, :, 1, :]))):
                        pe.wait_ge(s["even_odd"], 2 * o + (1 if n < 3 else 2))
                        for c in range(2):
                            m = 2 * n + c
                            if m >= 4:
                                pe.wait_ge(s["stored"], 10 * o + m - 3)
                            for t in range(TT):
                                mm = pe.matmul(ps[:, 4 + m % 4, :], dft[:, t, mat, :],
                                               taps[:, t, c * BANK:(c + 1) * BANK], start=t == 0, stop=t == TT - 1)
                            mm.then_inc(s["spectrum"], 1)

            @block.scalar
            def _(act):
                for n in range(2):
                    act.wait_ge(s["bounded"], n + 1)
                    act.activation(hdn[:], x, ACT.Sin).then_inc(s["sine"], 1)
                for o in range(2):
                    act.wait_ge(s["tapped"], o + 1)
                    for c in range(2):
                        if o or c:
                            act.wait_ge(s["abs_sum"], 2 * o + c)
                        act.activation(tmp[:], h[:, :, :, c * BANK:(c + 1) * BANK].rearrange("p a b c -> p (a b) c"),
                                       ACT.Abs).then_inc(s["abs"], 1)
                    act.wait_ge(s["stored"], 10 * o + 4)
                    act.activation(filters[:, o, KN1, :], filters[:, o, KA1, :], ACT.Copy)

            @block.vector
            def _(dve):
                step = lambda ins: core.dve.step(dve, ins)
                for n, bias in enumerate((b1, b2)):
                    dve.wait_ge(s["arg"], n + 1)
                    if n:
                        dve.wait_ge(s["sine"], n)
                    step(dve.tensor_scalar(x, ps[0:64, 0, 0:T], bias, freq, ALU.add, ALU.mult))
                    sine_steps(core, dve, x, k, s["bounded"])
                for o in range(2):
                    dve.wait_ge(s["taps"], o + 1)
                    dve.wait_ge(s["window"], 16)
                    if o:
                        dve.wait_ge(s["spectrum"], 10)
                    for b in range(8):
                        t, a, c = b // 4, b // 2 % 2, b % 2
                        at = slice(c * BANK, (c + 1) * BANK)
                        ins = dve.tensor_tensor(h[:, t, a, at], ps[:, b, :], window[:, t, at], ALU.mult)
                    step(ins)
                    dve.memset(h[0:1, 0, 1, :], 0.0).then_inc(s["tapped"], 1)
                    dve.wait_ge(s["tapped"], o + 1)
                    dve.tensor_tensor(even(o), h[:, :, 0, :], h[:, :, 1, :], ALU.add).then_inc(s["even_odd"], 1)
                    dve.wait_ge(s["abs"], 2 * o + 2)
                    dve.tensor_tensor(h[:, :, 1, :], h[:, :, 0, :], h[:, :, 1, :], ALU.subtract).then_inc(s["even_odd"], 1)
                    for c in range(2):
                        at = slice(c * BANK, (c + 1) * BANK)
                        dve.wait_ge(s["abs_sum"], 2 * o + c + 1)
                        step(dve.tensor_scalar(norm[:, at], ps[:, c, :], EPS, None, ALU.add))
                        step(dve.reciprocal(norm[:, at], norm[:, at]))
                    for n, part in enumerate((KA0, KA1, KN0, KB0, KB1)):
                        for c in range(2):
                            m = 2 * n + c
                            at = slice(c * BANK, (c + 1) * BANK)
                            dve.wait_ge(s["spectrum"], 10 * o + m + 1)
                            dve.tensor_tensor(filters[:, o, part, at], ps[:, 4 + m % 4, :], norm[:, at],
                                              ALU.mult).then_inc(s["stored"], 1)


def hyena_stage(core, o, u, dft, inverse, filters):
    nc, ps = core.nc, core.ps
    per = {"turned": 4, "token": 4, "spectrum": 2, "product": 12, "result": 2}
    s = core.hyena_signals
    after = {n: o * c for n, c in per.items()}
    with ExitStack() as own:
        sb = lambda name, shape: own.enter_context(nc.sbuf_tensor(f"hy{o}_{name}", shape, F32))
        z, y = sb("z", [P, TT, HY]), sb("y", [P, 4, BANK])
        t1, t2 = sb("t1", [P, 2, BANK]), sb("t2", [P, 2, BANK])
        with nc.Block() as block:
            @block.tensor
            def _(pe):
                for b in range(4):
                    t, c = b // 2, b % 2
                    for j in range(4):
                        mm = pe.transpose(ps[:, b, j * P:(j + 1) * P], u[:, 4 * c + j, t * P:(t + 1) * P],
                                          core.cst["ident"])
                    mm.then_inc(s["turned"], 1)
                pe.wait_ge(s["token"], after["token"] + 4)
                for c in range(2):
                    if c:
                        pe.wait_ge(s["product"], after["product"] + 6)
                    for b, mat in enumerate((COS0, COS1, SIN_N, SIN1)):
                        for t in range(TT):
                            mm = pe.matmul(ps[:, 4 + b, :], dft[:, t, mat, :], z[:, t, c * BANK:(c + 1) * BANK],
                                           start=t == 0, stop=t == TT - 1)
                    mm.then_inc(s["spectrum"], 1)
                    pe.wait_ge(s["product"], after["product"] + 6 * c + 6)
                    for j in range(4):
                        for f in range(4):
                            mm = pe.matmul(ps[:, 2 * c + j // 2, (j % 2) * T:(j % 2 + 1) * T],
                                           y[:, f, j * P:(j + 1) * P], inverse[:, f, :], start=f == 0, stop=f == 3)
                    mm.then_inc(s["result"], 1)

            @block.scalar
            def _(act):
                for b in range(4):
                    t, c = b // 2, b % 2
                    act.wait_ge(s["turned"], after["turned"] + b + 1)
                    act.activation(z[:, t, c * BANK:(c + 1) * BANK], ps[:, b, :], ACT.Copy).then_inc(s["token"], 1)

            @block.vector
            def _(dve):
                step = lambda ins: core.dve.step(dve, ins)
                za, zb = ps[:, 4:6, :], ps[:, 6:8, :]

                def gate(c):
                    dve.wait_ge(s["result"], after["result"] + c + 1)
                    for j in range(4):
                        n = 4 * c + j
                        bank = ps[:, 2 * c + j // 2, (j % 2) * T:(j % 2 + 1) * T]
                        step(dve.scalar_tensor_tensor(u[:, n, :], u[:, n, :],
                                                      core.prm["hy_bias"][:, o * HT + n:o * HT + n + 1], bank,
                                                      ALU.mult, ALU.add))
                    at = slice(4 * c, 4 * c + 4)
                    gates = slice((o + 1) * HT + 4 * c, (o + 1) * HT + 4 * c + 4)
                    step(dve.tensor_tensor(u[:, at, :], u[:, at, :], u[:, gates, :], ALU.mult))

                for c in range(2):
                    at = slice(c * BANK, (c + 1) * BANK)
                    dve.wait_ge(s["spectrum"], after["spectrum"] + c + 1)
                    if c:
                        dve.wait_ge(s["result"], after["result"] + 1)
                    k = lambda n: filters[:, o, n:n + 2, at]
                    dve.tensor_tensor(t1[:], za, k(KA0), ALU.mult).then_inc(s["product"], 1)
                    dve.tensor_tensor(t2[:], zb, k(KB0), ALU.mult).then_inc(s["product"], 1)
                    dve.wait_ge(s["product"], after["product"] + 6 * c + 2)
                    dve.tensor_tensor(y[:, 0:2, :], t1[:], t2[:], ALU.subtract).then_inc(s["product"], 1)
                    dve.wait_ge(s["product"], after["product"] + 6 * c + 3)
                    dve.tensor_tensor(t1[:], za, k(KB0), ALU.mult).then_inc(s["product"], 1)
                    dve.tensor_tensor(t2[:], zb, k(KN0), ALU.mult).then_inc(s["product"], 1)
                    dve.wait_ge(s["product"], after["product"] + 6 * c + 5)
                    dve.tensor_tensor(y[:, 2:4, :], t1[:], t2[:], ALU.add).then_inc(s["product"], 1)
                gate(0)
                gate(1)


def ssd_state_stage(core, ssd, xbc, xbc_ctx):
    nc, ps = core.nc, core.ps
    F, B = 0, 1
    s = {n: core.sem(f"state_{n}") for n in ("turned", "token", "xdt", "weighted", "sum", "taken")}
    NX = HEADS * HEAD
    jobs = [(2, F), (3, F), (3, B), (2, B), (0, F), (1, B)]
    extra = [(0, B), (1, F)]
    with ExitStack() as own:
        sb = lambda name, shape: own.enter_context(nc.sbuf_tensor(f"st_{name}", shape, F32))
        tok = sb("tok", [P, 4, NX + 2 * P])
        ctx_xdt, xw = sb("ctx_xdt", [P, HEADS, HEAD]), sb("xw", [P, 2, HEADS, HEAD])
        with nc.Block() as block:
            tiles = [(0, 4), (4, 4), (8, 2)]

            @block.tensor
            def _(pe):
                n = 0
                for q in (2, 3, 0, 1):
                    src = xbc if q < 2 else xbc_ctx
                    at = slice((q % 2) * P, (q % 2 + 1) * P)
                    for first, count in tiles:
                        if n >= 4:
                            pe.wait_ge(s["token"], n - 3)
                        for j in range(count):
                            mm = pe.transpose(ps[:, n % 4, j * P:(j + 1) * P], src[:, first + j, at], core.cst["ident"])
                        mm.then_inc(s["turned"], 1)
                        n += 1
                for j, (q, d) in enumerate(jobs):
                    pe.wait_ge(s["weighted"], j + 1)
                    if j >= 2:
                        pe.wait_ge(s["taken"], j - 1)
                    if j == 0:
                        pe.wait_ge(s["token"], 12)
                    for g in range(2):
                        mm = pe.matmul(ps[:, 4 + 2 * (j % 2) + g, :], tok[:, q, NX + g * P:NX + (g + 1) * P],
                                       xw[:, j % 2, 8 * g:8 * g + 8, :].rearrange("p h e -> p (h e)"),
                                       start=True, stop=True)
                    mm.then_inc(s["sum"], 1)

            @block.scalar
            def _(act):
                n = 0
                for q in (2, 3, 0, 1):
                    for first, count in tiles:
                        act.wait_ge(s["turned"], n + 1)
                        act.activation(tok[:, q, first * P:(first + count) * P], ps[:, n % 4, 0:count * P],
                                       ACT.Copy).then_inc(s["token"], 1)
                        n += 1

            @block.vector
            def _(dve):
                step = lambda ins: core.dve.step(dve, ins)
                ready = {2: 3, 3: 6, 0: 9, 1: 12}
                heads = lambda d: slice(d * HEADS, (d + 1) * HEADS)

                def take(j):
                    q, d = jobs[j]
                    dve.wait_ge(s["sum"], j + 1)
                    sums = ps[:, 4 + 2 * (j % 2):6 + 2 * (j % 2), :].rearrange("p g (h e) -> p (g h) e", e=HEAD)
                    etot = lambda q, d: spread(ssd.etot[:, q, heads(d)], 2, HEAD)
                    first = {F: 0, B: 1}[d]
                    dst = ssd.state[:, d, first if q >= 2 else 1 - first]
                    if j in (0, 2):
                        ins = dve.tensor_tensor(dst, sums, etot(5 - q, d), ALU.mult)
                    elif j in (1, 3):
                        ins = dve.tensor_tensor(dst, dst, sums, ALU.add)
                    else:
                        step(dve.tensor_tensor(dst, ssd.state[:, d, first], etot(q, d), ALU.mult))
                        ins = dve.tensor_tensor(dst, dst, sums, ALU.add)
                    ins.then_inc(s["taken"], 1)
                    dve.wait_ge(s["taken"], j + 1)

                for j, (q, d) in enumerate(jobs + extra):
                    dve.wait_ge(s["token"], ready[q])
                    x = tok[:, q, 0:NX].rearrange("p (h e) -> p h e", e=HEAD)
                    xdt = ctx_xdt[:] if q >= 2 else ssd.xdt[:, q, d]
                    step(dve.tensor_tensor(xdt, x, spread(ssd.dt[:, q, heads(d)], 2, HEAD), ALU.mult))
                    if j < len(jobs):
                        if j >= 2:
                            take(j - 2)
                        dve.tensor_tensor(xw[:, j % 2], xdt, spread(ssd.to_end[:, q, heads(d)], 2, HEAD),
                                          ALU.mult).then_inc(s["weighted"], 1)
                        dve.wait_ge(s["weighted"], j + 1)
                take(4)
                take(5)


def ssd_scan_stage(core, ssd, xbc, gate):
    nc, ps = core.nc, core.ps
    s = {n: core.sem(f"scan_{n}") for n in ("cb", "cum", "diff", "grown", "decay", "kernel", "turned_c", "y", "cbm")}
    units = [(c, h4) for c in range(TT) for h4 in range(4)]
    with ExitStack() as own:
        sb = lambda name, shape: own.enter_context(nc.sbuf_tensor(f"scan_{name}", shape, F32))
        cbm = sb("cbm", [P, TT, 2, 2, P])
        grown, decay = sb("grown", [P, 2, 2, 4, P]), sb("decay", [P, 2, 2, 4, P])
        with nc.Block() as block:
            @block.tensor
            def _(pe):
                for c in range(TT):
                    at = slice(c * P, (c + 1) * P)
                    for g in range(2):
                        mm = pe.matmul(ps[:, 2, (2 * c + g) * P:(2 * c + g + 1) * P], xbc[:, 8 + g, at],
                                       xbc[:, 10 + g, at], start=True, stop=True)
                mm.then_inc(s["cb"], 1)

                def sums(u):
                    c, h4 = units[u]
                    if u == 1:
                        pe.wait_ge(s["cbm"], 8)
                    if u >= 2:
                        pe.wait_ge(s["grown"], 2 * u - 2)
                    for d, tri in enumerate(("tri_f", "tri_b")):
                        for h in range(4):
                            hd = d * HEADS + 4 * h4 + h
                            mm = pe.matmul(ps[:, 2 * (u % 2) + d, h * P:(h + 1) * P],
                                           ssd.da[:, c, hd:hd + 1].broadcast_to([P, P]), core.cst[tri],
                                           start=True, stop=True)
                        mm.then_inc(s["cum"], 1)

                sums(0)
                for u, (c, h4) in enumerate(units):
                    if u + 1 < len(units):
                        sums(u + 1)
                    pe.wait_ge(s["kernel"], 2 * u + 2)
                    pe.wait_ge(s["turned_c"], 2 * u + 2)
                    for h in range(4):
                        head = 4 * h4 + h
                        ft, row = head // 2, (head % 2) * HEAD
                        out = ps[row:row + HEAD, 4 + ft // 2, (ft % 2) * T + c * P:(ft % 2) * T + (c + 1) * P]
                        for d in range(2):
                            pe.matmul(out, ssd.xdt[:, c, d, head, :], decay[:, u % 2, d, h, :],
                                      start=d == 0, stop=False)
                            mm = pe.matmul(out, ssd.state[:, d, c, head, :], grown[:, u % 2, d, h, :],
                                           start=False, stop=d == 1)
                    mm.then_inc(s["y"], 1)

            @block.scalar
            def _(act):
                for u in range(len(units)):
                    if u >= 2:
                        act.wait_ge(s["y"], u - 1)
                    for d in range(2):
                        act.wait_ge(s["diff"], 2 * u + d + 1)
                        act.activation(grown[:, u % 2, d].rearrange("p h l -> p (h l)"),
                                       ps[:, 2 * (u % 2) + d, :],
                                       ACT.Exp).then_inc(s["grown"], 1)
                    for d in range(2):
                        act.activation(decay[:, u % 2, d], decay[:, u % 2, d], ACT.Exp).then_inc(s["decay"], 1)

            @block.vector
            def _(dve):
                dve.wait_ge(s["cb"], 1)
                for c in range(TT):
                    for g in range(2):
                        for d, tri in enumerate(("tri_f", "tri_b")):
                            dve.tensor_tensor(cbm[:, c, g, d, :], ps[:, 2, (2 * c + g) * P:(2 * c + g + 1) * P],
                                              core.cst[tri], ALU.mult).then_inc(s["cbm"], 1)
                dve.wait_ge(s["cbm"], 8)

                def diffs(u):
                    c, h4 = units[u]
                    if u >= 2:
                        dve.wait_ge(s["y"], u - 1)
                    for d in range(2):
                        dve.wait_ge(s["cum"], 2 * u + d + 1)
                        for h in range(4):
                            hd = d * HEADS + 4 * h4 + h
                            ins = dve.tensor_scalar(decay[:, u % 2, d, h, :], ps[:, 2 * (u % 2) + d, h * P:(h + 1) * P],
                                                    ssd.cum[:, c, hd:hd + 1], 0.0, ALU.subtract, ALU.min)
                        ins.then_inc(s["diff"], 1)

                diffs(0)
                for u, (c, h4) in enumerate(units):
                    if u + 1 < len(units):
                        diffs(u + 1)
                    g = h4 // 2
                    for d in range(2):
                        slot = grown[:, u % 2, d]
                        dve.wait_ge(s["grown"], 2 * u + d + 1)
                        dve.tensor_tensor(slot, slot, spread(xbc[:, 10 + g, c * P:(c + 1) * P], 1, 4),
                                          ALU.mult).then_inc(s["turned_c"], 1)
                    for d in range(2):
                        slot = decay[:, u % 2, d]
                        dve.wait_ge(s["decay"], 2 * u + d + 1)
                        dve.tensor_tensor(slot, slot, spread(cbm[:, c, g, d, :], 1, 4), ALU.mult).then_inc(s["kernel"], 1)
                dve.wait_ge(s["y"], len(units))
                for ft in range(HT):
                    ins = dve.scalar_tensor_tensor(xbc[:, ft, :], xbc[:, ft, :], core.prm["ssd_d"][:, ft:ft + 1],
                                                   ps[:, 4 + ft // 2, (ft % 2) * T:(ft % 2 + 1) * T],
                                                   ALU.mult, ALU.add)
                core.dve.step(dve, ins)
                dve.tensor_tensor(xbc[:, 0:HT, :], xbc[:, 0:HT, :], gate[:], ALU.mult)


def mixer_norm_stage(core, z, y, h):
    nc, ps = core.nc, core.ps
    s = {n: core.sem(f"mixnorm_{n}") for n in ("squared", "summed", "rooted")}
    with ExitStack() as own:
        sb = lambda name, shape: own.enter_context(nc.sbuf_tensor(f"mn_{name}", shape, F32))
        sq, std = sb("sq", [P, 2 * HT, T]), sb("std", [P, HT + 2, T])
        with nc.Block() as block:
            @block.scalar
            def _(act):
                act.activation(sq[:, 0:HT, :], z[:, 0:HT, :], ACT.Square).then_inc(s["squared"], 1)
                act.activation(sq[:, HT:, :], y[:, 0:HT, :], ACT.Square).then_inc(s["squared"], 1)
                act.wait_ge(s["summed"], 1)
                eps = core.small[:, EPS_COL:EPS_COL + 1]
                act.activation(std[:, 0:HT, :].rearrange("p (b j) t -> p b (j t)", j=2), ps[:, 0:4, :], ACT.Sqrt,
                               bias=eps, scale=1.0 / P).then_inc(s["rooted"], 1)
                act.wait_ge(s["summed"], 2)
                act.activation(std[:, HT:, :], ps[:, 4:6, 0:T], ACT.Sqrt, bias=eps,
                               scale=2.0 / HY).then_inc(s["rooted"], 1)

            @block.tensor
            def _(pe):
                pe.wait_ge(s["squared"], 1)
                for b in range(4):
                    mm = pe.matmul(ps[:, b, :], core.ones[:], sq[:, 2 * b:2 * b + 2, :].rearrange("p j t -> p (j t)"),
                                   start=True, stop=True)
                mm.then_inc(s["summed"], 1)
                pe.wait_ge(s["squared"], 2)
                for g in range(2):
                    for j in range(4):
                        mm = pe.matmul(ps[:, 4 + g, 0:T], core.ones[:], sq[:, HT + 4 * g + j, :],
                                       start=j == 0, stop=j == 3)
                mm.then_inc(s["summed"], 1)

            @block.vector
            def _(dve):
                for half, (at, src, gain) in enumerate(((slice(0, HT), z, "hy_norm"), (slice(HT, HT + 2), y, "ssd_norm"))):
                    dve.wait_ge(s["rooted"], half + 1)
                    core.dve.step(dve, dve.reciprocal(std[:, at, :], std[:, at, :]))
                    for t in range(HT):
                        r = std[:, t, :] if half == 0 else std[:, HT + t // 4, :]
                        dve.scalar_tensor_tensor(h[:, half * HT + t, :], src[:, t, :],
                                                 core.prm[gain][:, t:t + 1], r, ALU.mult, ALU.mult)


def gated(core, part, last=False):
    def finish(dve, n, slots):
        at = bass.ds(n + part * KD, 1)
        ins = dve.scalar_tensor_tensor(core.x[:, n, :], slots[0], core.mod[:, at, 0], core.x[:, n, :], ALU.mult, ALU.add)
        if last:
            core.dve.step(dve, ins)
            add_squares(core, dve, n, slots[0])
    return finish


def first_block(core):
    nc = core.nc


    class Ssd:
        pass

    with ExitStack() as mixer:
        sb = lambda name, shape, dt=F32: mixer.enter_context(nc.sbuf_tensor(name, shape, dt))
        u, xbc, zg = sb("u", [P, HY_TILES, T]), sb("xbc", [P, XBC_TILES, T]), sb("zg", [P, Z_TILES, T])
        xbc_ctx = sb("xbc_ctx", [P, XBC_TILES, T])
        ssd = Ssd()
        ssd.dt, ssd.da, ssd.cum, ssd.to_end, ssd.etot = (sb(f"ssd_{n}", [P, 4, 2 * HEADS])
                                                         for n in ("dt", "da", "cum", "to_end", "etot"))
        with ExitStack() as projections:
            sb2 = lambda name, shape, dt=F32: projections.enter_context(nc.sbuf_tensor(name, shape, dt))
            wdt = sb2("wdt", [P, KD, 2 * HEADS])
            h_parts, ctx_parts = (sb2(n, [P, KD, 2, T], F32R) for n in ("h_parts", "ctx_parts"))
            with nc.sbuf_tensor("context", [P, KD, T], F32) as ctx_tile:
                start_stage(core, ctx_tile, [(wdt[:], "w_dt")], u, xbc[:, 0:2, :])
                shift = core.mod[:, 0:KD, :]
                rms_stage(core, "norm_ctx", ctx_tile, ctx_tile, KD, core.gain[:, KD:2 * KD], shift[:, :, 1],
                          xbc[:, 1, :])
                split_stage(core, ctx_tile, ctx_parts, KD)
            with nc.sbuf_tensor("h_mix", [P, KD, T], F32) as h:
                rms_stage(core, "norm_x", core.x, h, KD, core.gain[:, 0:KD], shift[:, :, 0], xbc[:, 0, :])

                def silu_z(act, n, slots):
                    return act.activation(zg[:, n, :], slots[0], ACT.Silu)

                linear_stage(core, "mix_in", [
                    conv3_layer(core, "w_mix", HY_TILES, [h_parts], 0, [u], core.prm["hy_conv_w"],
                                core.prm["hy_conv_b"], [GRID], h),
                    conv3_layer(core, "w_mix", XBC_TILES, [h_parts, ctx_parts], HY_TILES, [xbc, xbc_ctx],
                                core.prm["ssd_conv_w"], core.prm["ssd_conv_b"], [GRID, T]),
                    Layer("w_mix", Z_TILES, [h_parts], shape=silu_z, first=2 * (HY_TILES + XBC_TILES)),
                ], ("w_out", 0))
            dt_stage(core, wdt, h_parts, ctx_parts, ssd, xbc, xbc_ctx)
        with ExitStack() as hyena:
            sb2 = lambda name, shape: hyena.enter_context(nc.sbuf_tensor(name, shape, F32))
            dft, inverse = sb2("dft", [P, TT, 6, P]), sb2("inverse", [P, 4, T])
            filters = sb2("filters", [P, 2, 6, HY])
            dft_loaded = core.sem("dft_loaded")
            with nc.Block() as block:
                @block.sync
                def _(sp):
                    sp.dma_start(dft[:], core.dram["dft"]).then_inc(dft_loaded, 16)
                    sp.dma_start(inverse[:], core.dram["inverse"]).then_inc(dft_loaded, 16)
                    sp.wait_ge(dft_loaded, 32)
            filter_stage(core, dft, filters)
            for o in range(2):
                hyena_stage(core, o, u, dft, inverse, filters)
        with ExitStack() as scan:
            sb2 = lambda name, shape: scan.enter_context(nc.sbuf_tensor(name, shape, F32))
            ssd.state = sb2("ssd_state", [P, 2, TT, HEADS, HEAD])
            ssd.xdt = sb2("ssd_xdt", [P, TT, 2, HEADS, HEAD])
            ssd_state_stage(core, ssd, xbc, xbc_ctx)
            ssd_scan_stage(core, ssd, xbc, zg)
        parts = sb("mix_parts", [P, KD, 2, T], F32R)
        h = sb("h_mixed", [P, KD, T])
        mixer_norm_stage(core, u, xbc, h)
        linear_stage(core, "mix_out", [Layer("w_out", KD, [parts], finish=gated(core, 2, True), steps=3, squares=True, source=h)], ("w_mlp1", 0))
    with nc.sbuf_tensor("mlp_parts", [P, KD, 2, T], F32R) as parts:
        with nc.sbuf_tensor("h_mlp", [P, KD, T], F32) as h:
            rms_stage(core, "norm_mlp", core.x, h, KD, core.gain[:, 2 * KD:3 * KD], core.mod[:, 3 * KD:4 * KD, 0],
                      core.squares)
            split_stage(core, h, parts, KD)
        with nc.sbuf_tensor("hidden", [P, MLP_TILES, 2, T], F32R) as hidden:
            def squared_relu(dve, n, slots):
                v, hi = slots[0], hidden[:, n, 0, :]
                core.dve.step(dve, dve.scalar_tensor_tensor(v, v, 0.0, v, ALU.max, ALU.mult))
                core.dve.step(dve, dve.tensor_copy(hi, v))
                dve.tensor_tensor(hidden[:, n, 1, :], v, hi.bitcast(F32), ALU.subtract)

            chunks = MLP_TILES // KD
            down = [Layer("w_mlp2", KD, [hidden[:, c * KD:(c + 1) * KD]], finish=gated(core, 5, c == chunks - 1),
                          first=c * 2 * KD, squares=c == chunks - 1, steps=3 if c == chunks - 1 else 0)
                    for c in range(chunks)]
            linear_stage(core, "mlp", [Layer("w_mlp1", MLP_TILES, [parts], finish=squared_relu, steps=2), *down],
                         ("w_in_2", 0))
    rms_stage(core, "norm_first", core.x, core.x, KD, core.prm["final1"], squares=core.squares)


def s5_setup_stage(core, s5):
    nc, dram = core.nc, core.dram
    s = {n: core.sem(f"s5_{n}") for n in ("loaded", "c_loaded", "cleared", "dt", "rate", "exp", "bounded", "sine")}
    W = HT * 64
    with ExitStack() as own:
        sb = lambda name, shape: own.enter_context(nc.sbuf_tensor(f"s5_{name}", shape, F32))
        rep = sb("rep", [P, 5, W])
        dt, e, trig, k = sb("dt", [P, W]), sb("e", [P, W]), sb("trig", [P, 2, W]), sb("k", [P, 2, W])
        kr, ki, t1, t2, inv = (sb(n, [P, W]) for n in ("kr", "ki", "t1", "t2", "inv"))
        sdt = sb("sdt", [P, PAIRS])
        sk = sb("sk", [P, PAIRS])
        with nc.Block() as block:
            @block.sync
            def _(sp):
                sp.dma_start(rep[:], dram["s5_rep"]).then_inc(s["loaded"], 16)
                sp.wait_ge(s["cleared"], 1)
                for g in range(2):
                    for part in range(2):
                        sp.dma_start(s5.c[g * 64:(g + 1) * 64, part, :, g * 16:(g + 1) * 16],
                                     dram["s5_c"][part, g * 64:(g + 1) * 64]).then_inc(s["c_loaded"], 16)

            @block.scalar
            def _(act):
                act.activation(sdt[:], core.prm["log_dt"], ACT.Exp).then_inc(s["dt"], 1)
                act.wait_ge(s["loaded"], 16)
                act.activation(dt[:], rep[:, 2, :], ACT.Exp).then_inc(s["dt"], 1)
                act.wait_ge(s["rate"], 1)
                act.activation(s5.r[:], s5.r[:], ACT.Exp)
                act.wait_ge(s["rate"], 2)
                act.activation(e[:], e[:], ACT.Exp).then_inc(s["exp"], 1)
                act.wait_ge(s["bounded"], 1)
                act.activation(trig[:], trig[:], ACT.Sin).then_inc(s["sine"], 1)

            @block.vector
            def _(dve):
                step = lambda ins: core.dve.step(dve, ins)
                mul = lambda out, a, b: step(dve.tensor_tensor(out, a, b, ALU.mult))
                dve.memset(s5.c[:], 0.0).then_inc(s["cleared"], 1)
                dve.wait_ge(s["dt"], 1)
                dve.tensor_tensor(s5.r[:], core.prm["lam_re"], sdt[:], ALU.mult).then_inc(s["rate"], 1)
                mul(s5.turn[:], core.prm["lam_im"], sdt[:])
                step(dve.tensor_scalar(s5.turn[:], s5.turn[:], 1 / (2 * math.pi), None, ALU.mult))
                step(dve.tensor_scalar(sk[:], s5.turn[:], MAGIC, None, ALU.add))
                step(dve.tensor_scalar(sk[:], sk[:], -MAGIC, None, ALU.add))
                step(dve.tensor_tensor(s5.turn[:], s5.turn[:], sk[:], ALU.subtract))
                dve.wait_ge(s["dt"], 2)
                dve.tensor_tensor(e[:], rep[:, 0, :], dt[:], ALU.mult).then_inc(s["rate"], 1)
                mul(trig[:, 0, :], rep[:, 1, :], dt[:])
                step(dve.tensor_scalar(trig[:, 1, :], trig[:, 0, :], math.pi / 2, None, ALU.add))
                sine_steps(core, dve, trig[:], k[:], s["bounded"])
                mul(t1[:], rep[:, 0, :], rep[:, 0, :])
                mul(t2[:], rep[:, 1, :], rep[:, 1, :])
                step(dve.tensor_tensor(inv[:], t1[:], t2[:], ALU.add))
                step(dve.reciprocal(inv[:], inv[:]))
                dve.wait_ge(s["exp"], 1)
                dve.wait_ge(s["sine"], 1)
                re, im = k[:, 0, :], k[:, 1, :]
                mul(re, e[:], trig[:, 1, :])
                step(dve.tensor_scalar(re, re, -1.0, None, ALU.add))
                mul(im, e[:], trig[:, 0, :])
                mul(t1[:], re, rep[:, 0, :])
                mul(t2[:], im, rep[:, 1, :])
                step(dve.tensor_tensor(kr[:], t1[:], t2[:], ALU.add))
                mul(kr[:], kr[:], inv[:])
                mul(t1[:], im, rep[:, 0, :])
                mul(t2[:], re, rep[:, 1, :])
                step(dve.tensor_tensor(ki[:], t1[:], t2[:], ALU.subtract))
                mul(ki[:], ki[:], inv[:])
                for part, (a, b, op) in enumerate(((kr, ki, ALU.subtract), (ki, kr, ALU.add))):
                    mul(t1[:], a[:], rep[:, 3, :])
                    mul(t2[:], b[:], rep[:, 4, :])
                    step(dve.tensor_tensor(t1[:], t1[:], t2[:], op))
                    for g in range(2):
                        step(dve.tensor_scalar(s5.b[:, :, part, g, :], t1[:].rearrange("p (f e) -> p f e", e=64),
                                               core.cst["group"][:, g:g + 1], None, ALU.mult))
                dve.wait_ge(s["c_loaded"], 64)
                step(dve.tensor_scalar(s5.c[:, 1], s5.c[:, 1], -1.0, None, ALU.mult))
                dve.tensor_scalar(s5.c[:, 2], s5.c[:, 0], -1.0, None, ALU.mult)


MAGIC = 12582912.0


def local_mixers_stage(core, s5, proj, conv):
    nc, ps = core.nc, core.ps
    s = {n: core.sem(f"mix_{n}") for n in ("glu", "diag", "conv", "convolved", "turns", "phase", "trig", "bu", "turned",
                                           "rotated", "scan_r", "scan_i", "out_c", "out_s", "y", "skip", "summed")}
    pad = CONV31 - 1
    with ExitStack() as own:
        sb = lambda name, shape: own.enter_context(nc.sbuf_tensor(f"mix_{name}", shape, F32))
        c = sb("c", [P, HT, pad + T])
        diag = sb("diag", [P, 2, CONV31, P])
        phase, whole, trig = sb("phase", [P, 2, 2, T]), sb("whole", [P, 2, T]), sb("trig", [P, 2, 2, T])
        p1, p2, bt, v = sb("p1", [P, 2, T]), sb("p2", [P, 2, T]), sb("bt", [P, 2, T]), sb("v", [P, 2, 2, T])
        oc, os = sb("oc", [P, 2, 2, T]), sb("os", [P, 2, 2, T])
        with nc.Block() as block:
            @block.gpsimd
            def _(pool):
                def make_diag(f):
                    if f >= 2:
                        pool.wait_ge(s["conv"], f - 1)
                    taps = core.prm["conv_w"][:, f * CONV31:(f + 1) * CONV31]
                    pool.tensor_tensor(diag[:, f % 2], spread(core.cst["ident"], 1, CONV31), spread(taps, 2, P),
                                       ALU.mult).then_inc(s["diag"], 1)

                make_diag(0)
                for n in range(PAIRS):
                    if n % 4 == 1 and n // 4 + 1 < HT:
                        make_diag(n // 4 + 1)
                    pool.wait_ge(s["scan_i"], n + 1)
                    if n >= 2:
                        pool.wait_ge(s["y"], n - 1)
                    pool.tensor_tensor(os[:, n % 2], v[:, n % 2], spread(trig[:, n % 2, 0, :], 1, 2),
                                       ALU.mult).then_inc(s["out_s"], 1)

            @block.scalar
            def _(act):
                def make_turns(n):
                    if n >= 2:
                        act.wait_ge(s["trig"], n - 1)
                    ph, turn = phase[:, n % 2], s5.turn[:, n:n + 1]
                    act.activation(ph[:, 0, :], core.cst["iota"], ACT.Identity, scale=turn,
                                   bias=core.small[:, ZERO_COL:ZERO_COL + 1])
                    act.activation(ph[:, 1, :], core.cst["iota"], ACT.Identity, scale=turn,
                                   bias=core.small[:, QUARTER_COL:QUARTER_COL + 1]).then_inc(s["turns"], 1)

                make_turns(0)
                make_turns(1)
                for n in range(PAIRS):
                    act.wait_ge(s["phase"], n + 1)
                    if n >= 2:
                        act.wait_ge(s["out_c"], n - 1)
                        act.wait_ge(s["out_s"], n - 1)
                    act.activation(trig[:, n % 2], phase[:, n % 2], ACT.Sin, scale=TWO_PI).then_inc(s["trig"], 1)
                    if n + 2 < PAIRS:
                        make_turns(n + 2)
                    if n % 4 == 3:
                        f = n // 4
                        act.wait_ge(s["conv"], f + 1)
                        act.activation(conv[:, f, :], ps[:, 6 + f % 2, 0:T], ACT.Identity,
                                       bias=core.prm["conv_b"][:, f:f + 1]).then_inc(s["convolved"], 1)

            @block.tensor
            def _(pe):
                def outputs(n):
                    f, q = n // 4, n % 4
                    if q == 0 and f >= 2:
                        pe.wait_ge(s["skip"], f - 1)
                    pe.wait_ge(s["out_c"], n + 1)
                    pe.wait_ge(s["out_s"], n + 1)
                    terms = ((0, oc, 0), (2, os, 1), (1, os, 0), (1, oc, 1))
                    for m, (part, src, half) in enumerate(terms):
                        mm = pe.matmul(ps[32 * q:32 * q + 32, 2 + f % 2, 0:T], s5.c[:, part, n, :],
                                       src[:, n % 2, half, :], start=m == 0, stop=m == 3)
                    mm.then_inc(s["y"], 1)

                for n in range(PAIRS):
                    f, q = n // 4, n % 4
                    if n >= 2:
                        pe.wait_ge(s["turned"], n - 1)
                    rows = slice(32 * q, 32 * q + 32)
                    for part in range(2):
                        mm = pe.matmul(ps[:, n % 2, part * T:(part + 1) * T],
                                       s5.b[rows, f, part].rearrange("p g e -> p (g e)"),
                                       proj[rows, 2 * HT + f, :], start=True, stop=True)
                    mm.then_inc(s["bu"], 1)
                    if q == 0:
                        pe.wait_ge(s["diag"], f + 1)
                        pe.wait_ge(s["glu"], 1)
                        if f >= 2:
                            pe.wait_ge(s["convolved"], f - 1)
                    for k in range(8 * q, min(8 * q + 8, CONV31)):
                        mm = pe.matmul(ps[:, 6 + f % 2, 0:T], diag[:, f % 2, k, :], c[:, f, k:k + T],
                                       start=k == 0, stop=k == CONV31 - 1)
                    if q == 3:
                        mm.then_inc(s["conv"], 1)
                    if n:
                        outputs(n - 1)
                outputs(PAIRS - 1)

            @block.vector
            def _(dve):
                dve.memset(c[:, :, 0:pad], 0.0)
                dve.tensor_tensor(c[:, :, pad:], proj[:, 0:HT, :], proj[:, HT:2 * HT, :], ALU.mult).then_inc(s["glu"], 1)

                def skip(f):
                    dve.wait_ge(s["y"], 4 * f + 4)
                    u = proj[:, 2 * HT + f, :]
                    dve.scalar_tensor_tensor(u, u, core.prm["ssm_d"][:, f:f + 1], ps[:, 2 + f % 2, 0:T],
                                             ALU.mult, ALU.add).then_inc(s["skip"], 1)

                def make_phase(n):
                    dve.wait_ge(s["turns"], n + 1)
                    if n:
                        dve.wait_ge(s["phase"], n)
                    ph = phase[:, n % 2]
                    core.dve.step(dve, dve.tensor_scalar(whole[:], ph, MAGIC, -MAGIC, ALU.add, ALU.add))
                    dve.tensor_tensor(ph, ph, whole[:], ALU.subtract).then_inc(s["phase"], 1)

                make_phase(0)
                make_phase(1)
                for n in range(PAIRS):
                    dve.wait_ge(s["bu"], n + 1)
                    dve.wait_ge(s["trig"], n + 1)
                    bu = ps[:, n % 2, :].rearrange("p (a t) -> p a t", a=2)
                    cos, sin = (spread(trig[:, n % 2, a, :], 1, 2) for a in (1, 0))
                    dve.tensor_tensor(p1[:], bu, cos, ALU.mult)
                    dve.tensor_tensor(p2[:], bu, sin, ALU.mult).then_inc(s["turned"], 1)
                    dve.wait_ge(s["turned"], n + 1)
                    dve.tensor_tensor(bt[:, 0, :], p1[:, 0, :], p2[:, 1, :], ALU.add).then_inc(s["rotated"], 1)
                    dve.tensor_tensor(bt[:, 1, :], p1[:, 1, :], p2[:, 0, :], ALU.subtract).then_inc(s["rotated"], 1)
                    if n + 2 < PAIRS:
                        make_phase(n + 2)
                    if n >= 2:
                        dve.wait_ge(s["out_s"], n - 1)
                    rate = s5.r[:, n:n + 1].broadcast_to([P, T])
                    for a, done in enumerate(("scan_r", "scan_i")):
                        dve.wait_ge(s["rotated"], 2 * n + a + 1)
                        dve.tensor_tensor_scan(v[:, n % 2, a, :], rate, bt[:, a, :], 0.0, ALU.mult,
                                               ALU.add).then_inc(s[done], 1)
                    dve.wait_ge(s["scan_r"], n + 1)
                    dve.wait_ge(s["scan_i"], n + 1)
                    if n >= 2:
                        dve.wait_ge(s["y"], n - 1)
                    dve.tensor_tensor(oc[:, n % 2], v[:, n % 2], cos, ALU.mult).then_inc(s["out_c"], 1)
                    if n % 4 == 1 and n > 4:
                        skip(n // 4 - 1)
                skip(HT - 1)


def glu_stage(core, y, parts, next_w):
    with core.nc.Block() as block:
        @block.scalar
        def _(act):
            act.activation(y, y, ACT.Gelu_apprx_tanh)

    def gate(dve, n, slots):
        dve.tensor_tensor(y[:, n, :], y[:, n, :], slots[0], ALU.mult)

    linear_stage(core, "glu", [
        Layer("w_glu", HT, [parts], shape=lambda act, n, slots: act.activation(slots[0], slots[0], ACT.Sigmoid),
              finish=gate, quarters=2, source=y)], next_w)


def group_norm_stage(core, c, y, h):
    nc, ps = core.nc, core.ps
    s = {n: core.sem(f"gn_{n}") for n in ("sums", "squared", "centred", "rooted", "scaled", "silu", "ssm_out", "conv_out")}
    width = HT * P
    with ExitStack() as own:
        sb = lambda name, shape: own.enter_context(nc.sbuf_tensor(f"gn_{name}", shape, F32))
        sq, std = sb("sq", [P, HT, T]), sb("std", [P, 3, T])
        with nc.Block() as block:
            @block.tensor
            def _(pe):
                def total(bank, src):
                    for t in range(HT):
                        mm = pe.matmul(ps[:, bank, 0:T], core.ones[:], src[:, t, :], start=t == 0, stop=t == HT - 1)
                    mm.then_inc(s["sums"], 1)
                total(0, c)
                for n in range(3):
                    pe.wait_ge(s["squared"], n + 1)
                    total(n + 1, sq)

            @block.scalar
            def _(act):
                eps = core.small[:, EPS_COL:EPS_COL + 1]

                def root(n):
                    act.wait_ge(s["sums"], n + 2)
                    act.activation(std[:, n, :], ps[:, n + 1, 0:T], ACT.Sqrt, bias=eps,
                                   scale=1.0 / width).then_inc(s["rooted"], 1)
                act.activation(sq[:], y, ACT.Square).then_inc(s["squared"], 1)
                root(0)
                act.wait_ge(s["centred"], 1)
                act.activation(sq[:], c, ACT.Square).then_inc(s["squared"], 1)
                root(1)
                for t in range(HT):
                    act.wait_ge(s["scaled"], t + 1)
                    act.activation(c[:, t, :], c[:, t, :], ACT.Silu, bias=core.prm["ln_b"][:, t:t + 1]).then_inc(s["silu"], 1)
                act.wait_ge(s["silu"], HT)
                act.activation(sq[:], c, ACT.Square).then_inc(s["squared"], 1)
                root(2)

            @block.vector
            def _(dve):
                dve.wait_ge(s["sums"], 1)
                dve.scalar_tensor_tensor(c, spread(ps[:, 0, 0:T], 1, HT), -1.0 / width, c, ALU.mult,
                                         ALU.add).then_inc(s["centred"], 1)
                for n, (src, dst, gain) in enumerate(((y, h[:, HT:, :], "grp_ssm"), (c, c, "ln_g"),
                                                      (c, h[:, 0:HT, :], "grp_conv"))):
                    dve.wait_ge(s["rooted"], n + 1)
                    core.dve.step(dve, dve.reciprocal(std[:, n, :], std[:, n, :]))
                    for t in range(HT):
                        dve.scalar_tensor_tensor(dst[:, t, :], src[:, t, :], core.prm[gain][:, t:t + 1], std[:, n, :],
                                                 ALU.mult, ALU.mult).then_inc(s[("ssm_out", "scaled", "conv_out")[n]], 1)


def values_stage(core, mem, v, next_w):
    nc, ps = core.nc, core.ps
    Q, N = core.quarters, core.tiles
    blocks = D // BANK
    rounds = blocks // 2
    with nc.Block() as block:
        @block.sync
        def _(sp):
            stream(core, sp, "w_v", blocks * HALF, next_w, 0, Q)

        @block.scalar
        def _(act):
            begin(core, act, make_hi, 2 * KD, Q, core.begun)
            split_and_take(core, act, make_hi, lambda act, n, i, s: None, rounds, 2, KD, Q,
                           first_of_next(core, act, make_hi, Q + blocks * KD))

        @block.vector
        def _(dve):
            def take(dve, n, i, s):
                dve.wait_ge(core.multiplied, i * (2 * KD) + (Q + SLOTS + (s + 1) * KD))
                dve.tensor_copy(v[:, :, n, :], ps[:, 2 * s:2 * s + 2, :]).then_inc(core.summed, 1)
            begin(core, dve, make_lo, 2 * KD, Q, core.begun)
            split_and_take(core, dve, make_lo, take, rounds, 2, KD, Q,
                           first_of_next(core, dve, make_lo, Q + blocks * KD))

        @block.tensor
        def _(pe):
            with pe.Fori(0, rounds) as i:
                for b in range(2):
                    pe.wait_ge(core.summed, i * 2 + (N + b + 1))
                    for k in range(KD):
                        pe.wait_ge(core.split, i * (2 * KD) + (Q + b * KD + k + 1))
                        hi, lo = (w[:, k % SLOTS].rearrange("p k m -> p (k m)") for w in (core.hi, core.lo))
                        for m in range(TT):
                            rows = slice(m * P, (m + 1) * P)
                            for j, (part, w) in enumerate(((0, hi), (0, lo), (1, hi))):
                                mm = pe.matmul(ps[:, 2 * b + m, :], mem[:, k, part, rows], w,
                                               start=(j, k) == (0, 0), stop=(j, k) == (2, KD - 1))
                        mm.then_inc(core.multiplied, 1)
    core.quarters += blocks * KD
    core.tiles += blocks
    core.begun = True


def attention_stage(core, q, k, v, out):
    nc, ps = core.nc, core.ps
    s = {n: core.sem(f"att_{n}") for n in ("scores", "max", "exp", "scaled", "turned", "probs", "out", "rounded", "taken")}
    units = [(h, t) for h in range(MEM_HEADS) for t in range(TT)]
    scale = 1.0 / math.sqrt(D // MEM_HEADS)
    with ExitStack() as own:
        sb = lambda name, shape: own.enter_context(nc.sbuf_tensor(f"att_{name}", shape, F32))
        p, pt = sb("p", [P, 8, T]), sb("pt", [P, TT, MEM_HEADS, T])
        top, total = sb("top", [P, 8]), sb("total", [P, 8])
        with nc.Block() as block:
            @block.tensor
            def _(pe):
                for n, (h, t) in enumerate(units):
                    for d in range(4):
                        mm = pe.matmul(ps[:, n, 0:T], q[:, 4 * h + d, t * P:(t + 1) * P], k[:, 4 * h + d, :],
                                       start=d == 0, stop=d == 3)
                    mm.then_inc(s["scores"], 1)
                for n in range(8):
                    pe.wait_ge(s["scaled"], n + 1)
                    for m in range(TT):
                        mm = pe.transpose(ps[:, n, m * P:(m + 1) * P], p[:, n, m * P:(m + 1) * P], core.cst["ident"])
                    mm.then_inc(s["turned"], 1)
                for n in range(KD):
                    h = n // 4
                    pe.wait_ge(s["probs"], 8)
                    if n >= 8:
                        pe.wait_ge(s["taken"], n - 7)
                    for m in range(TT):
                        mm = pe.matmul(ps[:, n % 8, 0:T], v[:, m, n // 4, (n % 4) * P:(n % 4 + 1) * P], pt[:, m, h, :],
                                       start=m == 0, stop=m == TT - 1)
                    mm.then_inc(s["out"], 1)

            @block.scalar
            def _(act):
                for n in range(8):
                    act.wait_ge(s["max"], n + 1)
                    act.activation(p[:, n, :], ps[:, n, 0:T], ACT.Exp, bias=top[:, n:n + 1], scale=scale,
                                   accum_out=total[:, n:n + 1]).then_inc(s["exp"], 1)
                for n in range(KD):
                    act.wait_ge(s["out"], n + 1)
                    act.activation(out[:, n, 0, :], ps[:, n % 8, 0:T], ACT.Copy).then_inc(s["rounded"], 1)

            @block.vector
            def _(dve):
                for n in range(8):
                    dve.wait_ge(s["scores"], n + 1)
                    core.dve.step(dve, dve.reduce_max(top[:, n:n + 1], ps[:, n, 0:T], AX_X))
                    dve.tensor_scalar(top[:, n:n + 1], top[:, n:n + 1], -scale, None, ALU.mult).then_inc(s["max"], 1)
                for n in range(8):
                    dve.wait_ge(s["exp"], n + 1)
                    core.dve.step(dve, dve.reciprocal(total[:, n:n + 1], total[:, n:n + 1]))
                    dve.tensor_scalar(p[:, n, :], p[:, n, :], total[:, n:n + 1], None, ALU.mult).then_inc(s["scaled"], 1)
                for n, (h, t) in enumerate(units):
                    dve.wait_ge(s["turned"], n + 1)
                    dve.tensor_copy(pt[:, :, h, t * P:(t + 1) * P],
                                    ps[:, n, 0:T].rearrange("p (m l) -> p m l", m=TT)).then_inc(s["probs"], 1)
                for n in range(KD):
                    dve.wait_ge(s["rounded"], n + 1)
                    dve.tensor_tensor(out[:, n, 1, :], ps[:, n % 8, 0:T], out[:, n, 0, :].bitcast(F32),
                                      ALU.subtract).then_inc(s["taken"], 1)


def top_experts_stage(core, q, keys, turned):
    nc, ps = core.nc, core.ps
    s = {n: core.sem(f"top_{n}") for n in ("scores", "copied", "shifted", "exp", "ready", "turned", "taken")}
    with ExitStack() as own:
        sb = lambda name, shape, dt=F32: own.enter_context(nc.sbuf_tensor(f"top_{name}", shape, dt))
        sc = sb("sc", [P, TT, 2, PEER_HEADS, KEYS])
        val, idx = sb("val", [P, TT, 2, PEER_HEADS, TOPK]), sb("idx", [P, TT, 2, PEER_HEADS, TOPK], U32)
        idf = sb("idf", [P, TT, 2, PEER_HEADS, TOPK])
        cand = sb("cand", [P, TT, PEER_HEADS, TOPK * TOPK])
        best, pos = sb("best", [P, TT, PEER_HEADS, TOPK]), sb("pos", [P, TT, PEER_HEADS, TOPK], U32)
        half, halff = sb("half", [P, 2, TT, PEER_HEADS, TOPK], U32), sb("halff", [P, 2, TT, PEER_HEADS, TOPK])
        pick = sb("pick", [P, PEER_HEADS, TOPK, TOPK])
        chosen = sb("chosen", [P, TT, 3, PEER_HEADS, TOPK])
        total = sb("total", [P, TT, PEER_HEADS])
        with nc.Block() as block:
            @block.tensor
            def _(pe):
                for t in range(TT):
                    for a in range(2):
                        rows = slice(a * 64, a * 64 + 64)
                        for h in range(PEER_HEADS):
                            mm = pe.matmul(ps[:, 4 * t + 2 * a + h // 4, (h % 4) * P:(h % 4 + 1) * P],
                                           q[rows, h, t * P:(t + 1) * P], keys[rows, h, :], start=True, stop=True)
                        mm.then_inc(s["scores"], 1)
                for t in range(TT):
                    pe.wait_ge(s["ready"], t + 1)
                    for n in range(3):
                        mm = pe.transpose(ps[:, t, n * P:(n + 1) * P],
                                          chosen[:, t, n].rearrange("p h k -> p (h k)"), core.cst["ident"])
                    mm.then_inc(s["turned"], 1)

            @block.scalar
            def _(act):
                for t in range(TT):
                    for a in range(2):
                        act.wait_ge(s["scores"], 2 * t + a + 1)
                        act.activation(sc[:, t, a].rearrange("p (b h) n -> p b (h n)", b=2),
                                       ps[:, 4 * t + 2 * a:4 * t + 2 * a + 2, :], ACT.Copy).then_inc(s["copied"], 1)
                act.wait_ge(s["shifted"], 1)
                act.activation(chosen[:, :, 2], chosen[:, :, 2], ACT.Exp).then_inc(s["exp"], 1)
                for t in range(TT):
                    act.wait_ge(s["turned"], t + 1)
                    act.activation(turned[:, :, t * P:(t + 1) * P], ps[:, t, 0:3 * P].rearrange("p (n l) -> p n l", n=3),
                                   ACT.Copy)

            @block.vector
            def _(dve):
                step = lambda ins: core.dve.step(dve, ins)

                def top16(units, src, values, index):
                    for lo in (0, 8):
                        for u in units:
                            ins = dve.max(values(u)[:, lo:lo + 8], src(u))
                        step(ins)
                        for u in units:
                            ins = dve.max_index(index(u)[:, lo:lo + 8], values(u)[:, lo:lo + 8], src(u))
                        step(ins)
                        if lo == 0:
                            for u in units:
                                ins = dve.match_replace(src(u), values(u)[:, 0:8], src(u), -3.0e38)
                            step(ins)

                dve.wait_ge(s["copied"], 4)
                top16([(t, a, h) for t in range(TT) for a in range(2) for h in range(PEER_HEADS)],
                      lambda u: sc[:, u[0], u[1], u[2], :], lambda u: val[:, u[0], u[1], u[2], :],
                      lambda u: idx[:, u[0], u[1], u[2], :])
                step(dve.tensor_copy(idf[:], idx[:]))
                for t in range(TT):
                    pairs = cand[:, t].rearrange("p h (a b) -> p h a b", b=TOPK)
                    ins = dve.tensor_tensor(pairs, spread(val[:, t, 0], 3, TOPK), spread(val[:, t, 1], 2, TOPK), ALU.add)
                step(ins)
                top16([(t, h) for t in range(TT) for h in range(PEER_HEADS)],
                      lambda u: cand[:, u[0], u[1], :], lambda u: best[:, u[0], u[1], :],
                      lambda u: pos[:, u[0], u[1], :])
                dve.tensor_scalar(half[:, 0], pos[:], 4, None, ALU.logical_shift_right)
                step(dve.tensor_scalar(half[:, 1], pos[:], 15, None, ALU.bitwise_and))
                step(dve.tensor_copy(halff[:], half[:]))
                for t in range(TT):
                    ins = dve.tensor_tensor(chosen[:, t, 2], best[:, t],
                                            best[:, t, :, 0:1].broadcast_to([P, PEER_HEADS, TOPK]), ALU.subtract)
                ins.then_inc(s["shifted"], 1)
                ranks = core.cst["iota"][:, 0:TOPK].unsqueeze(1).unsqueeze(1).broadcast_to([P, PEER_HEADS, TOPK, TOPK])
                for t in range(TT):
                    for a in range(2):
                        step(dve.tensor_tensor(pick[:], ranks, spread(halff[:, a, t], 3, TOPK), ALU.is_equal))
                        step(dve.tensor_tensor(pick[:], pick[:], spread(idf[:, t, a], 2, TOPK), ALU.mult))
                        step(dve.tensor_reduce(chosen[:, t, a], pick[:], AX_X, ALU.add))
                dve.wait_ge(s["exp"], 1)
                for t in range(TT):
                    step(dve.tensor_reduce(total[:, t], chosen[:, t, 2], AX_X, ALU.add))
                step(dve.reciprocal(total[:], total[:]))
                for t in range(TT):
                    dve.tensor_tensor(chosen[:, t, 2], chosen[:, t, 2], spread(total[:, t], 2, TOPK),
                                      ALU.mult).then_inc(s["ready"], 1)


def gates_stage(core, turned, gates):
    nc, ps = core.nc, core.ps
    GROUP = 8
    s = {n: core.sem(f"gates_{n}") for n in ("left_act", "left_abs", "right", "multiplied", "stored")}
    keys = core.cst["iota"][:, 0:KEYS]
    left = core.hi[:].rearrange("p s k m -> p (s k) m")
    with nc.sbuf_tensor("gates_right", [P, GROUP, KEYS], F32) as right:
        rounds = T // GROUP
        with nc.Block() as block:
            @block.tensor
            def _(pe):
                pe.sem_inc(s["multiplied"], GROUP)
                with pe.Fori(0, rounds) as i:
                    for b in range(2):
                        pe.wait_ge(s["stored"], i * 2 + (b + 1))
                        for j in range(4):
                            n = 4 * b + j
                            if j == 3:
                                pe.wait_ge(s["left_act"], i * 2 + (b + 1))
                            pe.wait_ge(s["right"], i * GROUP + (n + 1))
                            pe.matmul(ps[:, b, j * P:(j + 1) * P], left[:, n, :].bitcast(F32), right[:, n, :],
                                      start=True, stop=True).then_inc(s["multiplied"], 1)

            @block.scalar
            def _(act):
                def make_left(i, b):
                    n = 4 * (b % 2) + 3
                    act.wait_ge(s["multiplied"], i * GROUP + (4 * b + 4))
                    act.activation(left[:, n, :], keys, ACT.Abs, scale=-1.0,
                                   bias=turned[:, 0, bass.ds(i * GROUP + (4 * b + 3), 1)]).then_inc(s["left_abs"], 1)
                    act.wait_ge(s["left_abs"], i * 2 + (b + 1))
                    act.activation(left[:, n, :], left[:, n, :].bitcast(F32), ACT.Relu, scale=-1.0,
                                   bias=core.ones[:, 0:1]).then_inc(s["left_act"], 1)

                def store(i, b):
                    act.wait_ge(s["multiplied"], i * GROUP + (GROUP + 4 * b + 4))
                    act.activation(gates[:, :, bass.ds(i * GROUP + 4 * b, 4)].rearrange("p j t -> p t j"),
                                   ps[:, b, :].rearrange("p (t j) -> p t j", t=4), ACT.Copy).then_inc(s["stored"], 1)

                act.sem_inc(s["stored"], 2)
                make_left(0, 0)
                with act.Fori(0, rounds - 1) as i:
                    for b in range(2):
                        make_left(i, b + 1)
                        store(i, b)
                make_left(rounds - 1, 1)
                store(rounds - 1, 0)
                store(rounds - 1, 1)

            @block.vector
            def _(dve):
                with dve.Fori(0, rounds) as i:
                    for b in range(2):
                        dve.wait_ge(s["multiplied"], i * GROUP + (4 * b + 3))
                        dve.tensor_tensor(left[:, 4 * b:4 * b + 3, :], spread(keys, 1, 3),
                                          spread(turned[:, 0, bass.ds(i * GROUP + 4 * b, 3)], 2, KEYS), ALU.is_equal)
                        for n in range(4 * b, 4 * b + 4):
                            at = bass.ds(i * GROUP + n, 1)
                            if n % 4 == 3:
                                dve.wait_ge(s["multiplied"], i * GROUP + (n + 1))
                            dve.tensor_scalar(right[:, n, :], keys, turned[:, 1, at], turned[:, 2, at],
                                              ALU.is_equal, ALU.mult).then_inc(s["right"], 1)


def onto_stream(core, last=True):
    def finish(dve, n, slots):
        ins = dve.tensor_tensor(core.x[:, n, :], core.x[:, n, :], slots[0], ALU.add)
        if last:
            core.dve.step(dve, ins)
            add_squares(core, dve, n, slots[0])
    return finish


def second_block(core):
    nc = core.nc

    class S5:
        pass

    with ExitStack() as mixers:
        sb = lambda name, shape: mixers.enter_context(nc.sbuf_tensor(name, shape, F32))
        proj, conv = sb("proj", [P, 3 * HT, T]), sb("conv", [P, HT, T])
        with nc.sbuf_tensor("in2_parts", [P, KD, 2, T], F32R) as parts, nc.sbuf_tensor("h_in2", [P, KD, T], F32) as h:
            rms_stage(core, "norm_mix2", core.x, h, KD, core.prm["norm_mix"])
            rows = lambda part: (lambda n: proj[:, n + part * HT, :])
            linear_stage(core, "in2", [
                Layer("w_in_2", HT, [parts], into=rows(0), source=h),
                Layer("w_in_2", HT, [parts], first=2 * HT,
                      shape=lambda act, n, slots: act.activation(slots[0], slots[0], ACT.Sigmoid),
                      finish=lambda dve, n, slots: dve.tensor_copy(proj[:, n + HT, :], slots[0])),
                Layer("w_in_2", HT, [parts], first=4 * HT, into=rows(2)),
            ], ("w_glu", 0))
        with ExitStack() as scans:
            sb2 = lambda name, shape: scans.enter_context(nc.sbuf_tensor(name, shape, F32))
            s5 = S5()
            s5.b, s5.c = sb2("s5_b", [P, HT, 2, 2, 64]), sb2("s5_cc", [P, 3, PAIRS, 32])
            s5.r, s5.turn = sb2("s5_r", [P, PAIRS]), sb2("s5_turn", [P, PAIRS])
            s5_setup_stage(core, s5)
            local_mixers_stage(core, s5, proj, conv)
        y = proj[:, 2 * HT:, :]
        with nc.sbuf_tensor("glu_parts", [P, HT, 2, T], F32R) as parts:
            glu_stage(core, y, parts, ("w_out_2", 0))
        with nc.sbuf_tensor("out2_parts", [P, KD, 2, T], F32R) as parts, nc.sbuf_tensor("h_out2", [P, KD, T], F32) as h:
            group_norm_stage(core, conv[:], y, h)
            linear_stage(core, "mix2_out", [Layer("w_out_2", KD, [parts], finish=onto_stream(core), source=h, squares=True, steps=3)], ("w_q", 0))
    with ExitStack() as attention:
        sb = lambda name, shape, dt=F32: attention.enter_context(nc.sbuf_tensor(name, shape, dt))
        q, k, v = sb("q", [P, KD, T]), sb("k", [P, KD, T]), sb("v", [P, TT, 4, BANK])
        parts, h, mem = sb("att_parts", [P, KD, 2, T], F32R), sb("h_att", [P, KD, T]), sb("mem", [P, KD, T])
        rms_stage(core, "norm_q", core.x, h, KD, core.prm["norm_mem"], squares=core.squares)
        linear_stage(core, "mem_q", [Layer("w_q", KD, [parts], into=lambda n: q[:, n, :], source=h)], ("w_k", 0),
                     loads=[(mem[:], "mem")])
        rms_stage(core, "norm_mem", mem, mem, KD, core.prm["mem_norm"])
        linear_stage(core, "mem_k", [Layer("w_k", KD, [parts], into=lambda n: k[:, n, :], source=mem)], ("w_v", 0))
        values_stage(core, parts, v, ("w_o", 0))
        attention_stage(core, q, k, v, parts)
        linear_stage(core, "mem_out", [Layer("w_o", KD, [parts], finish=onto_stream(core), squares=True, steps=3)], ("w_peer_q", 0))
    with nc.sbuf_tensor("expert_parts", [P, KD, 2, T], F32R) as parts, nc.sbuf_tensor("turned", [P, 3, T], F32) as turned:
        with ExitStack() as choice:
            sb = lambda name, shape: choice.enter_context(nc.sbuf_tensor(name, shape, F32))
            q, keys = sb("peer_q", [P, PEER_HEADS, T]), sb("peer_keys", [P, PEER_HEADS, KEYS])
            with nc.sbuf_tensor("h_ffn", [P, KD, T], F32) as h:
                rms_stage(core, "norm_ffn", core.x, h, KD, core.prm["norm_ffn"], squares=core.squares)
                linear_stage(core, "peer_q", [Layer("w_peer_q", PEER_HEADS, [parts], into=lambda n: q[:, n, :], source=h)],
                             ("w_u", 0), loads=[(keys[:], "peer_keys")], begin_next=False)
            top_experts_stage(core, q, keys, turned)
        with nc.sbuf_tensor("gates", [P, KEYS, T], F32) as gates:
            gates_stage(core, turned, gates)

            def gate_experts(dve, n, slots):
                dve.tensor_tensor(gates[:, n, :], gates[:, n, :], slots[0], ALU.mult)

            up = Layer("w_u", KEYS, [parts], finish=gate_experts,
                       shape=lambda act, n, slots: act.activation(slots[0], slots[0], ACT.Gelu_apprx_tanh))
            chunks = KEYS // KD
            down = [Layer("w_v_tab", KD, [parts], finish=onto_stream(core, c == chunks - 1), first=c * 2 * KD,
                          source=gates[:, c * KD:(c + 1) * KD, :], squares=c == chunks - 1,
                          steps=3 if c == chunks - 1 else 0) for c in range(chunks)]
            linear_stage(core, "experts", [up, *down], None)
    rms_stage(core, "norm_last", core.x, core.x, KD, core.prm["final2"], squares=core.squares)


def second_layout(a, d):
    d["mem"] = feature_major(a["mem_2"][0])
    d["w_in_2"] = blocks(a["w_in_2"][0])
    d["w_glu"] = blocks(a["ssm_glu_w_2"][0])
    d["w_out_2"] = blocks(a["w_out_2"][0])
    d["w_q"] = blocks(a["w_q_mem_2"][0])
    kv = a["w_kv_mem_2"][0]
    d["w_k"] = blocks(kv[:, :D])
    d["w_v"] = row_blocks(kv[:, D:])
    d["w_o"] = blocks(a["w_o_mem_2"][0])
    d["w_peer_q"] = blocks(a["peer_w_q_2"][0])
    d["peer_keys"] = a["peer_keys_2"][0].transpose(1, 3, 0, 2).reshape(P, PEER_HEADS, KEYS)
    by_second_key = lambda w: w.reshape(KEYS, KEYS, D).transpose(1, 0, 2).reshape(KEYS * KEYS, D)
    d["w_u"] = blocks(by_second_key(a["peer_u_2"][0]).T)
    d["w_v_tab"] = blocks(by_second_key(a["peer_v_2"][0]), D)
    over = lambda v: np.broadcast_to(v.reshape(HT, 8, 1, 64), (HT, 8, 16, 64))
    rep = [over(a["ssm_lam_re_2"][0]), over(a["ssm_lam_im_2"][0]),
           over(np.repeat(a["ssm_log_dt_2"][0], 64).reshape(-1, 64)),
           a["ssm_b_re_2"][0].reshape(HT, 8, 64, 16).transpose(0, 1, 3, 2),
           a["ssm_b_im_2"][0].reshape(HT, 8, 64, 16).transpose(0, 1, 3, 2)]
    d["s5_rep"] = np.stack([v.transpose(1, 2, 0, 3).reshape(P, HT * 64) for v in rep], axis=1)
    c = np.stack([a["ssm_c_re_2"][0], a["ssm_c_im_2"][0]]).reshape(2, PAIRS, 2, 16, 64)
    d["s5_c"] = c.transpose(0, 2, 4, 1, 3).reshape(2, P, PAIRS, 16)


def two_block_kernel(nc, dram, out):
    with ExitStack() as ctx:
        core = Core(nc, ctx, dram)
        first_block(core)
        stored = core.sem("result_stored")
        second_block(core)
        with nc.Block() as block:
            @block.sync
            def _(sp):
                sp.dma_start(out, core.x[:]).then_inc(stored, 16)
                sp.wait_ge(stored, 16)



def shape_constants():
    consts = np.zeros((P, N_CONST), np.float32)
    r = np.arange(P)
    at = lambda n: slice(CONST_AT[n], CONST_AT[n] + CONST_COLS[n])
    consts[:, at("ident")] = np.eye(P)
    consts[:, at("tri_f")] = r[:, None] <= r[None, :]
    consts[:, at("tri_b")] = r[:, None] >= r[None, :]
    consts[:, at("iota")] = np.arange(T)
    consts[:4, at("halves")] = np.arange(4)[:, None] % 2 == np.arange(2)
    consts[:, at("fold")] = r[:, None] % (2 * HEADS) == np.arange(2 * HEADS)
    consts[:, at("group")] = (r[:, None] // 16) % 2 == np.arange(2)
    f32 = np.float32
    t = np.linspace(0.0, 1.0, T, dtype=f32)[:, None]
    bands = 16
    w = (f32(2.0 * math.pi) * np.arange(T, dtype=f32)[:, None] / f32(T)).astype(f32)
    f = np.linspace(1e-4, bands - 1, bands, dtype=f32)[None, :]
    feats = np.concatenate([t, np.cos(f * w), -np.sin(f * w)], axis=-1).astype(f32)
    deltas = np.linspace(math.log(1e-2) / 1.5, math.log(1e-2) / 0.3, HY, dtype=f32)
    window = np.exp(-t * np.abs(deltas)).astype(f32)
    n = 2 * T
    tt, ff = np.arange(T)[:, None], np.arange(T)[None, :]
    angle = 2 * np.pi * ((tt * ff) % n) / n
    cos, sin = np.cos(angle), -np.sin(angle)
    nyquist = (-1.0) ** np.arange(T)
    cos_n, sin_n = cos[:, :P].copy(), sin[:, :P].copy()
    cos_n[:, 0] = sin_n[:, 0] = nyquist
    sin0 = sin[:, :P].copy()
    sin0[:, 0] = 0
    mats = np.stack([cos[:, :P], cos[:, P:], cos_n, sin_n, sin0, sin[:, P:]], axis=1)
    dft = mats.reshape(TT, P, 6, P).transpose(1, 0, 2, 3)
    ci, si = cos.T * 2 / n, sin.T * 2 / n
    ci[0] /= 2
    si[0] = nyquist / n
    inverse = np.concatenate([ci, si]).reshape(4, P, T).transpose(1, 0, 2)
    as32 = lambda a: np.ascontiguousarray(a, dtype=np.float32)
    return {"consts": consts, "feats": as32(feats.T), "dft": as32(dft), "inverse": as32(inverse),
            "window": as32(window.reshape(TT, P, HY).transpose(1, 0, 2))}


def columns(v):
    v = np.asarray(v)
    return v.reshape(-1, P).T


def blocks(w, chunk=None):
    K, N = w.shape
    chunk = chunk or K
    a = w.reshape(K // chunk, chunk // (HALF * P), HALF, P, N // P, P).transpose(0, 4, 1, 3, 2, 5)
    return a.reshape(-1, P, HALF * P)


def row_blocks(w):
    N = w.shape[1]
    a = w.reshape(KD // 2, 2, P, N // BANK, BANK).transpose(3, 0, 2, 1, 4)
    return a.reshape(-1, P, 2 * BANK)


def feature_major(x):
    return x.reshape(T, KD, P).transpose(2, 1, 0)


def lay_out(i):
    a = {n: np.asarray(v) for n, v in i.items()}
    w_in = a["w_in"][0]
    o0, o1 = HY_TILES * P, (HY_TILES + XBC_TILES) * P
    o2 = o1 + 2 * HEADS
    d = {
        "x": feature_major(a["x"][0]), "ctx": feature_major(a["ctx"][0]),
        "w_ada": row_blocks(a["w_ada"][0]),
        "w_mix": blocks(np.concatenate([w_in[:, :o1], w_in[:, o2:]], axis=1)),
        "w_dt": w_in[:, o1:o2].reshape(KD, P, 2 * HEADS).transpose(1, 0, 2),
        "w_out": blocks(a["w_out"][0]), "w_mlp1": blocks(a["w_mlp1"][0]), "w_mlp2": blocks(a["w_mlp2"][0], D),
        "filt_w1": a["filt_w1"][0], "filt_w2": a["filt_w2"][0], "filt_w3": a["filt_w3"][0],
    }
    rows = lambda v: np.broadcast_to(v.reshape(1, -1), (P, v.size))
    state = lambda v: v.reshape(PAIRS, P).T
    filt = np.stack([np.pad(a[n][0], (0, P - 64)) for n in ("filt_freq", "filt_b1", "filt_b2", "filt_b2")], axis=1)
    cols = {
        "cond": np.stack([a["c"][0], a["c_ctx"]], axis=1).reshape(KD, P, 2).transpose(1, 0, 2).reshape(P, 2 * KD),
        "b_ada": columns(a["b_ada"]), "norm1": columns(a["norm1_w"]),
        "hy_conv_w": columns(a["hy_conv_w"]), "hy_conv_b": columns(a["hy_conv_b"]),
        "hy_bias": columns(a["hy_bias"]), "hy_norm": columns(a["hy_norm_w"]),
        "ssd_conv_w": columns(a["ssd_conv_w"]), "ssd_conv_b": columns(a["ssd_conv_b"]),
        "ssd_d": columns(np.repeat(a["ssd_d"][0], HEAD)), "ssd_norm": columns(a["ssd_norm_w"]),
        "norm2": columns(a["norm2_w"]), "final1": columns(a["final_norm_w"]),
        "norm_mix": columns(a["norm_mix_g_2"]), "conv_b": columns(a["conv_b_2"]),
        "ln_g": columns(a["conv_ln_g_2"]), "ln_b": columns(a["conv_ln_b_2"]),
        "grp_conv": columns(a["grp_norm_conv_g_2"]), "grp_ssm": columns(a["grp_norm_ssm_g_2"]),
        "norm_mem": columns(a["norm_mem_g_2"]), "mem_norm": columns(a["mem_norm_g_2"]),
        "norm_ffn": columns(a["norm_ffn_g_2"]), "final2": columns(a["final_norm_g_2"]),
        "ssm_d": columns(a["ssm_d_2"]), "lam_re": state(a["ssm_lam_re_2"][0]),
        "lam_im": state(a["ssm_lam_im_2"][0]), "log_dt": state(np.repeat(a["ssm_log_dt_2"][0], 64)),
        "dt_bias": rows(a["dt_bias"][0]), "a_log": rows(a["a_log"][0]),
        "conv_w": a["conv_w_2"][0].reshape(CONV31, HT, P).transpose(2, 1, 0).reshape(P, -1),
        "filt": filt,
    }
    d["params"] = np.concatenate([cols[n] for n in PARAM_COLS], axis=1)
    second_layout(a, d)
    d = {n: np.ascontiguousarray(v) for n, v in d.items()}
    d.update(shape_constants())
    return d


def kernel(**inputs):
    from concourse import bacc
    from concourse.bass_utils import run_bass_kernel_spmd

    arrays = lay_out(inputs)
    nc = bacc.Bacc("TRN2", target_bir_lowering=False, num_devices=1, dynamic_dma_scratch_size=1024)
    dram = {n: nc.dram_tensor(f"in_{n}", v.shape, mybir.dt.from_np(v.dtype), kind="ExternalInput").ap()
            for n, v in arrays.items()}
    out = nc.dram_tensor("out", (P, KD, T), F32, kind="ExternalOutput").ap()
    two_block_kernel(nc, dram, out)
    r = run_bass_kernel_spmd(nc, [{f"in_{n}": v for n, v in arrays.items()}], core_ids=[0])
    return r.results[0]["out"].transpose(2, 1, 0).reshape(1, T, D)
```
